# Optimizing a Trainium2 kernel written in Bass

```python
import jax, jax.numpy as jnp
from jax import lax
import numpy as np

D_MODEL = 1024
BATCH = 1
SEQ = 512
DEPTH = 1

SSD_EXPAND = 2
SSD_D_INNER = SSD_EXPAND * D_MODEL
SSD_HEAD_DIM = 64
SSD_HEADS = SSD_D_INNER // SSD_HEAD_DIM
SSD_GROUPS = 4
SSD_HEADS_PER_GROUP = SSD_HEADS // SSD_GROUPS
SSD_STATE = 128
SSD_CONV = 4
SSD_CHUNK = 128
SSD_BC = SSD_GROUPS * SSD_STATE
SSD_XBC = SSD_D_INNER + 2 * SSD_BC
SSD_IN = SSD_D_INNER + SSD_XBC + SSD_HEADS

SGU_WIDTH = D_MODEL
SGU_GROUPS = 8
SGU_GROUP_DIM = SGU_WIDTH // SGU_GROUPS
SGU_CHUNK = 128
SGU_IN = 2 * SGU_WIDTH

N_BRANCH = 2
GATE_IN = N_BRANCH * D_MODEL
IN_COLS = SSD_IN + SGU_IN + GATE_IN
MIX_WIDTH = SSD_D_INNER + SGU_WIDTH

D_FF = 2816
FFN_CONV = 3

NORM_EPS = 1e-6
LN_EPS = 1e-5

kernel_name = "hybrid_ssd_sgu_convffn_block"

def rms_norm(x, w, eps=NORM_EPS):
    xf = x.astype(jnp.float32)
    y = xf * lax.rsqrt(jnp.mean(xf * xf, axis=-1, keepdims=True) + eps)
    return (y * w.astype(jnp.float32)).astype(x.dtype)

def layer_norm(x, w, b, eps=LN_EPS):
    xf = x.astype(jnp.float32)
    mu = jnp.mean(xf, axis=-1, keepdims=True)
    var = jnp.mean(jnp.square(xf - mu), axis=-1, keepdims=True)
    y = (xf - mu) * lax.rsqrt(var + eps) * w.astype(jnp.float32) + b.astype(jnp.float32)
    return y.astype(x.dtype)

def causal_dwconv(x, w, b):
    k = w.shape[0]
    s = x.shape[1]
    xp = jnp.pad(x, ((0, 0), (k - 1, 0), (0, 0)))
    y = b
    for i in range(k):
        y = y + w[i] * xp[:, i:i + s]
    return y

def segsum_exp(a_cum):
    t = a_cum.shape[-1]
    diff = a_cum[..., :, None] - a_cum[..., None, :]
    mask = jnp.tril(jnp.ones((t, t), dtype=bool))
    return jnp.exp(jnp.where(mask, diff, -jnp.inf))

def ssd_chunked(xh, dt, a, b_mat, c_mat):
    bsz, s = xh.shape[0], xh.shape[1]
    nc = s // SSD_CHUNK
    G, R, L, P, N = SSD_GROUPS, SSD_HEADS_PER_GROUP, SSD_CHUNK, SSD_HEAD_DIM, SSD_STATE
    xdt = (xh.astype(jnp.float32) * dt[..., None]).reshape(bsz, nc, L, G, R, P)
    adt = (dt * a).reshape(bsz, nc, L, G, R)
    a_cum = jnp.cumsum(jnp.transpose(adt, (0, 3, 4, 1, 2)), axis=-1)
    bm = b_mat.reshape(bsz, nc, L, G, N)
    cm = c_mat.reshape(bsz, nc, L, G, N)
    cb = jnp.einsum('bclgn,bcsgn->bgcls', cm, bm)
    decay = segsum_exp(a_cum)
    y_diag = jnp.einsum('bgcls,bgrcls,bcsgrp->bclgrp', cb, decay, xdt)
    decay_states = jnp.exp(a_cum[..., -1:] - a_cum)
    states = jnp.einsum('bcsgn,bgrcs,bcsgrp->bcgrpn', bm, decay_states, xdt)
    chunk_tot = jnp.pad(a_cum[..., -1], ((0, 0), (0, 0), (0, 0), (1, 0)))
    decay_chunk = segsum_exp(jnp.cumsum(chunk_tot, axis=-1))
    states = jnp.concatenate([jnp.zeros_like(states[:, :1]), states], axis=1)
    states = jnp.einsum('bgrzc,bcgrpn->bzgrpn', decay_chunk, states)[:, :-1]
    y_off = jnp.einsum('bclgn,bcgrpn,bgrcl->bclgrp', cm, states, jnp.exp(a_cum))
    return (y_diag + y_off).reshape(bsz, s, SSD_HEADS, P)

def ssd_branch(z, xbc, dt_raw, conv_w, conv_b, dt_bias, a_log, d_skip, norm_w):
    xbc = jax.nn.silu(causal_dwconv(xbc, conv_w, conv_b))
    xs, b_mat, c_mat = jnp.split(xbc, [SSD_D_INNER, SSD_D_INNER + SSD_BC], axis=-1)
    bsz, s = xs.shape[0], xs.shape[1]
    xh = xs.reshape(bsz, s, SSD_HEADS, SSD_HEAD_DIM)
    dt = jax.nn.softplus(dt_raw.astype(jnp.float32) + dt_bias.astype(jnp.float32))
    a = -jnp.exp(a_log.astype(jnp.float32))
    y = ssd_chunked(xh, dt, a,
                    b_mat.reshape(bsz, s, SSD_GROUPS, SSD_STATE),
                    c_mat.reshape(bsz, s, SSD_GROUPS, SSD_STATE))
    y = y + d_skip.astype(jnp.float32)[:, None] * xh.astype(jnp.float32)
    y = y.reshape(bsz, s, SSD_D_INNER).astype(xs.dtype)
    return rms_norm(y * jax.nn.silu(z), norm_w)

def sgu_branch(uv, ln_w, ln_b, w_spatial, b_spatial):
    uv = jax.nn.gelu(uv)
    u, v = jnp.split(uv, 2, axis=-1)
    v = layer_norm(v, ln_w, ln_b)
    bsz, s = v.shape[0], v.shape[1]
    nc = s // SGU_CHUNK
    vc = v.reshape(bsz, nc, SGU_CHUNK, SGU_GROUPS, SGU_GROUP_DIM)
    w_causal = w_spatial * jnp.tril(jnp.ones((SGU_CHUNK, SGU_CHUNK), w_spatial.dtype))
    mixed = jnp.einsum('gts,bcsgd->bctgd', w_causal, vc) + b_spatial.T[None, None, :, :, None]
    return u * mixed.reshape(bsz, s, SGU_WIDTH)

def setup_inputs(seed: int = 0) -> dict:
    key = jax.random.key(seed)
    ks = jax.random.split(key, 24)
    f32 = jnp.float32

    def nrm(k, shape, scale):
        return jax.random.normal(k, shape, f32) * scale

    x = jax.random.normal(ks[0], (BATCH, SEQ, D_MODEL), f32)
    norm1_w = 1.0 + nrm(ks[1], (DEPTH, D_MODEL), 0.02)
    w_in = nrm(ks[2], (DEPTH, D_MODEL, IN_COLS), D_MODEL ** -0.5)
    b_gate = nrm(ks[3], (DEPTH, GATE_IN), 0.1)
    conv_a_w = nrm(ks[4], (DEPTH, SSD_CONV, SSD_XBC), SSD_CONV ** -0.5)
    conv_a_b = nrm(ks[5], (DEPTH, SSD_XBC), 0.02)
    dt0 = jnp.exp(jax.random.uniform(ks[6], (DEPTH, SSD_HEADS), f32,
                                     float(np.log(1e-3)), float(np.log(1e-1))))
    dt_bias = dt0 + jnp.log(-jnp.expm1(-dt0))
    a_log = jnp.log(jax.random.uniform(ks[7], (DEPTH, SSD_HEADS), f32, 1.0, 16.0))
    d_skip = 1.0 + nrm(ks[8], (DEPTH, SSD_HEADS), 0.1)
    ssd_norm_w = 1.0 + nrm(ks[9], (DEPTH, SSD_D_INNER), 0.02)
    uv_b = nrm(ks[10], (DEPTH, SGU_IN), 0.02)
    v_ln_w = 1.0 + nrm(ks[11], (DEPTH, SGU_WIDTH), 0.02)
    v_ln_b = nrm(ks[12], (DEPTH, SGU_WIDTH), 0.02)
    w_spatial = nrm(ks[13], (DEPTH, SGU_GROUPS, SGU_CHUNK, SGU_CHUNK), SGU_CHUNK ** -0.5)
    b_spatial = 1.0 + nrm(ks[14], (DEPTH, SGU_GROUPS, SGU_CHUNK), 0.1)
    w_branch = jnp.concatenate(
        [nrm(ks[15], (DEPTH, SSD_D_INNER, D_MODEL), SSD_D_INNER ** -0.5),
         nrm(ks[16], (DEPTH, SGU_WIDTH, D_MODEL), SGU_WIDTH ** -0.5)], axis=1)
    w_out = nrm(ks[17], (DEPTH, D_MODEL, D_MODEL), D_MODEL ** -0.5)
    norm2_w = 1.0 + nrm(ks[18], (DEPTH, D_MODEL), 0.02)
    w_up = nrm(ks[19], (DEPTH, D_MODEL, 2 * D_FF), D_MODEL ** -0.5)
    conv_f_w = nrm(ks[20], (DEPTH, FFN_CONV, 2 * D_FF), FFN_CONV ** -0.5)
    conv_f_b = nrm(ks[21], (DEPTH, 2 * D_FF), 0.02)
    w_down = nrm(ks[22], (DEPTH, D_FF, D_MODEL), D_FF ** -0.5)
    final_norm_w = 1.0 + nrm(ks[23], (D_MODEL,), 0.02)
    return {"x": x, "norm1_w": norm1_w, "w_in": w_in, "b_gate": b_gate,
            "conv_a_w": conv_a_w, "conv_a_b": conv_a_b, "dt_bias": dt_bias,
            "a_log": a_log, "d_skip": d_skip, "ssd_norm_w": ssd_norm_w,
            "uv_b": uv_b, "v_ln_w": v_ln_w, "v_ln_b": v_ln_b,
            "w_spatial": w_spatial, "b_spatial": b_spatial, "w_branch": w_branch,
            "w_out": w_out, "norm2_w": norm2_w, "w_up": w_up, "conv_f_w": conv_f_w,
            "conv_f_b": conv_f_b, "w_down": w_down, "final_norm_w": final_norm_w}

def reference(x, norm1_w, w_in, b_gate, conv_a_w, conv_a_b, dt_bias, a_log, d_skip,
              ssd_norm_w, uv_b, v_ln_w, v_ln_b, w_spatial, b_spatial, w_branch, w_out,
              norm2_w, w_up, conv_f_w, conv_f_b, w_down, final_norm_w):
    h = x
    for l in range(DEPTH):
        n = rms_norm(h, norm1_w[l])
        proj = n @ w_in[l]
        z, xbc, dt_raw, uv, gates = jnp.split(
            proj, [SSD_D_INNER, SSD_D_INNER + SSD_XBC, SSD_IN, SSD_IN + SGU_IN], axis=-1)
        y_a = ssd_branch(z, xbc, dt_raw, conv_a_w[l], conv_a_b[l], dt_bias[l],
                         a_log[l], d_skip[l], ssd_norm_w[l])
        y_b = sgu_branch(uv + uv_b[l], v_ln_w[l], v_ln_b[l],
                         w_spatial[l], b_spatial[l])
        g_a, g_b = jnp.split(jax.nn.sigmoid(gates + b_gate[l]), 2, axis=-1)
        p_a = y_a @ w_branch[l, :SSD_D_INNER]
        p_b = y_b @ w_branch[l, SSD_D_INNER:]
        h = h + (g_a * p_a + g_b * p_b) @ w_out[l]
        n = rms_norm(h, norm2_w[l])
        up = causal_dwconv(n @ w_up[l], conv_f_w[l], conv_f_b[l])
        a_up, v_up = jnp.split(up, 2, axis=-1)
        h = h + (jax.nn.silu(a_up) * v_up) @ w_down[l]
    return rms_norm(h, final_norm_w)


_drawn_inputs = setup_inputs


def setup_inputs(seed=0):
    import zlib

    import numpy as np

    out = dict(_drawn_inputs(seed))
    spreads = {}
    factors = {'norm1_w': 2.87,
     'conv_a_b': 4.032,
     'ssd_norm_w': 5.872,
     'uv_b': 5.99,
     'v_ln_w': 8.0,
     'v_ln_b': 8.0,
     'norm2_w': 4.562,
     'conv_f_b': 4.399,
     'final_norm_w': 2.905}
    for name, (base, spread) in spreads.items():
        noise = np.random.default_rng([zlib.crc32(name.encode()), seed]).standard_normal(out[name].shape)
        drawn = base * np.exp(spread * noise) if base else spread * noise
        out[name] = __import__('jax').numpy.asarray(drawn.astype(out[name].dtype))
    for name, factor in factors.items():
        out[name] = (out[name] * factor).astype(out[name].dtype)
    return out
```

```python
from contextlib import ExitStack, contextmanager

import concourse.bass as bass
from concourse import mybir

F32 = mybir.dt.float32
F32R = mybir.dt.float32r
BF16 = mybir.dt.bfloat16
ALU = mybir.AluOpType
ACT = mybir.ActivationFunctionType

P = 128
W = 512
D = 1024
S = 512
NT = S // P
KD = D // P
DI = 2048
NH = 32
HD = 64
NG = 4
HG = NH // NG
SG = 8
FF = 2816
KF = FF // P
FC = KF // 2
NORM_EPS, LN_EPS = 1e-6, 1e-5

Z0, X0, B0, C0, DT0 = 0, DI, 2 * DI, 2 * DI + 512, 2 * DI + 1024
U0 = DT0 + NH
V0, GA0, GB0 = U0 + D, U0 + 2 * D, U0 + 3 * D

Q_B, Q_C, Q_X0, Q_Z, Q_V, Q_U, Q_GB, Q_PB, Q_GA, Q_PA, Q_WO, Q_UP = 0, 1, 2, 3, 10, 12, 14, 16, 18, 20, 24, 26
Q_DOWN = Q_UP + FC
UNITS = 4 * Q_DOWN + KF

J_PAR, J_N1, J_DT, J_CUM, J_TOT, J_PART = 0, 1, 9, 10, 11, 12
J_SSD, SSD_JOBS = 16, 24
J_WT = J_SSD + NG * SSD_JOBS
J_MIX = J_WT + 2
J_YB = J_MIX + SG
J_YA = J_YB + KD
J_M = J_YA + 2 * KD
J_N2 = J_M + KD
A_BT, A_CB = 0, 1
A_HEAD = (2, 3, 4, 5, 10, 11, 12, 13)
A_XS = (6, 7, 8, 9)
A_YD, A_OFF, A_ST = (14, 16, 19, 22), (None, 17, 20, 23), (15, 18, 21, None)

C_CAW, C_CAB, C_N1, C_N2, C_SN, C_BS, C_CFB, C_CF2, C_CF0 = 0, 96, 120, 128, 136, 152, 160, 204, 256


class Steps:

    def __init__(self, eng, sem):
        self.eng, self.sem, self.base, self.k = eng, sem, 0, 0

    def mark(self, ins):
        ins.then_inc(self.sem, 1)
        self.k += 1
        return self.base + self.k

    def wait(self, value):
        self.eng.wait_ge(self.sem, value)

    def link(self, ins):
        self.wait(self.mark(ins))

    @contextmanager
    def loop(self, n, per):
        base = self.base + self.k
        with self.eng.Fori(0, n) as i:
            self.base, self.k = base + i * per, 0
            yield i
            assert self.k == per, f"steps of the body: {self.k}, not {per}"
        self.base, self.k = base + n * per, 0


def hybrid_block(nc, x, norm1_w, w_in, b_gate, conv_a_w, conv_a_b, dt_bias, a_log, d_skip,
                 ssd_norm_w, uv_b, v_ln_w, v_ln_b, w_spatial, b_spatial, w_branch, w_out,
                 norm2_w, w_up, conv_f_w, conv_f_b, w_down, final_norm_w, out):
    ds = bass.ds
    x_v = x.rearrange("b (t p) d -> p (b t) d", p=P)
    out_v = out.rearrange("b (t p) d -> p (b t) d", p=P)
    win_v = w_in.rearrange("l (c p) n -> p (l c) n", p=P)
    wbr_v = w_branch.rearrange("l (c p) n -> p (l c) n", p=P)
    wout_v = w_out.rearrange("l (c p) n -> p (l c) n", p=P)
    wup_v = w_up.rearrange("l (c p) n -> p (l c) n", p=P)
    wdn_v = w_down.rearrange("l (c p) n -> p (l c) n", p=P)

    with ExitStack() as ctx:
        def sb(name, shape, dt=F32, where=ctx):
            return where.enter_context(nc.sbuf_tensor(name, shape, dt))

        def sem(name):
            return ctx.enter_context(nc.semaphore(name))

        raw = sb("raw", [P, 2, 2, W])
        whi = sb("whi", [P, 4, 2, W], F32R)
        wlo = sb("wlo", [P, 4, 2, W], F32R)
        t1h = sb("t1h", [P, KD, S], F32R)
        t1l = sb("t1l", [P, KD, S], F32R)
        ident = sb("ident", [P, P])
        tri = sb("tri", [P, P])
        par = sb("par", [P, 344])
        convx = sb("convx", [P, 2, W + 4])
        rst = sb("rst", [P, 4 * NT])
        msq = sb("msq", [P, 4 * NT])
        minus_half = sb("minus_half", [P, NT])
        ssq = sb("ssq", [P, 3 * NT])
        ssy = sb("ssy", [P, NT, NG])
        bns = sb("bns", [P, NT, 2, 6])
        bna = sb("bna", [P, NT, 2])
        junk = sb("junk", [P, W], BF16)

        s0 = ExitStack()
        xr = sb("xr", [P, NT, D], where=s0)
        xn = sb("xn", [P, NT, D], where=s0)
        prow = sb("prow", [P, 3, P], where=s0)
        s0.close()

        s1 = ExitStack()
        yy = sb("yy", [P, NT, DI], where=s1)
        s2 = ExitStack()
        bf = sb("bf", [P, NG, S], where=s2)
        cf = sb("cf", [P, NG, S], where=s2)
        bcur = sb("bcur", [P, S], where=s2)
        ccur = sb("ccur", [P, S], where=s2)
        bt = sb("bt", [P, NT, P], where=s2)
        cbm = sb("cbm", [P, NT, P], where=s2)
        mm = sb("mm", [P, HG, NT, P], where=s2)
        dif = sb("dif", [P, 2, NT, P], where=s2)
        xf = sb("xf", [P, NT, S], where=s2)
        xdt = sb("xdt", [P, NT, W], where=s2)
        dx = sb("dx", [P, NT, W], where=s2)
        xds = sb("xds", [P, W], where=s2)
        zs = sb("zs", [P, NT, W], where=s2)
        state = sb("state", [P, W], where=s2)
        yt = sb("yt", [P, W], where=s2)
        conv1 = sb("conv1", [P, 2, W], where=s2)
        sel = sb("sel", [P, HG, P], BF16, where=s2)
        acb = sb("acb", [P, NG, S], BF16, where=s2)
        small = sb("small", [P, 3, NH], where=s2)
        acum = sb("acum", [P, NT, NH], where=s2)
        eac = sb("eac", [P, NT, NH], where=s2)
        etot = sb("etot", [P, NT, NH], where=s2)
        dsd = sb("dsd", [P, NT, NH], where=s2)
        dt = sb("dt", [P, NT, NH], where=s2)
        s2.close()
        s2b = ExitStack()
        sb("before_mm", [P, 2 * NG * S + 2 * S + 2 * NT * P], where=s2b)
        ones = sb("ones", [P, P], where=s2b)
        wdt = sb("wdt", [P, KD, NH], where=s2b)
        wdth = sb("wdth", [P, KD, NH], F32R, where=s2b)
        wdtl = sb("wdtl", [P, KD, NH], F32R, where=s2b)
        dpre = sb("dpre", [P, NT, NH], where=s2b)
        dex = sb("dex", [P, NT, NH], where=s2b)
        du = sb("du", [P, NT, NH], where=s2b)
        dln = sb("dln", [P, NT, NH], where=s2b)
        adt = sb("adt", [P, NT, NH], where=s2b)
        part = sb("part", [P, NT, NG, 3, HG], where=s2b)
        parb = sb("parb", [P, NT, NG, HG], BF16, where=s2b)
        s2b.close()

        s3 = ExitStack()
        s4 = ExitStack()
        uvb = sb("uvb", [P, 2 * D], where=s4)
        lnw = sb("lnw", [P, D], where=s4)
        lnb = sb("lnb", [P, D], where=s4)
        vv = sb("vv", [P, NT, D], where=s4)
        s4.close()
        t2h = sb("t2h", [P, KD, S], F32R, where=s3)
        t2l = sb("t2l", [P, KD, S], F32R, where=s3)
        mg = sb("mg", [P, NT, D], where=s3)
        bgt = sb("bgt", [P, 2 * D], where=s3)
        wst = sb("wst", [P, SG, P], where=s3)
        s5 = ExitStack()
        uu = sb("uu", [P, NT, D], where=s5)
        wsp = sb("wsp", [P, SG, P], where=s5)
        s5.close()
        ga = sb("ga", [P, NT, D], where=s3)
        s3.close()
        s1.close()

        hh = sb("hh", [P, NT, D])
        s6 = ExitStack()
        hn = sb("hn", [P, NT, D], where=s6)
        s6.close()
        fth = sb("fth", [P, KF, S], F32R)
        ftl = sb("ftl", [P, KF, S], F32R)
        conv2 = sb("conv2", [P, 4, W])
        fnw = sb("fnw", [P, D])

        acc = ctx.enter_context(nc.psum_tensor("acc", [P, NT, W], F32))
        aux = ctx.enter_context(nc.psum_tensor("aux", [P, 4, W], F32))

        loaded = [sem(f"loaded{i}") for i in range(2)]
        hi_ready = sem("hi_ready")
        lo_ready = sem("lo_ready")
        unit_used = sem("unit_used")
        acc_ready = sem("acc_ready")
        acc_free = sem("acc_free")
        aux_ready = sem("aux_ready")
        aux_free = sem("aux_free")
        aux_hi = sem("aux_hi")
        consts = sem("consts")
        x_in = sem("x_in")
        prow_in = sem("prow_in")
        small_in = sem("small_in")
        wdt_in = sem("wdt_in")
        rows_in = sem("rows_in")
        gate_rows_in = sem("gate_rows_in")
        wsp_in = sem("wsp_in")
        xr_again = sem("xr_again")
        fnw_in = sem("fnw_in")
        squares = sem("squares")
        msq_ready = sem("msq_ready")
        rst_ready = sem("rst_ready")
        normed = sem("normed")
        wdt_hi = sem("wdt_hi")
        wdt_lo = sem("wdt_lo")
        dt_pre = sem("dt_pre")
        dt_exp = sem("dt_exp")
        dt_one = sem("dt_one")
        dt_ln = sem("dt_ln")
        adt_ready = sem("adt_ready")
        cum_ready = sem("cum_ready")
        cum_exp = sem("cum_exp")
        part_ready = sem("part_ready")
        conv_ready = sem("conv_ready")
        silu_ready = sem("silu_ready")
        cur_ready = sem("cur_ready")
        exp_ready = sem("exp_ready")
        m_ready = sem("m_ready")
        xdt_ready = sem("xdt_ready")
        dx_ready = sem("dx_ready")
        xds_ready = sem("xds_ready")
        state_dec = sem("state_dec")
        yt_ready = sem("yt_ready")
        y_ready = sem("y_ready")
        uv_act = sem("uv_act")
        ln_ready = sem("ln_ready")
        v_ready = sem("v_ready")
        wst_ready = sem("wst_ready")
        yb_ready = sem("yb_ready")
        g_act = sem("g_act")
        m_done = sem("m_done")
        flo = sem("flo")
        fsilu = sem("fsilu")
        fconv = sem("fconv")
        fprod = sem("fprod")
        fhi = sem("fhi")
        final = sem("final")
        stored = sem("stored")
        act_steps = sem("act_steps")
        dve_steps = sem("dve_steps")
        pool_steps = sem("pool_steps")

        T_X, T_UP = 8, 8 + 4 * NG

        block = ctx.enter_context(nc.Block())

        @block.sync
        def _(sp):
            def unit(q, p, halves):
                if not (isinstance(q, int) and 4 * q + p < 2):
                    sp.wait_ge(lo_ready, 4 * q + p - 1)
                for dst, src in halves:
                    sp.dma_start(dst, src).then_inc(loaded[p % 2], 16)

            def chunk(q, view, k0, col):
                for p in range(4):
                    unit(q, p, [(raw[:, p % 2, r, :], view[:, k0 + 2 * p + r, ds(col, W)]) for r in range(2)])

            sp.dma_start(prow[0:96, 0, :], conv_a_w.rearrange("l k (t p) -> (l k t) p", p=P)).then_inc(prow_in, 16)
            sp.dma_start(prow[96:120, 0, :], conv_a_b.rearrange("l (t p) -> (l t) p", p=P)).then_inc(prow_in, 16)
            sp.dma_start(prow[120:128, 0, :], norm1_w.rearrange("l (t p) -> (l t) p", p=P)).then_inc(prow_in, 16)
            sp.dma_start(prow[0:8, 1, :], norm2_w.rearrange("l (t p) -> (l t) p", p=P)).then_inc(prow_in, 16)
            sp.dma_start(prow[8:24, 1, :], ssd_norm_w.rearrange("l (t p) -> (l t) p", p=P)).then_inc(prow_in, 16)
            sp.dma_start(prow[24:32, 1, :], b_spatial.rearrange("l g p -> (l g) p")).then_inc(prow_in, 16)
            sp.dma_start(prow[32:76, 1, :], conv_f_b.rearrange("l (t p) -> (l t) p", p=P)).then_inc(prow_in, 16)
            cfw = conv_f_w.rearrange("l k (t p) -> (l k t) p", p=P)
            sp.dma_start(prow[76:120, 1, :], cfw[88:132, :]).then_inc(prow_in, 16)
            sp.dma_start(prow[0:88, 2, :], cfw[0:88, :]).then_inc(prow_in, 16)
            chunk(Q_B, win_v, 0, B0)
            chunk(Q_C, win_v, 0, C0)
            chunk(Q_X0, win_v, 0, X0)
            with sp.Fori(0, NG - 1) as j:
                chunk(Q_Z + 2 * j, win_v, 0, Z0 + j * W)
                chunk(Q_Z + 1 + 2 * j, win_v, 0, X0 + W + j * W)
            chunk(Q_Z + 2 * (NG - 1), win_v, 0, Z0 + (NG - 1) * W)
            row = lambda a: a.rearrange("l n -> (l n)").partition_broadcast(P)
            sp.wait_ge(cur_ready, 2 * NG)
            sp.dma_start(uvb[:, :], row(uv_b)).then_inc(rows_in, 16)
            sp.dma_start(lnw[:, :], row(v_ln_w)).then_inc(rows_in, 16)
            sp.dma_start(lnb[:, :], row(v_ln_b)).then_inc(rows_in, 16)
            chunk(Q_V, win_v, 0, V0)
            chunk(Q_V + 1, win_v, 0, V0 + W)
            sp.wait_ge(y_ready, NT * NG + 1)
            sp.dma_start(bgt[:, :], row(b_gate)).then_inc(gate_rows_in, 16)
            sp.dma_start(wsp[:, :, :], w_spatial.rearrange("l g t s -> t (l g) s")).then_inc(wsp_in, 16)
            for q, view, k0, col in ((Q_U, win_v, 0, U0), (Q_GB, win_v, 0, GB0), (Q_PB, wbr_v, 2 * KD, 0),
                                     (Q_GA, win_v, 0, GA0), (Q_PA, wbr_v, 0, 0), (Q_PA + 2, wbr_v, KD, 0)):
                with sp.Fori(0, 2) as i:
                    chunk(q + i, view, k0, col + i * W)
            sp.wait_ge(aux_ready, J_YA + 2 * KD)
            sp.dma_start(hh[:, :, :], x_v).then_inc(xr_again, 16)
            with sp.Fori(0, 2) as i:
                chunk(Q_WO + i, wout_v, 0, i * W)
            with sp.Fori(0, FC) as i:
                for p in range(4):
                    unit(Q_UP + i, p, [(raw[:, p % 2, r, :].rearrange("p (k n) -> p k n", k=2),
                                        wup_v[:, 2 * p:2 * p + 2, ds(r * FF + i * 256, 256)]) for r in range(2)])
            for n in range(KF):
                c, u = divmod(n, KF // 2)
                unit(Q_DOWN + n // 4, n % 4, [(raw[:, n % 2, r, :], wdn_v[:, 2 * u + r, c * W:(c + 1) * W]) for r in range(2)])
                if n == 0:
                    sp.wait_ge(aux_ready, J_N2 + 1)
                    sp.dma_start(fnw[:, :], final_norm_w.partition_broadcast(P)).then_inc(fnw_in, 16)
            for t in range(NT):
                sp.wait_ge(final, t + 1)
                sp.dma_start(out_v[:, t, :], hh[:, t, :]).then_inc(stored, 16)
            sp.wait_ge(stored, 16 * NT)

        @block.gpsimd
        def _(pool):
            st = Steps(pool, pool_steps)

            def lo(q, p):
                n = 4 * q + p
                pool.wait_ge(hi_ready, n + 1)
                nc.gpsimd.tensor_tensor(wlo[:, p, :, :], raw[:, p % 2, :, :], whi[:, p, :, :].bitcast(F32),
                                        ALU.subtract).then_inc(lo_ready, 1)

            n_root = [0]

            def root(i):
                n_root[0] += 1
                pool.wait_ge(msq_ready, n_root[0])
                cut = slice(i * NT, (i + 1) * NT)
                nc.gpsimd.tensor_tensor(rst[:, cut], msq[:, cut], minus_half[:, :], ALU.pow).then_inc(rst_ready, 1)

            for t, v in ((ident, 0.0), (tri, 1.0), (ones, 1.0), (convx, 0.0), (sel, 0.0), (acb, 0.0)):
                nc.gpsimd.memset(t[:], v).then_inc(consts, 1)
            nc.gpsimd.memset(minus_half[:, :], -0.5).then_inc(y_ready, 1)
            pool.wait_ge(y_ready, 1)
            pool.wait_ge(consts, 6)
            nc.gpsimd.affine_select(out=ident[:, :], in_=ident[:, :], compare_op=ALU.not_equal, fill=1.0,
                                    base=0, pattern=[[-1, P]], channel_multiplier=1).then_inc(consts, 1)
            nc.gpsimd.affine_select(out=tri[:, :], in_=tri[:, :], compare_op=ALU.is_ge, fill=0.0,
                                    base=0, pattern=[[1, P]], channel_multiplier=-1).then_inc(consts, 1)
            for i in range(3):
                nc.gpsimd.affine_select(out=sel[:, :, :], in_=sel[:, :, :], compare_op=ALU.not_equal,
                                        fill=1.0, base=-HG * i, pattern=[[-1, HG], [0, P]],
                                        channel_multiplier=1).then_inc(consts, 1)
                pool.wait_ge(consts, 9 + i)
            root(0)
            for q in range(Q_Z + 1):
                for p in range(4):
                    lo(q, p)

            def group(j):
                qz = Q_Z + 2 * j
                lo(qz + 1, 0)
                lo(qz + 1, 1)
                lo(qz + 1, 2)
                lo(qz + 1, 3)
                for c in range(NT):
                    g8 = ds(j * HG, HG)
                    if c < 3:
                        pool.wait_ge(xdt_ready, 4 * j + c + 1)
                        pool.wait_ge(aux_ready, J_SSD + SSD_JOBS * j + (A_ST[c - 1] + 1 if c else 0))
                        nc.gpsimd.tensor_tensor(
                            xds[:, :].rearrange("p (h d) -> p h d", h=HG),
                            xdt[:, c, :].rearrange("p (h d) -> p h d", h=HG),
                            dsd[:, c, g8].unsqueeze(2).to_broadcast([P, HG, HD]), ALU.mult).then_inc(xds_ready, 1)
                    if c in (1, 2):
                        pool.wait_ge(aux_free, J_SSD + SSD_JOBS * j + A_ST[c - 1] + 1)
                        pool.wait_ge(aux_ready, J_SSD + SSD_JOBS * j + A_OFF[c] + 1)
                        sv = state[:, :].rearrange("p (h d) -> p h d", h=HG)
                        nc.gpsimd.tensor_tensor(sv, sv, etot[:, c, g8].unsqueeze(2).to_broadcast([P, HG, HD]),
                                                ALU.mult).then_inc(state_dec, 1)
                    if c:
                        pool.wait_ge(yt_ready, 3 * j + c)
                    else:
                        pool.wait_ge(aux_free, J_SSD + SSD_JOBS * j + A_YD[0] + 1)
                    pool.wait_ge(acc_free, 4 * qz + c + 1)
                    nc.gpsimd.tensor_tensor(yy[:, c, ds(j * W, W)], yt[:, :], zs[:, c, :],
                                            ALU.mult).then_inc(y_ready, 1)
                    lo(qz + 2, c)

            with pool.Fori(0, NG - 1) as j:
                group(j)
            group(NG - 1)
            for p in range(4):
                lo(Q_U, p)
            root(1)
            root(2)
            for t in range(NT):
                pool.wait_ge(ln_ready, t + 1)
                if t == 0:
                    pool.wait_ge(rows_in, 48)
                st.link(nc.gpsimd.tensor_tensor(vv[:, t, :], vv[:, t, :], lnw[:, :], ALU.mult))
                nc.gpsimd.tensor_tensor(vv[:, t, :], vv[:, t, :], lnb[:, :], ALU.add).then_inc(v_ready, 1)
                lo(Q_U + 1, t)
            with pool.Fori(0, Q_UP + 1 - Q_GB) as i:
                for p in range(4):
                    lo(Q_GB + i, p)
            root(3)
            with pool.Fori(0, FC - 1) as i:
                for p in range(4):
                    lo(Q_UP + 1 + i, p)
            for n in range(KF):
                lo(Q_DOWN + n // 4, n % 4)
            root(0)

        @block.scalar
        def _(act):
            st = Steps(act, act_steps)

            def hi(q, p):
                act.wait_ge(loaded[p % 2], 32 * (2 * q + p // 2) + 32)
                if isinstance(q, int) and q > Q_DOWN:
                    c, u = divmod(4 * (q - 1 - Q_DOWN) + p, KF // 2)
                    if u == KF // 2 - 1:
                        act.wait_ge(acc_ready, 4 * (Q_DOWN + c + 1))
                    else:
                        act.wait_ge(unit_used, 3 * Q_DOWN + c * (KF // 2 - 1) + u + 1)
                elif not (isinstance(q, int) and q == 0):
                    if p == 3:
                        act.wait_ge(acc_ready, 4 * q)
                    else:
                        act.wait_ge(unit_used, 3 * q + p - 2)
                nc.scalar.activation(whi[:, p, :, :], raw[:, p % 2, :, :], ACT.Copy).then_inc(hi_ready, 1)

            def aux_split(job, dst, scale=1.0):
                act.wait_ge(aux_ready, job + 1)
                nc.scalar.activation(dst, aux[:, job % 4, :], ACT.Copy, scale=scale).then_inc(aux_hi, 1)

            def conv_in(a, f, tile):
                act.wait_ge(acc_ready, 4 * a + f + 1)
                if not (isinstance(tile, int) and tile < 2):
                    act.wait_ge(conv_ready, tile - 1)
                nc.scalar.activation(convx[:, f % 2, 3:3 + W], acc[:, f, :], ACT.Copy).then_inc(acc_free, 1)

            def conv_silu(f, tile, dst):
                act.wait_ge(conv_ready, tile + 1)
                nc.scalar.activation(dst, conv1[:, f % 2, :], ACT.Silu).then_inc(silu_ready, 1)

            def conv_chunk(a, tile, dst, between):
                hi(a + 1, 0)
                hi(a + 1, 1)
                hi(a + 1, 2)
                between(0)
                conv_in(a, 0, tile)
                conv_in(a, 1, tile + 1)
                conv_silu(0, tile, dst(0))
                between(1)
                conv_in(a, 2, tile + 2)
                conv_silu(1, tile + 1, dst(1))
                conv_in(a, 3, tile + 3)
                hi(a + 1, 3)
                between(2)
                conv_silu(2, tile + 2, dst(2))
                conv_silu(3, tile + 3, dst(3))

            for t in range(NT):
                act.dma_start(xr[:, t, :], x_v[:, t, :]).then_inc(x_in, 16)
            for t in range(NT):
                act.wait_ge(x_in, 16 * NT)
                nc.scalar.activation(xn[:, t, :], xr[:, t, :], ACT.Square,
                                     accum_out=ssq[:, t:t + 1]).then_inc(squares, 1)
            act.dma_start(wdt[:, :, :], win_v[:, :, DT0:DT0 + NH]).then_inc(wdt_in, 16)
            act.dma_start(small[:, 0, :], dt_bias.rearrange("l n -> (l n)").partition_broadcast(P)).then_inc(small_in, 16)
            act.dma_start(small[:, 1, :], a_log.rearrange("l n -> (l n)").partition_broadcast(P)).then_inc(small_in, 16)
            act.dma_start(small[:, 2, :], d_skip.rearrange("l n -> (l n)").partition_broadcast(P)).then_inc(small_in, 16)
            for p in range(4):
                hi(Q_B, p)
            act.wait_ge(aux_free, J_PAR + 1)
            for k in range(KD):
                aux_split(J_N1 + k, t1h[:, k, :], par[:, C_N1 + k:C_N1 + k + 1])
            act.wait_ge(wdt_in, 16)
            nc.scalar.activation(wdth[:, :, :], wdt[:, :, :], ACT.Copy).then_inc(wdt_hi, 1)
            act.wait_ge(dt_pre, 1)
            nc.scalar.activation(dex[:, :, :], du[:, :, :], ACT.Exp).then_inc(dt_exp, 1)
            act.wait_ge(small_in, 48)
            st.link(nc.scalar.activation(small[:, 1, :], small[:, 1, :], ACT.Exp))
            act.wait_ge(dt_one, 1)
            nc.scalar.activation(dln[:, :, :], du[:, :, :], ACT.Ln).then_inc(dt_ln, 1)
            nothing = lambda where: None

            def decay_tables(where):
                if where == 0:
                    act.wait_ge(aux_free, J_CUM + 1)
                    nc.scalar.activation(eac[:, :, :], acum[:, :, :], ACT.Exp).then_inc(cum_exp, 1)
                    act.wait_ge(cum_ready, 1)
                    nc.scalar.activation(etot[:, :, :], etot[:, :, :], ACT.Exp).then_inc(cum_exp, 1)
                    nc.scalar.activation(dsd[:, :, :], dsd[:, :, :], ACT.Exp).then_inc(cum_exp, 1)
                    for g in range(NG):
                        act.wait_ge(aux_ready, J_PART + g + 1)
                        nc.scalar.activation(acb[0:3 * HG, g, :], aux[0:3 * HG, (J_PART + g) % 4, :], ACT.Copy).then_inc(aux_free, 1)

            conv_chunk(Q_B, 0, lambda f: bf[:, f, :], nothing)
            conv_chunk(Q_C, 4, lambda f: cf[:, f, :], decay_tables)
            conv_chunk(Q_X0, T_X, lambda f: xf[:, f, :], nothing)

            def decay(j, *hs):
                for h in hs:
                    act.wait_ge(aux_free, J_SSD + SSD_JOBS * j + A_HEAD[h] + 1)
                    last = st.mark(nc.scalar.activation(dif[:, h % 2, :, :], dif[:, h % 2, :, :], ACT.Relu, scale=-1.0))
                st.wait(last)
                for h in hs:
                    nc.scalar.activation(dif[:, h % 2, :, :], dif[:, h % 2, :, :], ACT.Exp,
                                         scale=-1.0).then_inc(exp_ready, 1)

            def beside_z(j):
                a = Q_Z + 2 * j
                act.wait_ge(aux_ready, J_SSD + SSD_JOBS * j)
                g = ds(j, 1)
                nc.scalar.activation(bcur[:, :].unsqueeze(1), bf[:, g, :], ACT.Copy).then_inc(cur_ready, 1)
                nc.scalar.activation(ccur[:, :].unsqueeze(1), cf[:, g, :], ACT.Copy).then_inc(cur_ready, 1)
                hi(a + 1, 0)
                hi(a + 1, 1)
                decay(j, 0, 1)
                hi(a + 1, 2)
                decay(j, 2, 3)
                decay(j, 4, 5)
                for t in range(NT):
                    act.wait_ge(acc_ready, 4 * a + t + 1)
                    if t == 0:
                        act.wait_ge(y_ready, 4 * j + 1)
                    nc.scalar.activation(zs[:, t, :], acc[:, t, :], ACT.Silu).then_inc(acc_free, 1)
                hi(a + 1, 3)
                decay(j, 6, 7)

            def y_square(j, c):
                act.wait_ge(y_ready, NT * j + c + 2)
                act.wait_ge(squares, NT + NT * j + c)
                nc.scalar.activation(junk[:, :], yy[:, c, ds(j * W, W)], ACT.Square,
                                     accum_out=ssy[:, c, ds(j, 1)]).then_inc(squares, 1)

            with st.loop(NG - 1, HG) as j:
                beside_z(j)
                conv_chunk(Q_Z + 1 + 2 * j, T_X + 4 + 4 * j, lambda f: xf[:, f, :],
                           lambda where: y_square(j, where) if where < 3 else None)
                y_square(j, 3)
            beside_z(NG - 1)
            for p in range(4):
                hi(Q_V + 1, p)
            for c in range(NT):
                y_square(NG - 1, c)

            def activate(a, t, i, dst, func, done):
                act.wait_ge(acc_free, 4 * a + t + 1)
                cut = dst[:, t, ds(i * W, W)]
                nc.scalar.activation(cut, cut, func).then_inc(done, 1)

            def activated(q, i, dst, func, done):
                for p in range(3):
                    hi(q + 1, p)
                for t in range(NT):
                    activate(q, t, i, dst, func, done)
                    if t == 2:
                        hi(q + 1, 3)

            GELU = ACT.Gelu_apprx_tanh
            for t in range(NT):
                activate(Q_V, t, 0, vv, GELU, uv_act)
            activated(Q_V + 1, 1, vv, GELU, uv_act)
            with act.Fori(0, 2) as i:
                activated(Q_U + i, i, uu, GELU, uv_act)
            activated(Q_GB, 0, mg, ACT.Sigmoid, g_act)
            split_yb = lambda *ks: [aux_split(J_YB + k, t2h[:, k, :]) for k in ks]
            hi(Q_GB + 2, 0)
            hi(Q_GB + 2, 1)
            split_yb(0, 1)
            hi(Q_GB + 2, 2)
            split_yb(2, 3, 4, 5)
            hi(Q_GB + 2, 3)
            split_yb(6, 7)
            for t in range(NT):
                activate(Q_GB + 1, t, 1, mg, ACT.Sigmoid, g_act)
            with act.Fori(0, 2) as i:
                for p in range(4):
                    hi(Q_PB + 1 + i, p)
            sn = lambda k: par[:, C_SN + k:C_SN + k + 1]
            for i in range(2):
                hi(Q_GA + 1 + i, 0)
                hi(Q_GA + 1 + i, 1)
                aux_split(J_YA + 4 * i, t2h[:, 4 * i, :], sn(4 * i))
                aux_split(J_YA + 4 * i + 1, t2h[:, 4 * i + 1, :], sn(4 * i + 1))
                hi(Q_GA + 1 + i, 2)
                aux_split(J_YA + 4 * i + 2, t2h[:, 4 * i + 2, :], sn(4 * i + 2))
                aux_split(J_YA + 4 * i + 3, t2h[:, 4 * i + 3, :], sn(4 * i + 3))
                for t in range(NT):
                    activate(Q_GA + i, t, i, ga, ACT.Sigmoid, g_act)
                hi(Q_GA + 1 + i, 3)
            for i in range(2):
                for p in range(4):
                    hi(Q_PA + 1 + i, p)
                    aux_split(J_YA + KD + 4 * i + p, t1h[:, 4 * i + p, :], sn(KD + 4 * i + p))
            for p in range(4):
                hi(Q_PA + 3, p)
            split_m = lambda *ks: [aux_split(J_M + k, t2h[:, k, :]) for k in ks]
            hi(Q_WO, 0)
            hi(Q_WO, 1)
            split_m(0, 1)
            hi(Q_WO, 2)
            split_m(2, 3)
            hi(Q_WO, 3)
            split_m(4, 5, 6, 7)
            for i in range(2):
                for p in range(4):
                    hi(Q_WO + 1 + i, p)
            for t in range(NT):
                act.wait_ge(acc_free, 4 * (Q_WO + 1) + t + 1)
                nc.scalar.activation(hn[:, t, :], hh[:, t, :], ACT.Square,
                                     accum_out=ssq[:, NT + t:NT + t + 1]).then_inc(squares, 1)
            for k in range(KD):
                aux_split(J_N2 + k, t1h[:, k, :], par[:, C_N2 + k:C_N2 + k + 1])

            def ffn(i):
                q, tile = Q_UP + i, T_UP + 4 * i
                for p in range(3):
                    hi(q + 1, p)
                conv_in(q, 0, tile)
                conv_in(q, 1, tile + 1)
                for f in range(2):
                    act.wait_ge(conv_ready, tile + f + 1)
                    nc.scalar.activation(conv2[:, f, :], conv2[:, f, :], ACT.Silu).then_inc(fsilu, 1)
                    conv_in(q, 2 + f, tile + 2 + f)
                hi(q + 1, 3)
                for f in range(2):
                    act.wait_ge(fprod, 2 * i + f + 1)
                    nc.scalar.activation(fth[:, ds(2 * i + f, 1), :], conv2[:, 2 + f, :].unsqueeze(1),
                                         ACT.Copy).then_inc(fhi, 1)

            act.preload_act_table(ACT.Silu)
            with act.Fori(0, FC) as i:
                ffn(i)
            for n in range(4, KF):
                hi(Q_DOWN + n // 4, n % 4)
            for t in range(NT):
                act.wait_ge(acc_free, 4 * (Q_DOWN + 1) + t + 1)
                act.wait_ge(squares, 2 * NT + NT * NG + t)
                nc.scalar.activation(conv2[:, 0:2, :].rearrange("p a n -> p (a n)"), hh[:, t, :], ACT.Square,
                                     accum_out=ssq[:, 2 * NT + t:2 * NT + t + 1]).then_inc(squares, 1)

        @block.vector
        def _(dve):
            st = Steps(dve, dve_steps)
            V = nc.vector
            tok = lambda ap: ap.unsqueeze(1).to_broadcast([P, NT, NH])
            v4 = lambda ap: ap.rearrange("p (t n) -> p t n", t=4)
            vh = lambda ap: ap.rearrange("p (h d) -> p h d", h=HG)
            heads = lambda ap: ap.unsqueeze(2).to_broadcast([P, HG, HD])
            flat = lambda ap: ap.rearrange("p t n -> p (t n)")
            causal = tri[:, :].unsqueeze(1).to_broadcast([P, 4, P])

            n_root = [0]

            def rsqrt(i, src, n, eps, wait=True):
                V.tensor_scalar(msq[:, i * NT:(i + 1) * NT], src, 1.0 / n, eps, ALU.mult,
                                ALU.add).then_inc(msq_ready, 1)
                n_root[0] += 1
                if wait:
                    dve.wait_ge(rst_ready, n_root[0])

            n_hi = [0]

            def transposed(job, dst_l, dst_h, scale=1.0):
                n_hi[0] += 1
                dve.wait_ge(aux_hi, n_hi[0])
                V.scalar_tensor_tensor(dst_l, aux[:, job % 4, :], scale, dst_h.bitcast(F32), ALU.mult,
                                       ALU.subtract).then_inc(aux_free, 1)

            dve.wait_ge(squares, NT)
            rsqrt(0, ssq[:, 0:NT], D, NORM_EPS)
            for t in range(NT):
                V.tensor_scalar(xn[:, t, :], xr[:, t, :], rst[:, t:t + 1], None, ALU.mult).then_inc(normed, 1)
            dve.wait_ge(aux_ready, J_PAR + 1)
            st.link(V.tensor_copy(par[:, 0:248], aux[:, 0, 0:248]))
            V.tensor_copy(par[:, 256:344], aux[:, 0, 256:344]).then_inc(aux_free, 1)
            dve.wait_ge(aux_free, J_PAR + 1)
            for k in range(KD):
                transposed(J_N1 + k, t1l[:, k, :], t1h[:, k, :], par[:, C_N1 + k:C_N1 + k + 1])
            dve.wait_ge(wdt_hi, 1)
            V.tensor_tensor(wdtl[:, :, :], wdt[:, :, :], wdth[:, :, :].bitcast(F32), ALU.subtract).then_inc(wdt_lo, 1)

            bank3 = lambda job: aux[:, job % 4, 0:P].rearrange("p (t h) -> p t h", t=NT)
            dve.wait_ge(aux_ready, J_DT + 1)
            dve.wait_ge(small_in, 48)
            V.tensor_tensor(dpre[:, :, :], bank3(J_DT), tok(small[:, 0, :]), ALU.add).then_inc(aux_free, 1)
            dve.wait_ge(aux_free, J_DT + 1)
            V.scalar_tensor_tensor(du[:, :, :], dpre[:, :, :], -1.0, dpre[:, :, :], ALU.mult,
                                   ALU.min).then_inc(dt_pre, 1)
            dve.wait_ge(dt_exp, 1)
            V.tensor_scalar(du[:, :, :], dex[:, :, :], 1.0, None, ALU.add).then_inc(dt_one, 1)
            dve.wait_ge(dt_one, 1)
            st.link(V.scalar_tensor_tensor(dex[:, :, :], du[:, :, :], 1.0, dex[:, :, :], ALU.subtract, ALU.subtract))
            st.link(V.reciprocal(adt[:, :, :], du[:, :, :]))
            st.link(V.tensor_tensor(adt[:, :, :], adt[:, :, :], dex[:, :, :], ALU.mult))
            dve.wait_ge(dt_ln, 1)
            st.link(V.tensor_tensor(dln[:, :, :], dln[:, :, :], adt[:, :, :], ALU.subtract))
            st.link(V.scalar_tensor_tensor(dt[:, :, :], dpre[:, :, :], 0.0, dln[:, :, :], ALU.max, ALU.add))
            dve.wait_ge(act_steps, 1)
            V.scalar_tensor_tensor(adt[:, :, :], dt[:, :, :], -1.0, tok(small[:, 1, :]), ALU.mult,
                                   ALU.mult).then_inc(adt_ready, 1)

            def conv(f, taps, wcols, bcol, dst):
                off = 4 - taps
                src = convx[:, f % 2, :]
                st.link(V.tensor_scalar(dst, src[:, off:off + W], par[:, wcols[0]], par[:, bcol], ALU.mult, ALU.add))
                for i in range(1, taps):
                    ins = V.scalar_tensor_tensor(dst, src[:, off + i:off + i + W], par[:, wcols[i]], dst,
                                                 ALU.mult, ALU.add)
                    if i < taps - 1:
                        st.link(ins)
                    else:
                        ins.then_inc(conv_ready, 1)

            def conv_a(a, f, tile, col):
                dve.wait_ge(acc_free, 4 * a + f + 1)
                if not (isinstance(tile, int) and tile < 2):
                    dve.wait_ge(silu_ready, tile - 1)
                conv(f, 4, [ds(C_CAW + 24 * i + col, 1) for i in range(4)], ds(C_CAB + col, 1), conv1[:, f % 2, :])

            for f in range(4):
                conv_a(Q_B, f, f, 16 + f)

            dve.wait_ge(aux_ready, J_CUM + 1)
            V.tensor_copy(acum[:, :, :], bank3(J_CUM)).then_inc(aux_free, 1)
            dve.wait_ge(aux_free, J_CUM + 1)
            of_group = lambda ap: ap.rearrange("p t (g h) -> p t g h", g=NG)
            for t in range(NT):
                src = acum[:, t, :].rearrange("p (g h) -> p g h", g=NG)
                for i in range(2):
                    st.link(V.tensor_copy(parb[:, t, :, :], src))
                    st.link(V.tensor_copy(part[:, t, :, i, :], parb[:, t, :, :]))
                    ins = V.tensor_tensor(part[:, t, :, 2, :], src, part[:, t, :, i, :], ALU.subtract)
                    if i == 0:
                        st.link(ins)
                        src = part[:, t, :, 2, :]
                    else:
                        ins.then_inc(part_ready, 1)
            dve.wait_ge(aux_ready, J_TOT + 1)
            V.tensor_copy(etot[:, :, :], bank3(J_TOT)).then_inc(aux_free, 1)
            dve.wait_ge(aux_free, J_TOT + 1)
            V.tensor_tensor(dsd[:, :, :], etot[:, :, :], acum[:, :, :], ALU.subtract).then_inc(cum_ready, 1)

            for f in range(4):
                conv_a(Q_C, f, 4 + f, 20 + f)
            for f in range(4):
                conv_a(Q_X0, f, T_X + f, f)

            dve.wait_ge(cum_exp, 3)

            def beside_z(j):
                base = J_SSD + SSD_JOBS * j
                bank = lambda k: aux[:, (J_SSD + k) % 4, :]
                g8 = ds(HG * j, HG)

                def exponent(h):
                    dve.wait_ge(aux_ready, base + A_HEAD[h] + 1)
                    if h >= 2:
                        dve.wait_ge(m_ready, HG * j + h - 1)
                    V.tensor_tensor(dif[:, h % 2, :, :], v4(bank(A_HEAD[h])),
                                    acum[:, :, ds(HG * j + h, 1)].to_broadcast([P, NT, P]),
                                    ALU.subtract).then_inc(aux_free, 1)

                def masked(h):
                    dve.wait_ge(exp_ready, HG * j + h + 1)
                    V.tensor_tensor(mm[:, h, :, :], dif[:, h % 2, :, :], cbm[:, :, :], ALU.mult).then_inc(m_ready, 1)

                def tokens(c):
                    dve.wait_ge(aux_ready, base + A_XS[c] + 1)
                    V.tensor_tensor(vh(xdt[:, c, :]), vh(bank(A_XS[c])), heads(dt[:, c, g8]),
                                    ALU.mult).then_inc(xdt_ready, 1)
                    V.tensor_tensor(vh(dx[:, c, :]), vh(bank(A_XS[c])), heads(small[:, 2, g8]),
                                    ALU.mult).then_inc(aux_free, 1)

                dve.wait_ge(aux_ready, base + A_BT + 1)
                V.tensor_copy(bt[:, :, :], v4(bank(A_BT))).then_inc(aux_free, 1)
                dve.wait_ge(aux_ready, base + A_CB + 1)
                V.tensor_tensor(cbm[:, :, :], v4(bank(A_CB)), causal, ALU.mult).then_inc(aux_free, 1)
                exponent(0)
                exponent(1)
                dve.wait_ge(aux_free, base + A_CB + 1)
                masked(0)
                exponent(2)
                masked(1)
                exponent(3)
                tokens(0)
                tokens(1)
                masked(2)
                masked(3)
                tokens(2)
                tokens(3)
                exponent(4)
                exponent(5)
                masked(4)
                masked(5)
                exponent(6)
                exponent(7)
                masked(6)
                masked(7)

            def ssd_chunk(j, c):
                base = J_SSD + SSD_JOBS * j
                bank = lambda k: aux[:, (J_SSD + k) % 4, :]
                g8 = ds(HG * j, HG)
                dve.wait_ge(aux_ready, base + A_YD[c] + 1)
                dve.wait_ge(y_ready, NT * j + c + 1)
                V.tensor_tensor(yt[:, :], bank(A_YD[c]), dx[:, c, :], ALU.add).then_inc(aux_free, 1)
                if c:
                    dve.wait_ge(aux_ready, base + A_OFF[c] + 1)
                    dve.wait_ge(aux_free, base + A_YD[c] + 1)
                    V.tensor_tensor(vh(dx[:, c, :]), vh(bank(A_OFF[c])), heads(eac[:, c, g8]),
                                    ALU.mult).then_inc(aux_free, 1)
                    dve.wait_ge(aux_free, base + A_OFF[c] + 1)
                    V.tensor_tensor(yt[:, :], yt[:, :], dx[:, c, :], ALU.add).then_inc(yt_ready, 1)
                if c < NT - 1:
                    dve.wait_ge(aux_ready, base + A_ST[c] + 1)
                    if c:
                        dve.wait_ge(state_dec, 2 * j + c)
                        V.tensor_tensor(state[:, :], bank(A_ST[c]), state[:, :], ALU.add).then_inc(aux_free, 1)
                    else:
                        V.tensor_copy(state[:, :], bank(A_ST[c])).then_inc(aux_free, 1)

            with st.loop(NG - 1, 12) as j:
                beside_z(j)
                for c in range(3):
                    ssd_chunk(j, c)
                for f in range(4):
                    conv_a(Q_Z + 1 + 2 * j, f, T_X + 4 + 4 * j + f, 4 * j + 4 + f)
                ssd_chunk(j, 3)
            beside_z(NG - 1)
            for c in range(NT):
                ssd_chunk(NG - 1, c)

            def biased(a, i, dst, bias, col):
                for t in range(NT):
                    dve.wait_ge(acc_ready, 4 * a + t + 1)
                    V.tensor_tensor(dst[:, t, ds(i * W, W)], acc[:, t, :], bias[:, ds(col + i * W, W)],
                                    ALU.add).then_inc(acc_free, 1)

            dve.wait_ge(rows_in, 48)
            dve.wait_ge(y_ready, NT * NG + 1)
            with dve.Fori(0, 2) as i:
                biased(Q_V + i, i, vv, uvb, D)
            dve.wait_ge(squares, NT + NT * NG)
            st.link(V.reduce_sum(ssq[:, NT:2 * NT], ssy[:, :, :], mybir.AxisListType.X))
            rsqrt(1, ssq[:, NT:2 * NT], DI, NORM_EPS, wait=False)
            for i in range(2):
                dve.wait_ge(aux_ready, J_WT + i + 1)
                V.tensor_tensor(wst[:, 4 * i:4 * i + 4, :], v4(aux[:, (J_WT + i) % 4, :]), causal,
                                ALU.mult).then_inc(aux_free, 1)
            for t in range(NT):
                dve.wait_ge(uv_act, NT + t + 1)
                for i in range(2):
                    last = st.mark(V.bn_stats(bns[:, t, i, :], vv[:, t, i * W:(i + 1) * W]))
                st.wait(last)
                st.link(V.bn_aggr(bna[:, t, :], bns[:, t, :, :].rearrange("p a b -> p (a b)")))
            rsqrt(2, bna[:, :, 1], 1, LN_EPS)
            for t in range(NT):
                r = rst[:, 2 * NT + t:2 * NT + t + 1]
                V.tensor_scalar(vv[:, t, :], vv[:, t, :], bna[:, t, 0:1], r, ALU.subtract,
                                ALU.mult).then_inc(ln_ready, 1)
            with dve.Fori(0, 2) as i:
                biased(Q_U + i, i, uu, uvb, 0)
            dve.wait_ge(uv_act, 4 * NT)
            for g in range(SG):
                dve.wait_ge(aux_ready, J_MIX + g + 1)
                ug = uu[:, :, g * P:(g + 1) * P]
                V.scalar_tensor_tensor(ug, v4(aux[:, (J_MIX + g) % 4, :]), par[:, C_BS + g:C_BS + g + 1], ug,
                                       ALU.add, ALU.mult).then_inc(aux_free, 1)
            dve.wait_ge(gate_rows_in, 16)
            biased(Q_GB, 0, mg, bgt, D)
            for k in range(6):
                transposed(J_YB + k, t2l[:, k, :], t2h[:, k, :])
            biased(Q_GB + 1, 1, mg, bgt, D)
            for k in (6, 7):
                transposed(J_YB + k, t2l[:, k, :], t2h[:, k, :])
            dve.wait_ge(g_act, 2 * NT)
            with dve.Fori(0, 2) as i:
                for t in range(NT):
                    dve.wait_ge(acc_ready, 4 * Q_PB + 4 * i + t + 1)
                    m = mg[:, t, ds(i * W, W)]
                    V.tensor_tensor(m, acc[:, t, :], m, ALU.mult).then_inc(acc_free, 1)
            sn = lambda k: par[:, C_SN + k:C_SN + k + 1]
            for i in range(2):
                for k in range(4 * i, 4 * i + 4):
                    transposed(J_YA + k, t2l[:, k, :], t2h[:, k, :], sn(k))
                biased(Q_GA + i, i, ga, bgt, 0)

            n_merge = [0]

            def merge(half, c):
                cut = slice(c * W, (c + 1) * W)
                a = Q_PA + 2 * half + c
                for t in range(NT):
                    dve.wait_ge(acc_ready, 4 * a + t + 1)
                    pa = convx[:, t % 2, 3:3 + W]
                    if n_merge[0] + t >= 2:
                        dve.wait_ge(m_done, n_merge[0] + t - 1)
                    V.scalar_tensor_tensor(pa, acc[:, t, :], rst[:, NT + t:NT + t + 1], ga[:, t, cut],
                                           ALU.mult, ALU.mult).then_inc(acc_free, 1)
                    dve.wait_ge(acc_free, 4 * a + t + 1)
                    V.tensor_tensor(mg[:, t, cut], mg[:, t, cut], pa, ALU.add).then_inc(m_done, 1)
                n_merge[0] += NT

            def second_half(i):
                for k in range(4 * i, 4 * i + 4):
                    transposed(J_YA + KD + k, t1l[:, k, :], t1h[:, k, :], sn(KD + k))

            second_half(0)
            dve.wait_ge(g_act, 4 * NT)
            merge(0, 0)
            second_half(1)
            merge(0, 1)
            merge(1, 0)
            for k in range(4):
                transposed(J_M + k, t2l[:, k, :], t2h[:, k, :])
            merge(1, 1)
            for k in range(4, KD):
                transposed(J_M + k, t2l[:, k, :], t2h[:, k, :])

            def residual(a, c):
                for t in range(NT):
                    dve.wait_ge(acc_ready, 4 * a + t + 1)
                    cut = slice(c * W, (c + 1) * W)
                    V.tensor_tensor(hh[:, t, cut], acc[:, t, :], hh[:, t, cut], ALU.add).then_inc(acc_free, 1)

            dve.wait_ge(xr_again, 16)
            for c in range(2):
                residual(Q_WO + c, c)
            dve.wait_ge(squares, 2 * NT + NT * NG)
            rsqrt(3, ssq[:, NT:2 * NT], D, NORM_EPS)
            for t in range(NT):
                r = rst[:, 3 * NT + t:3 * NT + t + 1]
                V.tensor_scalar(hn[:, t, :], hh[:, t, :], r, None, ALU.mult).then_inc(normed, 1)
            for k in range(KD):
                transposed(J_N2 + k, t1l[:, k, :], t1h[:, k, :], par[:, C_N2 + k:C_N2 + k + 1])

            def ffn(i):
                a, tile = Q_UP + i, T_UP + 4 * i

                def conv_f(f):
                    col = 2 * i + f if f < 2 else KF + 2 * i + f - 2
                    dve.wait_ge(acc_free, 4 * a + f + 1)
                    if not isinstance(i, int):
                        dve.wait_ge(flo if f >= 2 else fprod, 2 * i)
                    conv(f, 3, [ds(C_CF0 + col, 1), ds(C_CF0 + 2 * KF + col, 1), ds(C_CF2 + col, 1)],
                         ds(C_CFB + col, 1), conv2[:, f, :])

                def product(f):
                    dve.wait_ge(conv_ready, tile + 2 + f + 1)
                    dve.wait_ge(fsilu, 2 * i + f + 1)
                    V.tensor_tensor(conv2[:, 2 + f, :], conv2[:, f, :], conv2[:, 2 + f, :],
                                    ALU.mult).then_inc(fprod, 1)

                conv_f(0)
                conv_f(1)
                conv_f(2)
                product(0)
                conv_f(3)
                product(1)
                for f in range(2):
                    dve.wait_ge(fhi, 2 * i + f + 1)
                    V.tensor_tensor(ftl[:, ds(2 * i + f, 1), :], conv2[:, 2 + f, :].unsqueeze(1),
                                    fth[:, ds(2 * i + f, 1), :].bitcast(F32), ALU.subtract).then_inc(flo, 1)

            ffn(0)
            with st.loop(FC - 1, 8) as i:
                ffn(i + 1)

            for c in range(2):
                residual(Q_UP + FC + c, c)
            dve.wait_ge(fnw_in, 16)
            dve.wait_ge(squares, 3 * NT + NT * NG)
            rsqrt(0, ssq[:, 2 * NT:3 * NT], D, NORM_EPS)
            for t in range(NT):
                r = rst[:, t:t + 1]
                V.scalar_tensor_tensor(hh[:, t, :], hh[:, t, :], r, fnw[:, :], ALU.mult, ALU.mult).then_inc(final, 1)

        @block.tensor
        def _(pe):
            MM = nc.tensor.matmul

            def unit(n, slot, first, last, a, acts, ks, kind, at=None):
                pe.wait_ge(lo_ready, n + 1)
                ah, al = acts
                for t in range(4):
                    if first and not (isinstance(a, int) and a == 0):
                        pe.wait_ge(acc_free, 4 * a + t - 3)
                    for r, k in enumerate(ks):
                        for i, (w, x) in enumerate(((whi, ah), (whi, al), (wlo, ah))):
                            flags = dict(start=first and r == 0 and i == 0, stop=last and r == 1 and i == 2)
                            if kind == "tokens":
                                ins = MM(acc[:, t, :], x[:, k, t * P:(t + 1) * P], w[:, slot, r, :], **flags)
                            elif kind == "channels":
                                ins = MM(acc[:, t, :], w[:, slot, r, t * P:(t + 1) * P], x[:, k, :], **flags)
                            else:
                                ins = MM(acc[:, t, :], w[:, slot, t // 2, r * 256 + t % 2 * P:r * 256 + t % 2 * P + P],
                                         x[:, k, :], **flags)
                    if last and t < 3:
                        ins.then_inc(acc_ready, 1)
                ins.then_inc(acc_ready if last else unit_used, 1)

            def gemm(q, a, acts, kind, between=None, parts=None):
                for p in range(4):
                    if parts is not None:
                        pe.wait_ge(aux_free, parts + 2 * p + 2)
                    unit(4 * q + p, p, p == 0, p == 3, a, acts, (2 * p, 2 * p + 1), kind)
                    if between:
                        between(p)

            def job(n, k=None):
                if not (isinstance(n, int) and n < 4):
                    pe.wait_ge(aux_free, n - 3)
                return aux[:, (n if k is None else k) % 4, :]

            def turn(n, src, last_inc=aux_ready):
                bank = job(n)
                for t in range(NT):
                    ins = nc.tensor.transpose(bank[:, t * P:(t + 1) * P], src(t), ident[:, :])
                ins.then_inc(aux_ready, 1)

            t1, t2 = (t1h, t1l), (t2h, t2l)

            pe.wait_ge(consts, 11)
            pe.wait_ge(prow_in, 9 * 16)
            for i, n in enumerate((P, 120, 88)):
                ins = nc.tensor.transpose(aux[:, 0, i * P:i * P + n], prow[0:n, i, :], ident[0:n, 0:n])
            ins.then_inc(aux_ready, 1)
            pe.wait_ge(normed, NT)
            for k in range(KD):
                turn(J_N1 + k, lambda t: xn[:, t, k * P:(k + 1) * P])
            pe.wait_ge(wdt_lo, 1)
            pe.wait_ge(aux_free, J_N1 + KD)
            bank = job(J_DT)
            for t in range(NT):
                for k in range(KD):
                    for i, (x, w) in enumerate(((t1h, wdth), (t1l, wdth), (t1h, wdtl))):
                        ins = MM(bank[:, t * NH:(t + 1) * NH], x[:, k, t * P:(t + 1) * P], w[:, k, :],
                                 start=k == 0 and i == 0, stop=k == KD - 1 and i == 2)
            ins.then_inc(aux_ready, 1)
            gemm(Q_B, Q_B, t1, "channels")
            flat = lambda ap: ap.rearrange("p t n -> p (t n)")

            def cumulative(p):
                if p == 0:
                    pe.wait_ge(adt_ready, 1)
                    for n, m in ((J_CUM, tri), (J_TOT, ones)):
                        MM(job(n)[:, 0:P], m[:, :], flat(adt[:, :, :]), start=True, stop=True).then_inc(aux_ready, 1)
                elif p == 2:
                    pe.wait_ge(part_ready, NT)
                    for g in range(NG):
                        bank = job(J_PART + g)
                        for t in range(NT):
                            ins = nc.tensor.transpose(bank[0:3 * HG, t * P:(t + 1) * P],
                                                      part[:, t, g, :, :].rearrange("p a h -> p (a h)"), ident[:, :])
                        ins.then_inc(aux_ready, 1)

            gemm(Q_C, Q_C, t1, "channels", cumulative)
            gemm(Q_X0, Q_X0, t1, "channels")
            pe.wait_ge(aux_free, J_SSD)

            def decays(j):
                base = J_SSD + SSD_JOBS * j
                bank = lambda k: job(base + k, J_SSD + k)

                def head(h):
                    MM(bank(A_HEAD[h]), sel[:, h, :], acb[:, ds(j, 1), :].rearrange("p a n -> p (a n)"),
                       start=True, stop=True).then_inc(aux_ready, 1)

                def tokens(c):
                    b = bank(A_XS[c])
                    for f in range(4):
                        ins = nc.tensor.transpose(b[:, f * P:(f + 1) * P], xf[:, f, c * P:(c + 1) * P], ident[:, :])
                    ins.then_inc(aux_ready, 1)

                def between(p):
                    if p == 0:
                        pe.wait_ge(cur_ready, 2 * j + 2)
                        b = bank(A_BT)
                        for c in range(NT):
                            ins = nc.tensor.transpose(b[:, c * P:(c + 1) * P], bcur[:, c * P:(c + 1) * P], ident[:, :])
                        ins.then_inc(aux_ready, 1)
                        b = bank(A_CB)
                        for c in range(NT):
                            cc = slice(c * P, (c + 1) * P)
                            ins = MM(b[:, cc], bcur[:, cc], ccur[:, cc], start=True, stop=True)
                        ins.then_inc(aux_ready, 1)
                        head(0)
                        head(1)
                    elif p == 1:
                        head(2)
                        head(3)
                        pe.wait_ge(silu_ready, T_X + 4 * j + 4)
                        tokens(0)
                        tokens(1)
                    elif p == 2:
                        tokens(2)
                        tokens(3)
                        head(4)
                        head(5)
                    else:
                        head(6)
                        head(7)

                return between

            def chunks(j):
                base = J_SSD + SSD_JOBS * j
                bank = lambda k: job(base + k, J_SSD + k)

                def between(c):
                    if c == 0:
                        pe.wait_ge(m_ready, HG * j + HG)
                        pe.wait_ge(xdt_ready, NT * j + NT)
                    b = bank(A_YD[c])
                    for h in range(HG):
                        cut = slice(h * HD, (h + 1) * HD)
                        ins = MM(b[:, cut], mm[:, h, c, :], xdt[:, c, cut], start=True, stop=True)
                    ins.then_inc(aux_ready, 1)
                    if c:
                        pe.wait_ge(aux_free, base + A_ST[c - 1] + 1)
                        MM(bank(A_OFF[c]), ccur[:, c * P:(c + 1) * P], state[:, :], start=True,
                           stop=True).then_inc(aux_ready, 1)
                    if c < NT - 1:
                        pe.wait_ge(xds_ready, 3 * j + c + 1)
                        MM(bank(A_ST[c]), bt[:, c, :], xds[:, :], start=True, stop=True).then_inc(aux_ready, 1)

                return between

            with pe.Fori(0, NG - 1) as j:
                gemm(Q_Z + 2 * j, Q_Z + 2 * j, t1, "tokens", decays(j))
                gemm(Q_Z + 1 + 2 * j, Q_Z + 1 + 2 * j, t1, "channels", chunks(j))
            gemm(Q_Z + 2 * NG - 2, Q_Z + 2 * NG - 2, t1, "tokens", decays(NG - 1))
            gemm(Q_V, Q_V, t1, "tokens", chunks(NG - 1))
            gemm(Q_V + 1, Q_V + 1, t1, "tokens")

            pe.wait_ge(wsp_in, 16)
            for i in range(2):
                turn(J_WT + i, lambda t: wsp[:, 4 * i + t, :])
            with pe.Fori(0, 2) as i:
                gemm(Q_U + i, Q_U + i, t1, "tokens")
            gemm(Q_GB, Q_GB, t1, "tokens", None)
            pe.wait_ge(v_ready, NT)
            pe.wait_ge(aux_free, J_WT + 2)
            for g in range(SG):
                MM(job(J_MIX + g), wst[:, g, :], vv[:, :, g * P:(g + 1) * P], start=True,
                   stop=True).then_inc(aux_ready, 1)

            def turn_yb(p):
                for k in (2 * p, 2 * p + 1):
                    pe.wait_ge(aux_free, J_MIX + k + 1)
                    turn(J_YB + k, lambda t: uu[:, t, k * P:(k + 1) * P])

            gemm(Q_GB + 1, Q_GB + 1, t1, "tokens", turn_yb)
            with pe.Fori(0, 2) as i:
                gemm(Q_PB + i, Q_PB + i, t2, "tokens", parts=J_YB)
            for i in range(2):
                gemm(Q_GA + i, Q_GA + i, t1, "tokens",
                     lambda p: turn(J_YA + 4 * i + p, lambda t: yy[:, t, (4 * i + p) * P:(4 * i + p + 1) * P]))
            for i in range(2):
                def second_half(p):
                    k = KD + 4 * i + p
                    turn(J_YA + k, lambda t: yy[:, t, k * P:(k + 1) * P])

                gemm(Q_PA + i, Q_PA + i, t2, "tokens", second_half, parts=J_YA)
            gemm(Q_PA + 2, Q_PA + 2, t1, "tokens", parts=J_YA + KD)

            def turn_m(p):
                if p == 1:
                    pe.wait_ge(m_done, 3 * NT)
                for k in {1: (0, 1), 2: (2, 3)}.get(p, ()):
                    turn(J_M + k, lambda t: mg[:, t, k * P:(k + 1) * P])

            gemm(Q_PA + 3, Q_PA + 3, t1, "tokens", turn_m)
            pe.wait_ge(m_done, 4 * NT)
            for k in range(4, KD):
                turn(J_M + k, lambda t: mg[:, t, k * P:(k + 1) * P])
            for i in range(2):
                gemm(Q_WO + i, Q_WO + i, t2, "tokens", parts=J_M)

            pe.wait_ge(normed, 2 * NT)
            for k in range(KD):
                turn(J_N2 + k, lambda t: hn[:, t, k * P:(k + 1) * P])
            with pe.Fori(0, FC) as i:
                gemm(Q_UP + i, Q_UP + i, t1, "pairs", parts=J_N2)
            half = KF // 2
            for n in range(KF):
                c, u = divmod(n, half)
                pe.wait_ge(flo, 2 * u + 2)
                unit(4 * Q_DOWN + n, n % 4, u == 0, u == half - 1, Q_UP + FC + c, (fth, ftl),
                     (2 * u, 2 * u + 1), "tokens")


_INS = ["x", "norm1_w", "w_in", "b_gate", "conv_a_w", "conv_a_b", "dt_bias", "a_log", "d_skip", "ssd_norm_w",
        "uv_b", "v_ln_w", "v_ln_b", "w_spatial", "b_spatial", "w_branch", "w_out", "norm2_w", "w_up",
        "conv_f_w", "conv_f_b", "w_down", "final_norm_w"]


def kernel(**inputs):
    import numpy as np
    import concourse.bacc as bacc
    from concourse import mybir as mb
    from concourse.bass_utils import run_bass_kernel_spmd

    nc = bacc.Bacc("TRN2", target_bir_lowering=False, num_devices=1)
    arrays, args = {}, []
    for name in _INS:
        a = np.ascontiguousarray(inputs[name])
        arrays[f"in_{name}"] = a
        args.append(nc.dram_tensor(f"in_{name}", a.shape, mb.dt.from_np(a.dtype), kind="ExternalInput").ap())
    out = nc.dram_tensor("out_0", (1, S, D), F32, kind="ExternalOutput").ap()
    hybrid_block(nc, *args, out)
    return run_bass_kernel_spmd(nc, [arrays], core_ids=[0]).results[0]["out_0"]
```

```python
from contextlib import ExitStack, contextmanager

import concourse.bass as bass
from concourse import mybir

F32 = mybir.dt.float32
F32R = mybir.dt.float32r
BF16 = mybir.dt.bfloat16
ALU = mybir.AluOpType
ACT = mybir.ActivationFunctionType

P = 128
W = 512
D = 1024
S = 512
NT = S // P
KD = D // P
DI = 2048
NH = 32
HD = 64
NG = 4
HG = NH // NG
SG = 8
FF = 2816
KF = FF // P
FC = KF // 2
NORM_EPS, LN_EPS = 1e-6, 1e-5

Z0, X0, B0, C0, DT0 = 0, DI, 2 * DI, 2 * DI + 512, 2 * DI + 1024
U0 = DT0 + NH
V0, GA0, GB0 = U0 + D, U0 + 2 * D, U0 + 3 * D

Q_B, Q_C, Q_X0, Q_Z, Q_V, Q_U, Q_GB, Q_PB, Q_GA, Q_PA, Q_WO, Q_UP = 0, 1, 2, 3, 10, 12, 14, 16, 18, 20, 24, 26
Q_DOWN = Q_UP + FC
UNITS = 4 * Q_DOWN + KF

J_PAR, J_N1, J_DT, J_CUM, J_TOT, J_PART = 0, 1, 9, 10, 11, 12
J_SSD, SSD_JOBS = 16, 24
J_WT = J_SSD + NG * SSD_JOBS
J_MIX = J_WT + 2
J_YB = J_MIX + SG
J_YA = J_YB + KD
J_M = J_YA + 2 * KD
J_N2 = J_M + KD
J_RB = J_N2 + KD
A_BT, A_CB = 0, 1
A_HEAD = (2, 3, 4, 5, 6, 7, 8, 9)
A_XS = (10, 11, 12, 13)
A_YD, A_OFF, A_ST = (14, 16, 19, 22), (None, 17, 20, 23), (15, 18, 21, None)

C_CAW, C_CAB, C_N1, C_N2, C_SN, C_BS, C_CFB, C_CF2, C_CF0 = 0, 96, 120, 128, 136, 152, 160, 204, 256


class Steps:

    def __init__(self, eng, sem):
        self.eng, self.sem, self.base, self.k = eng, sem, 0, 0

    def mark(self, ins):
        ins.then_inc(self.sem, 1)
        self.k += 1
        return self.base + self.k

    def wait(self, value):
        self.eng.wait_ge(self.sem, value)

    def link(self, ins):
        self.wait(self.mark(ins))

    @contextmanager
    def loop(self, n, per):
        base = self.base + self.k
        with self.eng.Fori(0, n) as i:
            self.base, self.k = base + i * per, 0
            yield i
            assert self.k == per, f"steps of the body: {self.k}, not {per}"
        self.base, self.k = base + n * per, 0


def hybrid_block(nc, x, norm1_w, w_in, b_gate, conv_a_w, conv_a_b, dt_bias, a_log, d_skip,
                 ssd_norm_w, uv_b, v_ln_w, v_ln_b, w_spatial, b_spatial, w_branch, w_out,
                 norm2_w, w_up, conv_f_w, conv_f_b, w_down, final_norm_w, out):
    ds = bass.ds
    x_v = x.rearrange("b (t p) d -> p (b t) d", p=P)
    out_v = out.rearrange("b (t p) d -> p (b t) d", p=P)
    win_v = w_in.rearrange("l (c p) n -> p (l c) n", p=P)
    wbr_v = w_branch.rearrange("l (c p) n -> p (l c) n", p=P)
    wout_v = w_out.rearrange("l (c p) n -> p (l c) n", p=P)
    wup_v = w_up.rearrange("l (c p) n -> p (l c) n", p=P)
    wdn_v = w_down.rearrange("l (c p) n -> p (l c) n", p=P)

    with ExitStack() as ctx:
        def sb(name, shape, dt=F32, where=ctx):
            return where.enter_context(nc.sbuf_tensor(name, shape, dt))

        def sem(name):
            return ctx.enter_context(nc.semaphore(name))

        raw = sb("raw", [P, 2, 2, W])
        whi = sb("whi", [P, 4, 2, W], F32R)
        wlo = sb("wlo", [P, 4, 2, W], F32R)
        t1h = sb("t1h", [P, KD, S], F32R)
        t1l = sb("t1l", [P, KD, S], F32R)
        ident = sb("ident", [P, P])
        tri = sb("tri", [P, P])
        par = sb("par", [P, 344])
        convx = sb("convx", [P, 2, W + 4])
        rst = sb("rst", [P, 4 * NT])
        msq = sb("msq", [P, 4 * NT])
        minus_half = sb("minus_half", [P, NT])
        ssq = sb("ssq", [P, 3 * NT])
        ssy = sb("ssy", [P, NT, NG])
        bns = sb("bns", [P, NT, 2, 6])
        bna = sb("bna", [P, NT, 2])
        junk = sb("junk", [P, W], BF16)

        s0 = ExitStack()
        xr = sb("xr", [P, NT, D], where=s0)
        xn = sb("xn", [P, NT, D], where=s0)
        prow = sb("prow", [P, 3, P], where=s0)
        s0.close()

        s1 = ExitStack()
        yy = sb("yy", [P, NT, DI], where=s1)
        s2 = ExitStack()
        bf = sb("bf", [P, NG, S], where=s2)
        cf = sb("cf", [P, NG, S], where=s2)
        bcur = sb("bcur", [P, S], where=s2)
        ccur = sb("ccur", [P, S], where=s2)
        bt = sb("bt", [P, NT, P], where=s2)
        cbm = sb("cbm", [P, NT, P], where=s2)
        mm = sb("mm", [P, HG, NT, P], where=s2)
        dif = sb("dif", [P, 2, NT, P], where=s2)
        xf = sb("xf", [P, NT, S], where=s2)
        xdt = sb("xdt", [P, NT, W], where=s2)
        dx = sb("dx", [P, NT, W], where=s2)
        xds = sb("xds", [P, W], where=s2)
        zs = sb("zs", [P, NT, W], where=s2)
        state = sb("state", [P, W], where=s2)
        yt = sb("yt", [P, W], where=s2)
        conv1 = sb("conv1", [P, 2, W], where=s2)
        sel = sb("sel", [P, HG, P], BF16, where=s2)
        acb = sb("acb", [P, NG, S], BF16, where=s2)
        small = sb("small", [P, 3, NH], where=s2)
        acum = sb("acum", [P, NT, NH], where=s2)
        eac = sb("eac", [P, NT, NH], where=s2)
        etot = sb("etot", [P, NT, NH], where=s2)
        dsd = sb("dsd", [P, NT, NH], where=s2)
        dt = sb("dt", [P, NT, NH], where=s2)
        s2.close()
        s2b = ExitStack()
        sb("before_mm", [P, 2 * NG * S + 2 * S + 2 * NT * P], where=s2b)
        ones = sb("ones", [P, P], where=s2b)
        wdt = sb("wdt", [P, KD, NH], where=s2b)
        wdth = sb("wdth", [P, KD, NH], F32R, where=s2b)
        wdtl = sb("wdtl", [P, KD, NH], F32R, where=s2b)
        dpre = sb("dpre", [P, NT, NH], where=s2b)
        dex = sb("dex", [P, NT, NH], where=s2b)
        du = sb("du", [P, NT, NH], where=s2b)
        dln = sb("dln", [P, NT, NH], where=s2b)
        adt = sb("adt", [P, NT, NH], where=s2b)
        part = sb("part", [P, NT * NG, 3, HG], where=s2b)
        parb = sb("parb", [P, NT * NG, HG], BF16, where=s2b)
        s2b.close()

        s3 = ExitStack()
        s4 = ExitStack()
        uvb = sb("uvb", [P, 2 * D], where=s4)
        lnw = sb("lnw", [P, D], where=s4)
        lnb = sb("lnb", [P, D], where=s4)
        vv = sb("vv", [P, NT, D], where=s4)
        s4.close()
        t2h = sb("t2h", [P, KD, S], F32R, where=s3)
        t2l = sb("t2l", [P, KD, S], F32R, where=s3)
        mg = sb("mg", [P, NT, D], where=s3)
        bgt = sb("bgt", [P, 2 * D], where=s3)
        wst = sb("wst", [P, SG, P], where=s3)
        s5 = ExitStack()
        uu = sb("uu", [P, NT, D], where=s5)
        wsp = sb("wsp", [P, SG, P], where=s5)
        s5.close()
        ga = sb("ga", [P, NT, D], where=s3)
        s3.close()
        s1.close()

        hh = sb("hh", [P, NT, D])
        s6 = ExitStack()
        hn = sb("hn", [P, NT, D], where=s6)
        s6.close()
        fth = sb("fth", [P, KF, S], F32R)
        ftl = sb("ftl", [P, KF, S], F32R)
        conv2 = sb("conv2", [P, 4, W])
        rbc = sb("rbc", [P, S])
        s7 = ExitStack()
        ones2 = sb("ones2", [P, P], where=s7)
        diag = sb("diag", [P, S], where=s7)
        s7.close()
        fnw = sb("fnw", [P, D])

        acc = ctx.enter_context(nc.psum_tensor("acc", [P, NT, W], F32))
        aux = ctx.enter_context(nc.psum_tensor("aux", [P, 4, W], F32))

        loaded = [sem(f"loaded{i}") for i in range(2)]
        hi_ready = sem("hi_ready")
        lo_ready = sem("lo_ready")
        unit_used = sem("unit_used")
        acc_ready = sem("acc_ready")
        acc_free = sem("acc_free")
        aux_ready = sem("aux_ready")
        aux_free = sem("aux_free")
        aux_hi = sem("aux_hi")
        consts = sem("consts")
        x_in = [sem(f"x_in{t}") for t in range(NT)]
        prow_in = sem("prow_in")
        small_in = sem("small_in")
        wdt_in = sem("wdt_in")
        rows_in = sem("rows_in")
        gate_rows_in = sem("gate_rows_in")
        wsp_in = sem("wsp_in")
        xr_again = sem("xr_again")
        fnw_in = sem("fnw_in")
        squares = sem("squares")
        msq_ready = sem("msq_ready")
        rst_ready = sem("rst_ready")
        normed = sem("normed")
        wdt_hi = sem("wdt_hi")
        wdt_lo = sem("wdt_lo")
        dt_pre = sem("dt_pre")
        dt_exp = sem("dt_exp")
        dt_one = sem("dt_one")
        dt_ln = sem("dt_ln")
        diag_ready = sem("diag_ready")
        adt_ready = sem("adt_ready")
        cum_ready = sem("cum_ready")
        cum_exp = sem("cum_exp")
        part_ready = sem("part_ready")
        conv_ready = sem("conv_ready")
        silu_ready = sem("silu_ready")
        cur_ready = sem("cur_ready")
        exp_ready = sem("exp_ready")
        m_ready = sem("m_ready")
        xdt_ready = sem("xdt_ready")
        dx_ready = sem("dx_ready")
        xds_ready = sem("xds_ready")
        state_dec = sem("state_dec")
        yt_ready = sem("yt_ready")
        y_ready = sem("y_ready")
        uv_act = sem("uv_act")
        ln_ready = sem("ln_ready")
        v_ready = sem("v_ready")
        wst_ready = sem("wst_ready")
        yb_ready = sem("yb_ready")
        g_act = sem("g_act")
        m_done = sem("m_done")
        flo = sem("flo")
        fsilu = sem("fsilu")
        fconv = sem("fconv")
        fprod = sem("fprod")
        fhi = sem("fhi")
        final = sem("final")
        stored = sem("stored")
        act_steps = sem("act_steps")
        dve_steps = sem("dve_steps")
        pool_steps = sem("pool_steps")

        T_X, T_UP = 8, 8 + 4 * NG

        block = ctx.enter_context(nc.Block())

        @block.sync
        def _(sp):
            def unit(q, p, halves):
                if not (isinstance(q, int) and 4 * q + p < 2):
                    sp.wait_ge(lo_ready, 4 * q + p - 1)
                for dst, src in halves:
                    sp.dma_start(dst, src).then_inc(loaded[p % 2], 16)

            def chunk(q, view, k0, col):
                for p in range(4):
                    unit(q, p, [(raw[:, p % 2, r, :], view[:, k0 + 2 * p + r, ds(col, W)]) for r in range(2)])

            for t in range(NT):
                sp.dma_start(xr[:, t, :], x_v[:, t, :]).then_inc(x_in[t], 16)
            chunk(Q_B, win_v, 0, B0)
            chunk(Q_C, win_v, 0, C0)
            chunk(Q_X0, win_v, 0, X0)
            with sp.Fori(0, NG - 1) as j:
                chunk(Q_Z + 2 * j, win_v, 0, Z0 + j * W)
                chunk(Q_Z + 1 + 2 * j, win_v, 0, X0 + W + j * W)
            chunk(Q_Z + 2 * (NG - 1), win_v, 0, Z0 + (NG - 1) * W)
            row = lambda a: a.rearrange("l n -> (l n)").partition_broadcast(P)
            sp.wait_ge(cur_ready, 2 * NG)
            sp.dma_start(uvb[:, :], row(uv_b)).then_inc(rows_in, 16)
            sp.dma_start(lnw[:, :], row(v_ln_w)).then_inc(rows_in, 16)
            sp.dma_start(lnb[:, :], row(v_ln_b)).then_inc(rows_in, 16)
            chunk(Q_V, win_v, 0, V0)
            chunk(Q_V + 1, win_v, 0, V0 + W)
            sp.wait_ge(y_ready, NT * NG + 1)
            sp.dma_start(bgt[:, :], row(b_gate)).then_inc(gate_rows_in, 16)
            sp.dma_start(wsp[:, :, :], w_spatial.rearrange("l g t s -> t (l g) s")).then_inc(wsp_in, 16)
            for q, view, k0, col in ((Q_U, win_v, 0, U0), (Q_GB, win_v, 0, GB0), (Q_PB, wbr_v, 2 * KD, 0),
                                     (Q_GA, win_v, 0, GA0), (Q_PA, wbr_v, 0, 0), (Q_PA + 2, wbr_v, KD, 0)):
                with sp.Fori(0, 2) as i:
                    chunk(q + i, view, k0, col + i * W)
            sp.wait_ge(aux_ready, J_YA + 2 * KD)
            sp.dma_start(hh[:, :, :], x_v).then_inc(xr_again, 16)
            with sp.Fori(0, 2) as i:
                chunk(Q_WO + i, wout_v, 0, i * W)
            with sp.Fori(0, FC) as i:
                for p in range(4):
                    unit(Q_UP + i, p, [(raw[:, p % 2, r, :].rearrange("p (k n) -> p k n", k=2),
                                        wup_v[:, 2 * p:2 * p + 2, ds(r * FF + i * 256, 256)]) for r in range(2)])
            for n in range(KF):
                c, u = divmod(n, KF // 2)
                unit(Q_DOWN + n // 4, n % 4, [(raw[:, n % 2, r, :], wdn_v[:, 2 * u + r, c * W:(c + 1) * W]) for r in range(2)])
                if n == 0:
                    sp.wait_ge(aux_ready, J_RB + 1)
                    sp.dma_start(fnw[:, :], final_norm_w.partition_broadcast(P)).then_inc(fnw_in, 16)
            for t in range(NT):
                sp.wait_ge(final, t + 1)
                sp.dma_start(out_v[:, t, :], hh[:, t, :]).then_inc(stored, 16)
            sp.wait_ge(stored, 16 * NT)

        @block.gpsimd
        def _(pool):
            st = Steps(pool, pool_steps)

            def lo(q, p):
                n = 4 * q + p
                pool.wait_ge(hi_ready, n + 1)
                nc.gpsimd.tensor_tensor(wlo[:, p, :, :], raw[:, p % 2, :, :], whi[:, p, :, :].bitcast(F32),
                                        ALU.subtract).then_inc(lo_ready, 1)

            n_root = [0]

            def root(i, lo=0, hi=NT):
                n_root[0] += 1
                pool.wait_ge(msq_ready, n_root[0])
                cut = slice(i * NT + lo, i * NT + hi)
                nc.gpsimd.tensor_tensor(rst[:, cut], msq[:, cut], minus_half[:, lo:hi], ALU.pow).then_inc(rst_ready, 1)

            for t, v in ((ident, 0.0), (tri, 1.0), (ones, 1.0), (convx, 0.0)):
                nc.gpsimd.memset(t[:], v).then_inc(consts, 1)
            nc.gpsimd.memset(minus_half[:, :], -0.5).then_inc(y_ready, 1)
            pool.wait_ge(y_ready, 1)
            pool.wait_ge(consts, 4)
            nc.gpsimd.affine_select(out=ident[:, :], in_=ident[:, :], compare_op=ALU.not_equal, fill=1.0,
                                    base=0, pattern=[[-1, P]], channel_multiplier=1).then_inc(consts, 1)
            nc.gpsimd.affine_select(out=tri[:, :], in_=tri[:, :], compare_op=ALU.is_ge, fill=0.0,
                                    base=0, pattern=[[1, P]], channel_multiplier=-1).then_inc(consts, 1)
            root(0)
            for t in (sel, acb):
                nc.gpsimd.memset(t[:], 0.0).then_inc(consts, 1)
            pool.wait_ge(consts, 8)
            for i in range(3):
                nc.gpsimd.affine_select(out=sel[:, :, :], in_=sel[:, :, :], compare_op=ALU.not_equal,
                                        fill=1.0, base=-HG * i, pattern=[[-1, HG], [0, P]],
                                        channel_multiplier=1).then_inc(consts, 1)
                pool.wait_ge(consts, 9 + i)
            for q in range(Q_Z + 1):
                for p in range(4):
                    lo(q, p)

            def group(j):
                qz = Q_Z + 2 * j
                lo(qz + 1, 0)
                lo(qz + 1, 1)
                lo(qz + 1, 2)
                lo(qz + 1, 3)
                for c in range(NT):
                    g8 = ds(j * HG, HG)
                    if c < 3:
                        pool.wait_ge(xdt_ready, 4 * j + c + 1)
                        pool.wait_ge(aux_ready, J_SSD + SSD_JOBS * j + (A_ST[c - 1] + 1 if c else 0))
                        nc.gpsimd.tensor_tensor(
                            xds[:, :].rearrange("p (h d) -> p h d", h=HG),
                            xdt[:, c, :].rearrange("p (h d) -> p h d", h=HG),
                            dsd[:, c, g8].unsqueeze(2).to_broadcast([P, HG, HD]), ALU.mult).then_inc(xds_ready, 1)
                    if c in (1, 2):
                        pool.wait_ge(aux_free, J_SSD + SSD_JOBS * j + A_ST[c - 1] + 1)
                        pool.wait_ge(aux_ready, J_SSD + SSD_JOBS * j + A_OFF[c] + 1)
                        sv = state[:, :].rearrange("p (h d) -> p h d", h=HG)
                        nc.gpsimd.tensor_tensor(sv, sv, etot[:, c, g8].unsqueeze(2).to_broadcast([P, HG, HD]),
                                                ALU.mult).then_inc(state_dec, 1)
                    if c:
                        pool.wait_ge(yt_ready, 3 * j + c)
                    else:
                        pool.wait_ge(aux_free, J_SSD + SSD_JOBS * j + A_YD[0] + 1)
                    pool.wait_ge(acc_free, 4 * qz + c + 1)
                    nc.gpsimd.tensor_tensor(yy[:, c, ds(j * W, W)], yt[:, :], zs[:, c, :],
                                            ALU.mult).then_inc(y_ready, 1)
                    lo(qz + 2, c)

            with pool.Fori(0, NG - 1) as j:
                group(j)
            group(NG - 1)
            for p in range(4):
                lo(Q_U, p)
            root(1)
            root(2)
            for t in range(NT):
                pool.wait_ge(ln_ready, t + 1)
                if t == 0:
                    pool.wait_ge(rows_in, 48)
                st.link(nc.gpsimd.tensor_tensor(vv[:, t, :], vv[:, t, :], lnw[:, :], ALU.mult))
                nc.gpsimd.tensor_tensor(vv[:, t, :], vv[:, t, :], lnb[:, :], ALU.add).then_inc(v_ready, 1)
                lo(Q_U + 1, t)
            with pool.Fori(0, Q_UP + 1 - Q_GB) as i:
                for p in range(4):
                    lo(Q_GB + i, p)
            root(3)
            with pool.Fori(0, FC - 1) as i:
                for p in range(4):
                    lo(Q_UP + 1 + i, p)
            for n in range(KF):
                lo(Q_DOWN + n // 4, n % 4)
            for t in range(NT):
                root(0, t, t + 1)

        @block.scalar
        def _(act):
            st = Steps(act, act_steps)

            def hi(q, p):
                act.wait_ge(loaded[p % 2], 32 * (2 * q + p // 2) + 32)
                if isinstance(q, int) and q > Q_DOWN:
                    c, u = divmod(4 * (q - 1 - Q_DOWN) + p, KF // 2)
                    if u == KF // 2 - 1:
                        act.wait_ge(acc_ready, 4 * (Q_DOWN + c + 1))
                    else:
                        act.wait_ge(unit_used, 3 * Q_DOWN + c * (KF // 2 - 1) + u + 1)
                elif not (isinstance(q, int) and q == 0):
                    if p == 3:
                        act.wait_ge(acc_ready, 4 * q)
                    else:
                        act.wait_ge(unit_used, 3 * q + p - 2)
                nc.scalar.activation(whi[:, p, :, :], raw[:, p % 2, :, :], ACT.Copy).then_inc(hi_ready, 1)

            def aux_split(job, dst, scale=1.0):
                act.wait_ge(aux_ready, job + 1)
                nc.scalar.activation(dst, aux[:, job % 4, :], ACT.Copy, scale=scale).then_inc(aux_hi, 1)

            def conv_in(a, f, tile):
                act.wait_ge(acc_ready, 4 * a + f + 1)
                if not (isinstance(tile, int) and tile < 2):
                    act.wait_ge(conv_ready, tile - 1)
                nc.scalar.activation(convx[:, f % 2, 3:3 + W], acc[:, f, :], ACT.Copy).then_inc(acc_free, 1)

            def conv_silu(f, tile, dst):
                act.wait_ge(conv_ready, tile + 1)
                nc.scalar.activation(dst, conv1[:, f % 2, :], ACT.Silu).then_inc(silu_ready, 1)

            def conv_chunk(a, tile, dst, between):
                hi(a + 1, 0)
                hi(a + 1, 1)
                hi(a + 1, 2)
                between(0)
                conv_in(a, 0, tile)
                conv_in(a, 1, tile + 1)
                conv_silu(0, tile, dst(0))
                between(1)
                conv_in(a, 2, tile + 2)
                conv_silu(1, tile + 1, dst(1))
                conv_in(a, 3, tile + 3)
                hi(a + 1, 3)
                between(2)
                conv_silu(2, tile + 2, dst(2))
                conv_silu(3, tile + 3, dst(3))

            act.dma_start(prow[0:96, 0, :], conv_a_w.rearrange("l k (t p) -> (l k t) p", p=P)).then_inc(prow_in, 16)
            act.dma_start(prow[96:120, 0, :], conv_a_b.rearrange("l (t p) -> (l t) p", p=P)).then_inc(prow_in, 16)
            act.dma_start(prow[120:128, 0, :], norm1_w.rearrange("l (t p) -> (l t) p", p=P)).then_inc(prow_in, 16)
            act.dma_start(prow[0:8, 1, :], norm2_w.rearrange("l (t p) -> (l t) p", p=P)).then_inc(prow_in, 16)
            act.dma_start(prow[8:24, 1, :], ssd_norm_w.rearrange("l (t p) -> (l t) p", p=P)).then_inc(prow_in, 16)
            act.dma_start(prow[24:32, 1, :], b_spatial.rearrange("l g p -> (l g) p")).then_inc(prow_in, 16)
            act.dma_start(prow[32:76, 1, :], conv_f_b.rearrange("l (t p) -> (l t) p", p=P)).then_inc(prow_in, 16)
            cfw = conv_f_w.rearrange("l k (t p) -> (l k t) p", p=P)
            act.dma_start(prow[76:120, 1, :], cfw[88:132, :]).then_inc(prow_in, 16)
            act.dma_start(prow[0:88, 2, :], cfw[0:88, :]).then_inc(prow_in, 16)
            act.preload_act_table(ACT.Copy)
            for t in range(NT):
                act.wait_ge(x_in[t], 16)
                nc.scalar.activation(xn[:, t, :], xr[:, t, :], ACT.Square,
                                     accum_out=ssq[:, t:t + 1]).then_inc(squares, 1)
            act.dma_start(wdt[:, :, :], win_v[:, :, DT0:DT0 + NH]).then_inc(wdt_in, 16)
            act.dma_start(small[:, 0, :], dt_bias.rearrange("l n -> (l n)").partition_broadcast(P)).then_inc(small_in, 16)
            act.dma_start(small[:, 1, :], a_log.rearrange("l n -> (l n)").partition_broadcast(P)).then_inc(small_in, 16)
            act.dma_start(small[:, 2, :], d_skip.rearrange("l n -> (l n)").partition_broadcast(P)).then_inc(small_in, 16)
            hi(Q_B, 0)
            act.wait_ge(rst_ready, 1)
            nc.scalar.activation(xn[:, NT - 1, :], xr[:, NT - 1, :], ACT.Copy, scale=rst[:, NT - 1:NT]).then_inc(normed, 1)
            act.wait_ge(aux_free, J_PAR + 1)
            for k in range(KD):
                aux_split(J_N1 + k, t1h[:, k, :], par[:, C_N1 + k:C_N1 + k + 1])
                if k in (3, 5, 7):
                    hi(Q_B, (k - 1) // 2)
            act.wait_ge(wdt_in, 16)
            nc.scalar.activation(wdth[:, :, :], wdt[:, :, :], ACT.Copy).then_inc(wdt_hi, 1)
            nothing = lambda where: None

            def decay_tables(where):
                if where == 0:
                    act.wait_ge(consts, 11)
                    act.wait_ge(aux_free, J_CUM + 1)
                    nc.scalar.activation(eac[:, :, :], acum[:, :, :], ACT.Exp).then_inc(cum_exp, 1)
                    act.wait_ge(cum_ready, 1)
                    nc.scalar.activation(etot[:, :, :], etot[:, :, :], ACT.Exp).then_inc(cum_exp, 1)
                    nc.scalar.activation(dsd[:, :, :], dsd[:, :, :], ACT.Exp).then_inc(cum_exp, 1)
                    for g in range(NG):
                        act.wait_ge(aux_ready, J_PART + g + 1)
                        nc.scalar.activation(acb[0:3 * HG, g, :], aux[0:3 * HG, (J_PART + g) % 4, :], ACT.Copy).then_inc(aux_free, 1)

            def current(g, which):
                src, dst = ((bf, bcur), (cf, ccur))[which]
                nc.scalar.activation(dst[:, :].unsqueeze(1), src[:, ds(g, 1), :], ACT.Copy).then_inc(cur_ready, 1)

            conv_chunk(Q_B, 0, lambda f: bf[:, f, :], nothing)
            act.wait_ge(dt_pre, 1)
            nc.scalar.activation(dex[:, :, :], du[:, :, :], ACT.Exp).then_inc(dt_exp, 1)
            act.wait_ge(small_in, 48)
            st.link(nc.scalar.activation(small[:, 1, :], small[:, 1, :], ACT.Exp))
            act.wait_ge(dt_one, 1)
            nc.scalar.activation(dln[:, :, :], du[:, :, :], ACT.Ln).then_inc(dt_ln, 1)
            conv_chunk(Q_C, 4, lambda f: cf[:, f, :], nothing)
            conv_chunk(Q_X0, T_X, lambda f: xf[:, f, :], decay_tables)
            act.wait_ge(silu_ready, 8)
            current(0, 0)
            current(0, 1)

            def decay(j, *hs):
                for h in hs:
                    act.wait_ge(aux_free, J_SSD + SSD_JOBS * j + A_HEAD[h] + 1)
                    last = st.mark(nc.scalar.activation(dif[:, h % 2, :, :], dif[:, h % 2, :, :], ACT.Relu, scale=-1.0))
                st.wait(last)
                for h in hs:
                    nc.scalar.activation(dif[:, h % 2, :, :], dif[:, h % 2, :, :], ACT.Exp,
                                         scale=-1.0).then_inc(exp_ready, 1)

            def beside_z(j):
                a = Q_Z + 2 * j
                hi(a + 1, 0)
                decay(j, 0, 1)
                hi(a + 1, 1)
                decay(j, 2, 3)
                decay(j, 4, 5)
                hi(a + 1, 2)
                decay(j, 6, 7)
                act.preload_act_table(ACT.Silu)
                for t in range(NT):
                    act.wait_ge(acc_ready, 4 * a + t + 1)
                    if t == 0:
                        act.wait_ge(y_ready, 4 * j + 1)
                    nc.scalar.activation(zs[:, t, :], acc[:, t, :], ACT.Silu).then_inc(acc_free, 1)
                hi(a + 1, 3)

            def y_square(j, c):
                act.wait_ge(y_ready, NT * j + c + 2)
                act.wait_ge(squares, NT + NT * j + c)
                nc.scalar.activation(junk[:, :], yy[:, c, ds(j * W, W)], ACT.Square,
                                     accum_out=ssy[:, c, ds(j, 1)]).then_inc(squares, 1)

            with st.loop(NG - 1, HG) as j:
                beside_z(j)

                def between(where):
                    if where == 1:
                        current(j + 1, 0)
                    elif where == 2:
                        act.wait_ge(aux_ready, J_SSD + SSD_JOBS * j + SSD_JOBS)
                        current(j + 1, 1)
                    y_square(j, where)

                conv_chunk(Q_Z + 1 + 2 * j, T_X + 4 + 4 * j, lambda f: xf[:, f, :], between)
                y_square(j, 3)
            beside_z(NG - 1)
            for p in range(4):
                hi(Q_V + 1, p)
            for c in range(NT):
                y_square(NG - 1, c)

            def activate(a, t, i, dst, func, done):
                act.wait_ge(acc_free, 4 * a + t + 1)
                cut = dst[:, t, ds(i * W, W)]
                nc.scalar.activation(cut, cut, func).then_inc(done, 1)

            def activated(q, i, dst, func, done):
                for p in range(3):
                    hi(q + 1, p)
                for t in range(NT):
                    activate(q, t, i, dst, func, done)
                    if t == 2:
                        hi(q + 1, 3)

            GELU = ACT.Gelu_apprx_tanh
            for t in range(NT):
                activate(Q_V, t, 0, vv, GELU, uv_act)
            activated(Q_V + 1, 1, vv, GELU, uv_act)
            with act.Fori(0, 2) as i:
                activated(Q_U + i, i, uu, GELU, uv_act)
            activated(Q_GB, 0, mg, ACT.Sigmoid, g_act)
            split_yb = lambda *ks: [aux_split(J_YB + k, t2h[:, k, :]) for k in ks]
            hi(Q_GB + 2, 0)
            hi(Q_GB + 2, 1)
            split_yb(0, 1)
            hi(Q_GB + 2, 2)
            split_yb(2, 3, 4, 5)
            hi(Q_GB + 2, 3)
            split_yb(6, 7)
            for t in range(NT):
                activate(Q_GB + 1, t, 1, mg, ACT.Sigmoid, g_act)
            with act.Fori(0, 2) as i:
                for p in range(4):
                    hi(Q_PB + 1 + i, p)
            sn = lambda k: par[:, C_SN + k:C_SN + k + 1]
            for i in range(2):
                hi(Q_GA + 1 + i, 0)
                hi(Q_GA + 1 + i, 1)
                aux_split(J_YA + 4 * i, t2h[:, 4 * i, :], sn(4 * i))
                aux_split(J_YA + 4 * i + 1, t2h[:, 4 * i + 1, :], sn(4 * i + 1))
                hi(Q_GA + 1 + i, 2)
                aux_split(J_YA + 4 * i + 2, t2h[:, 4 * i + 2, :], sn(4 * i + 2))
                for t in range(NT):
                    activate(Q_GA + i, t, i, ga, ACT.Sigmoid, g_act)
                hi(Q_GA + 1 + i, 3)
                aux_split(J_YA + 4 * i + 3, t2h[:, 4 * i + 3, :], sn(4 * i + 3))
            for i in range(2):
                for p in range(4):
                    hi(Q_PA + 1 + i, p)
                    aux_split(J_YA + KD + 4 * i + p, t1h[:, 4 * i + p, :], sn(KD + 4 * i + p))
            for p in range(4):
                hi(Q_PA + 3, p)
            split_m = lambda *ks: [aux_split(J_M + k, t2h[:, k, :]) for k in ks]
            hi(Q_WO, 0)
            hi(Q_WO, 1)
            split_m(0, 1)
            hi(Q_WO, 2)
            split_m(2, 3)
            hi(Q_WO, 3)
            hi(Q_WO + 1, 0)
            split_m(4, 5)
            hi(Q_WO + 1, 1)
            split_m(6, 7)
            hi(Q_WO + 1, 2)
            hi(Q_WO + 1, 3)
            split_h = lambda *ks: [aux_split(J_N2 + k, t1h[:, k, :], par[:, C_N2 + k:C_N2 + k + 1]) for k in ks]
            hi(Q_UP, 0)
            hi(Q_UP, 1)
            split_h(0, 1)
            hi(Q_UP, 2)
            split_h(2, 3)
            hi(Q_UP, 3)
            for t in range(NT):
                act.wait_ge(acc_free, 4 * (Q_WO + 1) + t + 1)
                nc.scalar.activation(hn[:, t, :], hh[:, t, :], ACT.Square,
                                     accum_out=ssq[:, NT + t:NT + t + 1]).then_inc(squares, 1)

            def ffn(i, first=False):
                q, tile = Q_UP + i, T_UP + 4 * i
                hi(q + 1, 0)
                if first:
                    split_h(4, 5)
                hi(q + 1, 1)
                if first:
                    split_h(6, 7)
                hi(q + 1, 2)
                for f in range(2):
                    act.wait_ge(conv_ready, tile + f + 1)
                    nc.scalar.activation(conv2[:, f, :], conv2[:, f, :], ACT.Silu).then_inc(fsilu, 1)
                hi(q + 1, 3)
                for f in range(2):
                    act.wait_ge(fprod, 2 * i + f + 1)
                    nc.scalar.activation(fth[:, ds(2 * i + f, 1), :], conv2[:, 2 + f, :].unsqueeze(1),
                                         ACT.Copy).then_inc(fhi, 1)

            ffn(0, first=True)
            act.preload_act_table(ACT.Silu)
            with act.Fori(0, FC - 1) as i:
                ffn(i + 1)
            for n in range(4, KF):
                hi(Q_DOWN + n // 4, n % 4)
            for t in range(NT):
                act.wait_ge(acc_free, 4 * (Q_DOWN + 1) + t + 1)
                act.wait_ge(squares, 2 * NT + NT * NG + t)
                nc.scalar.activation(conv2[:, 0:2, :].rearrange("p a n -> p (a n)"), hh[:, t, :], ACT.Square,
                                     accum_out=ssq[:, 2 * NT + t:2 * NT + t + 1]).then_inc(squares, 1)

        @block.vector
        def _(dve):
            st = Steps(dve, dve_steps)
            V = nc.vector
            tok = lambda ap: ap.unsqueeze(1).to_broadcast([P, NT, NH])
            v4 = lambda ap: ap.rearrange("p (t n) -> p t n", t=4)
            vh = lambda ap: ap.rearrange("p (h d) -> p h d", h=HG)
            heads = lambda ap: ap.unsqueeze(2).to_broadcast([P, HG, HD])
            flat = lambda ap: ap.rearrange("p t n -> p (t n)")
            causal = tri[:, :].unsqueeze(1).to_broadcast([P, 4, P])

            n_root = [0]

            def rsqrt(i, src, n, eps, wait=True):
                V.tensor_scalar(msq[:, i * NT:(i + 1) * NT], src, 1.0 / n, eps, ALU.mult,
                                ALU.add).then_inc(msq_ready, 1)
                n_root[0] += 1
                if wait:
                    dve.wait_ge(rst_ready, n_root[0])

            n_hi = [0]

            def transposed(job, dst_l, dst_h, scale=1.0):
                n_hi[0] += 1
                dve.wait_ge(aux_hi, n_hi[0])
                V.scalar_tensor_tensor(dst_l, aux[:, job % 4, :], scale, dst_h.bitcast(F32), ALU.mult,
                                       ALU.subtract).then_inc(aux_free, 1)

            dve.wait_ge(squares, NT)
            rsqrt(0, ssq[:, 0:NT], D, NORM_EPS)
            for t in range(NT - 1):
                V.tensor_scalar(xn[:, t, :], xr[:, t, :], rst[:, t:t + 1], None, ALU.mult).then_inc(normed, 1)
            dve.wait_ge(aux_ready, J_PAR + 1)
            st.link(V.tensor_copy(par[:, 0:248], aux[:, 0, 0:248]))
            V.tensor_copy(par[:, 256:344], aux[:, 0, 256:344]).then_inc(aux_free, 1)
            dve.wait_ge(aux_free, J_PAR + 1)
            for k in range(KD):
                transposed(J_N1 + k, t1l[:, k, :], t1h[:, k, :], par[:, C_N1 + k:C_N1 + k + 1])
            dve.wait_ge(wdt_hi, 1)
            V.tensor_tensor(wdtl[:, :, :], wdt[:, :, :], wdth[:, :, :].bitcast(F32), ALU.subtract).then_inc(wdt_lo, 1)

            def conv(f, taps, wcols, bcol, dst):
                off = 4 - taps
                src = convx[:, f % 2, :]
                st.link(V.tensor_scalar(dst, src[:, off:off + W], par[:, wcols[0]], par[:, bcol], ALU.mult, ALU.add))
                for i in range(1, taps):
                    ins = V.scalar_tensor_tensor(dst, src[:, off + i:off + i + W], par[:, wcols[i]], dst,
                                                 ALU.mult, ALU.add)
                    if i < taps - 1:
                        st.link(ins)
                    else:
                        ins.then_inc(conv_ready, 1)

            def conv_a(a, f, tile, col):
                dve.wait_ge(acc_free, 4 * a + f + 1)
                if not (isinstance(tile, int) and tile < 2):
                    dve.wait_ge(silu_ready, tile - 1)
                conv(f, 4, [ds(C_CAW + 24 * i + col, 1) for i in range(4)], ds(C_CAB + col, 1), conv1[:, f % 2, :])

            for f in range(4):
                conv_a(Q_B, f, f, 16 + f)

            bank3 = lambda job: aux[:, job % 4, 0:P].rearrange("p (t h) -> p t h", t=NT)
            dve.wait_ge(aux_ready, J_DT + 1)
            dve.wait_ge(small_in, 48)
            V.tensor_tensor(dpre[:, :, :], bank3(J_DT), tok(small[:, 0, :]), ALU.add).then_inc(aux_free, 1)
            dve.wait_ge(aux_free, J_DT + 1)
            V.scalar_tensor_tensor(du[:, :, :], dpre[:, :, :], -1.0, dpre[:, :, :], ALU.mult,
                                   ALU.min).then_inc(dt_pre, 1)
            dve.wait_ge(dt_exp, 1)
            V.tensor_scalar(du[:, :, :], dex[:, :, :], 1.0, None, ALU.add).then_inc(dt_one, 1)
            dve.wait_ge(dt_one, 1)
            st.link(V.scalar_tensor_tensor(dex[:, :, :], du[:, :, :], 1.0, dex[:, :, :], ALU.subtract, ALU.subtract))
            st.link(V.reciprocal(adt[:, :, :], du[:, :, :]))
            st.link(V.tensor_tensor(adt[:, :, :], adt[:, :, :], dex[:, :, :], ALU.mult))
            dve.wait_ge(dt_ln, 1)
            st.link(V.tensor_tensor(dln[:, :, :], dln[:, :, :], adt[:, :, :], ALU.subtract))
            st.link(V.scalar_tensor_tensor(dt[:, :, :], dpre[:, :, :], 0.0, dln[:, :, :], ALU.max, ALU.add))
            dve.wait_ge(act_steps, 1)
            V.scalar_tensor_tensor(adt[:, :, :], dt[:, :, :], -1.0, tok(small[:, 1, :]), ALU.mult,
                                   ALU.mult).then_inc(adt_ready, 1)

            dve.wait_ge(aux_ready, J_CUM + 1)
            V.tensor_copy(acum[:, :, :], bank3(J_CUM)).then_inc(aux_free, 1)
            dve.wait_ge(aux_free, J_CUM + 1)
            src = acum[:, :, :].rearrange("p t (g h) -> p (t g) h", g=NG)
            for i in range(2):
                st.link(V.tensor_copy(parb[:, :, :], src))
                st.link(V.tensor_copy(part[:, :, i, :], parb[:, :, :]))
                ins = V.tensor_tensor(part[:, :, 2, :], src, part[:, :, i, :], ALU.subtract)
                if i == 0:
                    st.link(ins)
                    src = part[:, :, 2, :]
            ins.then_inc(part_ready, 1)
            dve.wait_ge(aux_ready, J_TOT + 1)
            V.tensor_copy(etot[:, :, :], bank3(J_TOT)).then_inc(aux_free, 1)
            dve.wait_ge(aux_free, J_TOT + 1)
            V.tensor_tensor(dsd[:, :, :], etot[:, :, :], acum[:, :, :], ALU.subtract).then_inc(cum_ready, 1)

            for f in range(4):
                conv_a(Q_C, f, 4 + f, 20 + f)
            for f in range(4):
                conv_a(Q_X0, f, T_X + f, f)

            dve.wait_ge(cum_exp, 3)

            def beside_z(j):
                base = J_SSD + SSD_JOBS * j
                bank = lambda k: aux[:, (J_SSD + k) % 4, :]
                g8 = ds(HG * j, HG)

                def exponent(h):
                    dve.wait_ge(aux_ready, base + A_HEAD[h] + 1)
                    if h >= 2:
                        dve.wait_ge(m_ready, HG * j + h - 1)
                    V.tensor_tensor(dif[:, h % 2, :, :], v4(bank(A_HEAD[h])),
                                    acum[:, :, ds(HG * j + h, 1)].to_broadcast([P, NT, P]),
                                    ALU.subtract).then_inc(aux_free, 1)

                def masked(h):
                    dve.wait_ge(exp_ready, HG * j + h + 1)
                    V.tensor_tensor(mm[:, h, :, :], dif[:, h % 2, :, :], cbm[:, :, :], ALU.mult).then_inc(m_ready, 1)

                def tokens(c):
                    dve.wait_ge(aux_ready, base + A_XS[c] + 1)
                    V.tensor_tensor(vh(xdt[:, c, :]), vh(bank(A_XS[c])), heads(dt[:, c, g8]),
                                    ALU.mult).then_inc(xdt_ready, 1)
                    V.tensor_tensor(vh(dx[:, c, :]), vh(bank(A_XS[c])), heads(small[:, 2, g8]),
                                    ALU.mult).then_inc(aux_free, 1)

                dve.wait_ge(aux_ready, base + A_BT + 1)
                V.tensor_copy(bt[:, :, :], v4(bank(A_BT))).then_inc(aux_free, 1)
                dve.wait_ge(aux_ready, base + A_CB + 1)
                V.tensor_tensor(cbm[:, :, :], v4(bank(A_CB)), causal, ALU.mult).then_inc(aux_free, 1)
                exponent(0)
                exponent(1)
                dve.wait_ge(aux_free, base + A_CB + 1)
                for h in range(2, HG):
                    masked(h - 2)
                    exponent(h)
                masked(HG - 2)
                masked(HG - 1)
                for c in range(NT):
                    tokens(c)

            def ssd_chunk(j, c):
                base = J_SSD + SSD_JOBS * j
                bank = lambda k: aux[:, (J_SSD + k) % 4, :]
                g8 = ds(HG * j, HG)
                dve.wait_ge(aux_ready, base + A_YD[c] + 1)
                dve.wait_ge(y_ready, NT * j + c + 1)
                V.tensor_tensor(yt[:, :], bank(A_YD[c]), dx[:, c, :], ALU.add).then_inc(aux_free, 1)
                if c:
                    dve.wait_ge(aux_ready, base + A_OFF[c] + 1)
                    dve.wait_ge(aux_free, base + A_YD[c] + 1)
                    V.tensor_tensor(vh(dx[:, c, :]), vh(bank(A_OFF[c])), heads(eac[:, c, g8]),
                                    ALU.mult).then_inc(aux_free, 1)
                    dve.wait_ge(aux_free, base + A_OFF[c] + 1)
                    V.tensor_tensor(yt[:, :], yt[:, :], dx[:, c, :], ALU.add).then_inc(yt_ready, 1)
                if c < NT - 1:
                    dve.wait_ge(aux_ready, base + A_ST[c] + 1)
                    if c:
                        dve.wait_ge(state_dec, 2 * j + c)
                        V.tensor_tensor(state[:, :], bank(A_ST[c]), state[:, :], ALU.add).then_inc(aux_free, 1)
                    else:
                        V.tensor_copy(state[:, :], bank(A_ST[c])).then_inc(aux_free, 1)

            with st.loop(NG - 1, 12) as j:
                beside_z(j)
                for c in range(3):
                    ssd_chunk(j, c)
                for f in range(4):
                    conv_a(Q_Z + 1 + 2 * j, f, T_X + 4 + 4 * j + f, 4 * j + 4 + f)
                ssd_chunk(j, 3)
            beside_z(NG - 1)
            for c in range(NT):
                ssd_chunk(NG - 1, c)

            def biased(a, i, dst, bias, col):
                for t in range(NT):
                    dve.wait_ge(acc_ready, 4 * a + t + 1)
                    V.tensor_tensor(dst[:, t, ds(i * W, W)], acc[:, t, :], bias[:, ds(col + i * W, W)],
                                    ALU.add).then_inc(acc_free, 1)

            dve.wait_ge(rows_in, 48)
            dve.wait_ge(y_ready, NT * NG + 1)
            with dve.Fori(0, 2) as i:
                biased(Q_V + i, i, vv, uvb, D)
            dve.wait_ge(squares, NT + NT * NG)
            st.link(V.reduce_sum(ssq[:, NT:2 * NT], ssy[:, :, :], mybir.AxisListType.X))
            rsqrt(1, ssq[:, NT:2 * NT], DI, NORM_EPS, wait=False)
            for i in range(2):
                dve.wait_ge(aux_ready, J_WT + i + 1)
                V.tensor_tensor(wst[:, 4 * i:4 * i + 4, :], v4(aux[:, (J_WT + i) % 4, :]), causal,
                                ALU.mult).then_inc(aux_free, 1)
            for t in range(NT):
                dve.wait_ge(uv_act, NT + t + 1)
                for i in range(2):
                    last = st.mark(V.bn_stats(bns[:, t, i, :], vv[:, t, i * W:(i + 1) * W]))
                st.wait(last)
                st.link(V.bn_aggr(bna[:, t, :], bns[:, t, :, :].rearrange("p a b -> p (a b)")))
            rsqrt(2, bna[:, :, 1], 1, LN_EPS)
            for t in range(NT):
                r = rst[:, 2 * NT + t:2 * NT + t + 1]
                V.tensor_scalar(vv[:, t, :], vv[:, t, :], bna[:, t, 0:1], r, ALU.subtract,
                                ALU.mult).then_inc(ln_ready, 1)
            with dve.Fori(0, 2) as i:
                biased(Q_U + i, i, uu, uvb, 0)
            dve.wait_ge(uv_act, 4 * NT)
            for g in range(SG):
                dve.wait_ge(aux_ready, J_MIX + g + 1)
                ug = uu[:, :, g * P:(g + 1) * P]
                V.scalar_tensor_tensor(ug, v4(aux[:, (J_MIX + g) % 4, :]), par[:, C_BS + g:C_BS + g + 1], ug,
                                       ALU.add, ALU.mult).then_inc(aux_free, 1)
            dve.wait_ge(gate_rows_in, 16)
            biased(Q_GB, 0, mg, bgt, D)
            for k in range(6):
                transposed(J_YB + k, t2l[:, k, :], t2h[:, k, :])
            biased(Q_GB + 1, 1, mg, bgt, D)
            for k in (6, 7):
                transposed(J_YB + k, t2l[:, k, :], t2h[:, k, :])
            dve.wait_ge(g_act, 2 * NT)
            with dve.Fori(0, 2) as i:
                for t in range(NT):
                    dve.wait_ge(acc_ready, 4 * Q_PB + 4 * i + t + 1)
                    m = mg[:, t, ds(i * W, W)]
                    V.tensor_tensor(m, acc[:, t, :], m, ALU.mult).then_inc(acc_free, 1)
            sn = lambda k: par[:, C_SN + k:C_SN + k + 1]
            for i in range(2):
                for k in range(4 * i, 4 * i + 3):
                    transposed(J_YA + k, t2l[:, k, :], t2h[:, k, :], sn(k))
                biased(Q_GA + i, i, ga, bgt, 0)
                k = 4 * i + 3
                transposed(J_YA + k, t2l[:, k, :], t2h[:, k, :], sn(k))

            n_merge = [0]

            def merge(half, c):
                cut = slice(c * W, (c + 1) * W)
                a = Q_PA + 2 * half + c
                for t in range(NT):
                    dve.wait_ge(acc_ready, 4 * a + t + 1)
                    pa = convx[:, t % 2, 3:3 + W]
                    if n_merge[0] + t >= 2:
                        dve.wait_ge(m_done, n_merge[0] + t - 1)
                    V.scalar_tensor_tensor(pa, acc[:, t, :], rst[:, NT + t:NT + t + 1], ga[:, t, cut],
                                           ALU.mult, ALU.mult).then_inc(acc_free, 1)
                    dve.wait_ge(acc_free, 4 * a + t + 1)
                    V.tensor_tensor(mg[:, t, cut], mg[:, t, cut], pa, ALU.add).then_inc(m_done, 1)
                n_merge[0] += NT

            def second_half(*ks):
                for k in ks:
                    transposed(J_YA + KD + k, t1l[:, k, :], t1h[:, k, :], sn(KD + k))

            second_half(0, 1, 2)
            dve.wait_ge(g_act, 4 * NT)
            merge(0, 0)
            second_half(3, 4, 5, 6)
            merge(0, 1)
            second_half(7)
            merge(1, 0)
            for k in range(4):
                transposed(J_M + k, t2l[:, k, :], t2h[:, k, :])
            merge(1, 1)
            for k in range(4, KD):
                transposed(J_M + k, t2l[:, k, :], t2h[:, k, :])

            def residual(a, c, *tiles):
                for t in tiles or range(NT):
                    dve.wait_ge(acc_ready, 4 * a + t + 1)
                    cut = slice(c * W, (c + 1) * W)
                    V.tensor_tensor(hh[:, t, cut], acc[:, t, :], hh[:, t, cut], ALU.add).then_inc(acc_free, 1)

            dve.wait_ge(xr_again, 16)
            residual(Q_WO, 0)
            on_channels = lambda k: transposed(J_N2 + k, t1l[:, k, :], t1h[:, k, :], par[:, C_N2 + k:C_N2 + k + 1])
            for k in range(4):
                on_channels(k)
            residual(Q_WO + 1, 1)
            for k in range(4, KD):
                on_channels(k)
            dve.wait_ge(squares, 2 * NT + NT * NG)
            st.link(V.memset(ones2[:, :], 1.0))
            rsqrt(3, ssq[:, NT:2 * NT], D, NORM_EPS)
            for t in range(NT):
                ins = V.tensor_scalar(diag[:, t * P:(t + 1) * P], ident[:, :], rst[:, 3 * NT + t:3 * NT + t + 1], None,
                                      ALU.mult)
            ins.then_inc(diag_ready, 1)
            dve.wait_ge(aux_ready, J_RB + 1)
            V.tensor_copy(rbc[:, :], aux[:, J_RB % 4, :]).then_inc(aux_free, 1)
            dve.wait_ge(aux_free, J_RB + 1)

            def ffn(i):
                a, tile = Q_UP + i, T_UP + 4 * i

                def scaled(f):
                    if f >= 2:
                        dve.wait_ge(conv_ready, tile + f - 1)
                    dve.wait_ge(acc_ready, 4 * a + f + 1)
                    V.tensor_tensor(convx[:, f % 2, 3:3 + W], acc[:, f, :], rbc[:, :], ALU.mult).then_inc(acc_free, 1)

                def conv_f(f):
                    col = 2 * i + f if f < 2 else KF + 2 * i + f - 2
                    dve.wait_ge(acc_free, 4 * a + f + 1)
                    if not isinstance(i, int):
                        dve.wait_ge(flo if f >= 2 else fprod, 2 * i)
                    conv(f, 3, [ds(C_CF0 + col, 1), ds(C_CF0 + 2 * KF + col, 1), ds(C_CF2 + col, 1)],
                         ds(C_CFB + col, 1), conv2[:, f, :])

                def product(f):
                    dve.wait_ge(conv_ready, tile + 2 + f + 1)
                    dve.wait_ge(fsilu, 2 * i + f + 1)
                    V.tensor_tensor(conv2[:, 2 + f, :], conv2[:, f, :], conv2[:, 2 + f, :],
                                    ALU.mult).then_inc(fprod, 1)

                scaled(0)
                scaled(1)
                conv_f(0)
                scaled(2)
                conv_f(1)
                scaled(3)
                conv_f(2)
                product(0)
                conv_f(3)
                product(1)
                for f in range(2):
                    dve.wait_ge(fhi, 2 * i + f + 1)
                    V.tensor_tensor(ftl[:, ds(2 * i + f, 1), :], conv2[:, 2 + f, :].unsqueeze(1),
                                    fth[:, ds(2 * i + f, 1), :].bitcast(F32), ALU.subtract).then_inc(flo, 1)

            ffn(0)
            with st.loop(FC - 1, 8) as i:
                ffn(i + 1)

            residual(Q_DOWN, 0)
            dve.wait_ge(fnw_in, 16)
            for t in range(NT):
                residual(Q_DOWN + 1, 1, t)
                r = rst[:, t:t + 1]
                dve.wait_ge(squares, 2 * NT + NT * NG + t + 1)
                V.tensor_scalar(msq[:, t:t + 1], ssq[:, 2 * NT + t:2 * NT + t + 1], 1.0 / D, NORM_EPS, ALU.mult,
                                ALU.add).then_inc(msq_ready, 1)
                dve.wait_ge(rst_ready, n_root[0] + t + 1)
                V.scalar_tensor_tensor(hh[:, t, :], hh[:, t, :], r, fnw[:, :], ALU.mult, ALU.mult).then_inc(final, 1)

        @block.tensor
        def _(pe):
            MM = nc.tensor.matmul

            def unit(n, slot, first, last, a, acts, ks, kind, at=None):
                pe.wait_ge(lo_ready, n + 1)
                ah, al = acts
                for t in range(4):
                    if first and not (isinstance(a, int) and a == 0):
                        pe.wait_ge(acc_free, 4 * a + t - 3)
                    for r, k in enumerate(ks):
                        for i, (w, x) in enumerate(((whi, ah), (whi, al), (wlo, ah))):
                            flags = dict(start=first and r == 0 and i == 0, stop=last and r == 1 and i == 2)
                            if kind == "tokens":
                                ins = MM(acc[:, t, :], x[:, k, t * P:(t + 1) * P], w[:, slot, r, :], **flags)
                            elif kind == "channels":
                                ins = MM(acc[:, t, :], w[:, slot, r, t * P:(t + 1) * P], x[:, k, :], **flags)
                            else:
                                ins = MM(acc[:, t, :], w[:, slot, t // 2, r * 256 + t % 2 * P:r * 256 + t % 2 * P + P],
                                         x[:, k, :], **flags)
                    if last and t < 3:
                        ins.then_inc(acc_ready, 1)
                ins.then_inc(acc_ready if last else unit_used, 1)

            def gemm(q, a, acts, kind, between=None, parts=None):
                for p in range(4):
                    if parts is not None:
                        pe.wait_ge(aux_free, parts + 2 * p + 2)
                    unit(4 * q + p, p, p == 0, p == 3, a, acts, (2 * p, 2 * p + 1), kind)
                    if between:
                        between(p)

            def job(n, k=None):
                if not (isinstance(n, int) and n < 4):
                    pe.wait_ge(aux_free, n - 3)
                return aux[:, (n if k is None else k) % 4, :]

            def turn(n, src, last_inc=aux_ready):
                bank = job(n)
                for t in range(NT):
                    ins = nc.tensor.transpose(bank[:, t * P:(t + 1) * P], src(t), ident[:, :])
                ins.then_inc(aux_ready, 1)

            t1, t2 = (t1h, t1l), (t2h, t2l)

            pe.wait_ge(consts, 6)
            pe.wait_ge(prow_in, 9 * 16)
            for i, n in enumerate((P, 120, 88)):
                ins = nc.tensor.transpose(aux[:, 0, i * P:i * P + n], prow[0:n, i, :], ident[0:n, 0:n])
            ins.then_inc(aux_ready, 1)
            pe.wait_ge(normed, NT)
            for k in range(KD):
                turn(J_N1 + k, lambda t: xn[:, t, k * P:(k + 1) * P])

            def raw_dt(p):
                if p == 3:
                    pe.wait_ge(wdt_lo, 1)
                    bank = job(J_DT)
                    for t in range(NT):
                        for k in range(KD):
                            for i, (x, w) in enumerate(((t1h, wdth), (t1l, wdth), (t1h, wdtl))):
                                ins = MM(bank[:, t * NH:(t + 1) * NH], x[:, k, t * P:(t + 1) * P], w[:, k, :],
                                         start=k == 0 and i == 0, stop=k == KD - 1 and i == 2)
                    ins.then_inc(aux_ready, 1)

            gemm(Q_B, Q_B, t1, "channels", raw_dt, parts=J_N1)
            flat = lambda ap: ap.rearrange("p t n -> p (t n)")

            def cumulative(p):
                if p == 1:
                    pe.wait_ge(adt_ready, 1)
                    for n, m in ((J_CUM, tri), (J_TOT, ones)):
                        MM(job(n)[:, 0:P], m[:, :], flat(adt[:, :, :]), start=True, stop=True).then_inc(aux_ready, 1)

            def parts_over(p):
                if p == 0:
                    pe.wait_ge(part_ready, 1)
                    for g in range(NG):
                        bank = job(J_PART + g)
                        for t in range(NT):
                            ins = nc.tensor.transpose(bank[0:3 * HG, t * P:(t + 1) * P],
                                                      part[:, t * NG + g, :, :].rearrange("p a h -> p (a h)"), ident[:, :])
                        ins.then_inc(aux_ready, 1)

            gemm(Q_C, Q_C, t1, "channels", cumulative)
            gemm(Q_X0, Q_X0, t1, "channels", parts_over)
            pe.wait_ge(aux_free, J_SSD)
            pe.wait_ge(consts, 11)

            def decays(j):
                base = J_SSD + SSD_JOBS * j
                bank = lambda k: job(base + k, J_SSD + k)

                def head(h):
                    MM(bank(A_HEAD[h]), sel[:, h, :], acb[:, ds(j, 1), :].rearrange("p a n -> p (a n)"),
                       start=True, stop=True).then_inc(aux_ready, 1)

                def tokens(c):
                    b = bank(A_XS[c])
                    for f in range(4):
                        ins = nc.tensor.transpose(b[:, f * P:(f + 1) * P], xf[:, f, c * P:(c + 1) * P], ident[:, :])
                    ins.then_inc(aux_ready, 1)

                def between(p):
                    if p == 0:
                        pe.wait_ge(cur_ready, 2 * j + 2)
                        b = bank(A_BT)
                        for c in range(NT):
                            ins = nc.tensor.transpose(b[:, c * P:(c + 1) * P], bcur[:, c * P:(c + 1) * P], ident[:, :])
                        ins.then_inc(aux_ready, 1)
                        b = bank(A_CB)
                        for c in range(NT):
                            cc = slice(c * P, (c + 1) * P)
                            ins = MM(b[:, cc], bcur[:, cc], ccur[:, cc], start=True, stop=True)
                        ins.then_inc(aux_ready, 1)
                        head(0)
                        head(1)
                    elif p == 1:
                        for h in (2, 3, 4, 5):
                            head(h)
                    elif p == 2:
                        head(6)
                        head(7)
                        pe.wait_ge(silu_ready, T_X + 4 * j + 4)
                        tokens(0)
                        tokens(1)
                    else:
                        tokens(2)
                        tokens(3)

                return between

            def chunks(j):
                base = J_SSD + SSD_JOBS * j
                bank = lambda k: job(base + k, J_SSD + k)

                def between(c):
                    if c == 0:
                        pe.wait_ge(m_ready, HG * j + HG)
                        pe.wait_ge(xdt_ready, NT * j + NT)
                    b = bank(A_YD[c])
                    for h in range(HG):
                        cut = slice(h * HD, (h + 1) * HD)
                        ins = MM(b[:, cut], mm[:, h, c, :], xdt[:, c, cut], start=True, stop=True)
                    ins.then_inc(aux_ready, 1)
                    if c:
                        pe.wait_ge(aux_free, base + A_ST[c - 1] + 1)
                        MM(bank(A_OFF[c]), ccur[:, c * P:(c + 1) * P], state[:, :], start=True,
                           stop=True).then_inc(aux_ready, 1)
                    if c < NT - 1:
                        pe.wait_ge(xds_ready, 3 * j + c + 1)
                        MM(bank(A_ST[c]), bt[:, c, :], xds[:, :], start=True, stop=True).then_inc(aux_ready, 1)

                return between

            with pe.Fori(0, NG - 1) as j:
                gemm(Q_Z + 2 * j, Q_Z + 2 * j, t1, "tokens", decays(j))
                gemm(Q_Z + 1 + 2 * j, Q_Z + 1 + 2 * j, t1, "channels", chunks(j))
            gemm(Q_Z + 2 * NG - 2, Q_Z + 2 * NG - 2, t1, "tokens", decays(NG - 1))
            last = chunks(NG - 1)
            gemm(Q_V, Q_V, t1, "tokens", lambda p: last(p) if p < 2 else (last(2), last(3)) if p == 2 else None)
            gemm(Q_V + 1, Q_V + 1, t1, "tokens")

            pe.wait_ge(wsp_in, 16)
            for i in range(2):
                turn(J_WT + i, lambda t: wsp[:, 4 * i + t, :])
            with pe.Fori(0, 2) as i:
                gemm(Q_U + i, Q_U + i, t1, "tokens")
            gemm(Q_GB, Q_GB, t1, "tokens", None)
            pe.wait_ge(v_ready, NT)
            pe.wait_ge(aux_free, J_WT + 2)
            for g in range(SG):
                MM(job(J_MIX + g), wst[:, g, :], vv[:, :, g * P:(g + 1) * P], start=True,
                   stop=True).then_inc(aux_ready, 1)

            def turn_yb(p):
                for k in (2 * p, 2 * p + 1):
                    pe.wait_ge(aux_free, J_MIX + k + 1)
                    turn(J_YB + k, lambda t: uu[:, t, k * P:(k + 1) * P])

            gemm(Q_GB + 1, Q_GB + 1, t1, "tokens", turn_yb)
            with pe.Fori(0, 2) as i:
                gemm(Q_PB + i, Q_PB + i, t2, "tokens", parts=J_YB)
            for i in range(2):
                gemm(Q_GA + i, Q_GA + i, t1, "tokens",
                     lambda p: turn(J_YA + 4 * i + p, lambda t: yy[:, t, (4 * i + p) * P:(4 * i + p + 1) * P]))
            for i in range(2):
                def second_half(p):
                    k = KD + 4 * i + p
                    turn(J_YA + k, lambda t: yy[:, t, k * P:(k + 1) * P])

                gemm(Q_PA + i, Q_PA + i, t2, "tokens", second_half, parts=J_YA)
            gemm(Q_PA + 2, Q_PA + 2, t1, "tokens", parts=J_YA + KD)

            def turn_m(p):
                if p == 1:
                    pe.wait_ge(m_done, 3 * NT)
                for k in {1: (0, 1), 2: (2, 3)}.get(p, ()):
                    turn(J_M + k, lambda t: mg[:, t, k * P:(k + 1) * P])

            gemm(Q_PA + 3, Q_PA + 3, t1, "tokens", turn_m)

            def rest_m(p):
                if p == 0:
                    pe.wait_ge(m_done, 4 * NT)
                for k in {0: (4, 5), 1: (6, 7)}.get(p, ()):
                    turn(J_M + k, lambda t: mg[:, t, k * P:(k + 1) * P])

            def turn_h(*ks):
                for k in ks:
                    turn(J_N2 + k, lambda t: hh[:, t, k * P:(k + 1) * P])

            def first_h(p):
                if p == 1:
                    pe.wait_ge(acc_free, 4 * Q_WO + 4)
                if p in (1, 2):
                    turn_h(2 * p - 2, 2 * p - 1)

            gemm(Q_WO, Q_WO, t2, "tokens", rest_m, parts=J_M)
            gemm(Q_WO + 1, Q_WO + 1, t2, "tokens", first_h)

            def rest_h(p):
                if p == 0:
                    pe.wait_ge(acc_free, 4 * Q_WO + 8)
                if p in (0, 1):
                    turn_h(2 * p + 4, 2 * p + 5)
                if p == 2:
                    pe.wait_ge(diag_ready, 1)
                    MM(job(J_RB), ones2[:, :], diag[:, :], start=True, stop=True).then_inc(aux_ready, 1)

            gemm(Q_UP, Q_UP, t1, "pairs", rest_h, parts=J_N2)
            with pe.Fori(0, FC - 1) as i:
                gemm(Q_UP + 1 + i, Q_UP + 1 + i, t1, "pairs")
            half = KF // 2
            for n in range(KF - 4):
                c, u = divmod(n, half)
                pe.wait_ge(flo, 2 * u + 2)
                unit(4 * Q_DOWN + n, n % 4, u == 0, u == half - 1, Q_DOWN + c, (fth, ftl),
                     (2 * u, 2 * u + 1), "tokens")
            for t in range(4):
                for n in range(KF - 4, KF):
                    if t == 0:
                        pe.wait_ge(lo_ready, 4 * Q_DOWN + n + 1)
                    for r in range(2):
                        k = 2 * (n - half) + r
                        for i, (w, x) in enumerate(((whi, fth), (whi, ftl), (wlo, fth))):
                            ins = MM(acc[:, t, :], x[:, k, t * P:(t + 1) * P], w[:, n % 4, r, :], start=False,
                                     stop=n == KF - 1 and r == 1 and i == 2)
                ins.then_inc(acc_ready, 1)


_INS = ["x", "norm1_w", "w_in", "b_gate", "conv_a_w", "conv_a_b", "dt_bias", "a_log", "d_skip", "ssd_norm_w",
        "uv_b", "v_ln_w", "v_ln_b", "w_spatial", "b_spatial", "w_branch", "w_out", "norm2_w", "w_up",
        "conv_f_w", "conv_f_b", "w_down", "final_norm_w"]


def kernel(**inputs):
    import numpy as np
    import concourse.bacc as bacc
    from concourse import mybir as mb
    from concourse.bass_utils import run_bass_kernel_spmd

    nc = bacc.Bacc("TRN2", target_bir_lowering=False, num_devices=1)
    arrays, args = {}, []
    for name in _INS:
        a = np.ascontiguousarray(inputs[name])
        arrays[f"in_{name}"] = a
        args.append(nc.dram_tensor(f"in_{name}", a.shape, mb.dt.from_np(a.dtype), kind="ExternalInput").ap())
    out = nc.dram_tensor("out_0", (1, S, D), F32, kind="ExternalOutput").ap()
    hybrid_block(nc, *args, out)
    return run_bass_kernel_spmd(nc, [arrays], core_ids=[0]).results[0]["out_0"]
```

```python
from contextlib import ExitStack, contextmanager

import concourse.bass as bass
from concourse import mybir

F32 = mybir.dt.float32
F32R = mybir.dt.float32r
BF16 = mybir.dt.bfloat16
ALU = mybir.AluOpType
ACT = mybir.ActivationFunctionType

P = 128
W = 512
D = 1024
S = 512
NT = S // P
KD = D // P
DI = 2048
NH = 32
HD = 64
NG = 4
HG = NH // NG
SG = 8
FF = 2816
KF = FF // P
FC = KF // 2
NORM_EPS, LN_EPS = 1e-6, 1e-5

Z0, X0, B0, C0, DT0 = 0, DI, 2 * DI, 2 * DI + 512, 2 * DI + 1024
U0 = DT0 + NH
V0, GA0, GB0 = U0 + D, U0 + 2 * D, U0 + 3 * D

Q_B, Q_C, Q_X0, Q_Z, Q_V, Q_U, Q_GB, Q_PB, Q_GA, Q_PA, Q_WO, Q_UP = 0, 1, 2, 3, 10, 12, 14, 16, 18, 20, 24, 26
Q_DOWN = Q_UP + FC
UNITS = 4 * Q_DOWN + KF

J_PAR, J_N1, J_DTC, J_DT, J_CUM, J_TOT, J_ROWS = 0, 1, 9, 10, 11, 12, 13
J_SSD, SSD_JOBS = J_ROWS + 1, 16
J_WT = J_SSD + NG * SSD_JOBS
J_MIX = J_WT + 2
J_RY = J_MIX + SG
J_YA = J_RY + 1
J_N2 = J_YA + 2 * KD
J_RB = J_N2 + KD
A_BT, A_CB = 0, 1
A_XS = (2, 3, 4, 5)
A_YD, A_OFF, A_ST = (6, 8, 11, 14), (None, 9, 12, 15), (7, 10, 13, None)

C_CAW, C_CAB, C_N1, C_N2, C_SN, C_UB, C_CFB, C_CF2, C_CF0, C_GB = 0, 96, 120, 128, 136, 152, 160, 204, 256, 344


class Steps:

    def __init__(self, eng, sem):
        self.eng, self.sem, self.base, self.k = eng, sem, 0, 0

    def mark(self, ins):
        ins.then_inc(self.sem, 1)
        self.k += 1
        return self.base + self.k

    def wait(self, value):
        self.eng.wait_ge(self.sem, value)

    def link(self, ins):
        self.wait(self.mark(ins))

    @contextmanager
    def loop(self, n, per):
        base = self.base + self.k
        with self.eng.Fori(0, n) as i:
            self.base, self.k = base + i * per, 0
            yield i
            assert self.k == per, f"steps of the body: {self.k}, not {per}"
        self.base, self.k = base + n * per, 0


def hybrid_block(nc, x, norm1_w, w_in, b_gate, conv_a_w, conv_a_b, dt_bias, a_log, d_skip,
                 ssd_norm_w, uv_b, v_ln_w, v_ln_b, w_spatial, b_spatial, w_branch, w_out,
                 norm2_w, w_up, conv_f_w, conv_f_b, w_down, final_norm_w, out):
    ds = bass.ds
    x_v = x.rearrange("b (t p) d -> p (b t) d", p=P)
    out_v = out.rearrange("b (t p) d -> p (b t) d", p=P)
    win_v = w_in.rearrange("l (c p) n -> p (l c) n", p=P)
    wbr_v = w_branch.rearrange("l (c p) n -> p (l c) n", p=P)
    wout_v = w_out.rearrange("l (c p) n -> p (l c) n", p=P)
    wup_v = w_up.rearrange("l (c p) n -> p (l c) n", p=P)
    wdn_v = w_down.rearrange("l (c p) n -> p (l c) n", p=P)

    with ExitStack() as ctx:
        def sb(name, shape, dt=F32, where=ctx):
            return where.enter_context(nc.sbuf_tensor(name, shape, dt))

        def sem(name):
            return ctx.enter_context(nc.semaphore(name))

        raw = sb("raw", [P, 2, 2, W])
        whi = sb("whi", [P, 4, 2, W], F32R)
        wlo = sb("wlo", [P, 4, 2, W], F32R)
        t1h = sb("t1h", [P, KD, S], F32R)
        t1l = sb("t1l", [P, KD, S], F32R)
        ident = sb("ident", [P, P])
        tri = sb("tri", [P, P])
        par = sb("par", [P, 360])
        convx = sb("convx", [P, 2, W + 4])
        rst = sb("rst", [P, 4 * NT])
        msq = sb("msq", [P, 4 * NT])
        half_ms = sb("half_ms", [P, NT])
        minus_half = sb("minus_half", [P, NT])
        ssq = sb("ssq", [P, 4 * NT])
        bns = sb("bns", [P, NT, 2, 6])
        bna = sb("bna", [P, NT, 2])

        s0 = ExitStack()
        xr = sb("xr", [P, NT, D], where=s0)
        xn = sb("xn", [P, NT, D], where=s0)
        prow = sb("prow", [P, 3, P], where=s0)
        s0.close()

        s1 = ExitStack()
        yy = sb("yy", [P, NT, DI], where=s1)
        s2 = ExitStack()
        bf = sb("bf", [P, NG, S], where=s2)
        cf = sb("cf", [P, NG, S], where=s2)
        bcur = sb("bcur", [P, S], where=s2)
        ccur = sb("ccur", [P, S], where=s2)
        bt = sb("bt", [P, NT, P], where=s2)
        cbm = sb("cbm", [P, NT, P], where=s2)
        mm = sb("mm", [P, HG, NT, P], where=s2)
        dif = sb("dif", [P, 4, NT, P], where=s2)
        xf = sb("xf", [P, NT, S], where=s2)
        xdt = sb("xdt", [P, NT, W], where=s2)
        dx = sb("dx", [P, NT, W], where=s2)
        xds = sb("xds", [P, W], where=s2)
        zs = sb("zs", [P, NT, W], where=s2)
        state = sb("state", [P, W], where=s2)
        yt = sb("yt", [P, W], where=s2)
        conv1 = sb("conv1", [P, 2, W], where=s2)
        small = sb("small", [P, 3, NH], where=s2)
        acum = sb("acum", [P, NT, NH], where=s2)
        eac = sb("eac", [P, NT, NH], where=s2)
        etot = sb("etot", [P, NT, NH], where=s2)
        dsd = sb("dsd", [P, NT, NH], where=s2)
        dt = sb("dt", [P, NT, NH], where=s2)
        s2.close()
        s2b = ExitStack()
        sb("before_mm", [P, 2 * NG * S + 2 * S + 2 * NT * P], where=s2b)
        ones = sb("ones", [P, P], where=s2b)
        wdt = sb("wdt", [P, KD, NH], where=s2b)
        wdts = sb("wdts", [P, KD, 2 * NH], F32R, where=s2b)
        dtc = sb("dtc", [P, S], where=s2b)
        rows = sb("rows", [P, S], where=s2b)
        dpre = sb("dpre", [P, NT, NH], where=s2b)
        dex = sb("dex", [P, NT, NH], where=s2b)
        du = sb("du", [P, NT, NH], where=s2b)
        dln = sb("dln", [P, NT, NH], where=s2b)
        adt = sb("adt", [P, NT, NH], where=s2b)
        s2b.close()

        s3 = ExitStack()
        s4 = ExitStack()
        uvb = sb("uvb", [P, D], where=s4)
        lnw = sb("lnw", [P, D], where=s4)
        lnb = sb("lnb", [P, D], where=s4)
        vv = sb("vv", [P, NT, D], where=s4)
        s4.close()
        t2h = sb("t2h", [P, KD, S], F32R, where=s3)
        t2l = sb("t2l", [P, KD, S], F32R, where=s3)
        mg = sb("mg", [P, KD, S], where=s3)
        bsb = sb("bsb", [P, SG * P], where=s3)
        rby = sb("rby", [P, S], where=s3)
        ones1 = sb("ones1", [P, P], where=s3)
        diag1 = sb("diag1", [P, S], where=s3)
        wst = sb("wst", [P, SG, P], where=s3)
        s5 = ExitStack()
        uu = sb("uu", [P, KD, S], where=s5)
        wsp = sb("wsp", [P, SG, P], where=s5)
        s5.close()
        ga = sb("ga", [P, KD, S], where=s3)
        s3.close()
        s1.close()

        hh = sb("hh", [P, NT, D])
        s6 = ExitStack()
        hn = sb("hn", [P, NT, D], where=s6)
        s6.close()
        fth = sb("fth", [P, KF, S], F32R)
        ftl = sb("ftl", [P, KF, S], F32R)
        conv2 = sb("conv2", [P, 4, W])
        rbc = sb("rbc", [P, S])
        s7 = ExitStack()
        ones2 = sb("ones2", [P, P], where=s7)
        diag = sb("diag", [P, S], where=s7)
        s7.close()
        fnw = sb("fnw", [P, D])

        ac_rows = nc.dram_tensor("ac_rows", (NH, S), F32).ap()

        acc = ctx.enter_context(nc.psum_tensor("acc", [P, NT, W], F32))
        aux = ctx.enter_context(nc.psum_tensor("aux", [P, 4, W], F32))

        loaded = [sem(f"loaded{i}") for i in range(2)]
        hi_ready = sem("hi_ready")
        lo_ready = sem("lo_ready")
        unit_used = sem("unit_used")
        acc_ready = sem("acc_ready")
        acc_free = sem("acc_free")
        aux_ready = sem("aux_ready")
        aux_free = sem("aux_free")
        aux_hi = sem("aux_hi")
        consts = sem("consts")
        x_in = [sem(f"x_in{t}") for t in range(NT)]
        prow_in = sem("prow_in")
        small_in = sem("small_in")
        wdt_in = sem("wdt_in")
        rows_in = sem("rows_in")
        bsb_in = sem("bsb_in")
        wsp_in = sem("wsp_in")
        xr_again = sem("xr_again")
        fnw_in = sem("fnw_in")
        squares = sem("squares")
        msq_ready = sem("msq_ready")
        rst_ready = sem("rst_ready")
        normed = sem("normed")
        wdt_hi = sem("wdt_hi")
        wdt_lo = sem("wdt_lo")
        dt_pre = sem("dt_pre")
        dt_exp = sem("dt_exp")
        dt_one = sem("dt_one")
        dt_ln = sem("dt_ln")
        diag_ready = sem("diag_ready")
        adt_ready = sem("adt_ready")
        cum_ready = sem("cum_ready")
        cum_exp = sem("cum_exp")
        rows_out = sem("rows_out")
        pair_in = [sem(f"pair_in{i}") for i in range(2)]
        dif_ready = sem("dif_ready")
        conv_ready = sem("conv_ready")
        silu_ready = sem("silu_ready")
        cur_ready = sem("cur_ready")
        exp_ready = sem("exp_ready")
        m_ready = sem("m_ready")
        xdt_ready = sem("xdt_ready")
        xds_ready = sem("xds_ready")
        state_dec = sem("state_dec")
        yt_ready = sem("yt_ready")
        y_ready = sem("y_ready")
        uv_act = sem("uv_act")
        ln_ready = sem("ln_ready")
        v_ready = sem("v_ready")
        yb_ready = sem("yb_ready")
        ga_ready = sem("ga_ready")
        own_hi = sem("own_hi")
        own_lo = sem("own_lo")
        m_done = sem("m_done")
        flo = sem("flo")
        fsilu = sem("fsilu")
        fprod = sem("fprod")
        fhi = sem("fhi")
        final = sem("final")
        stored = sem("stored")
        act_steps = sem("act_steps")
        dve_steps = sem("dve_steps")

        T_X, T_UP = 8, 8 + 4 * NG

        block = ctx.enter_context(nc.Block())

        @block.sync
        def _(sp):
            def unit(q, p, halves):
                if not (isinstance(q, int) and 4 * q + p < 2):
                    sp.wait_ge(lo_ready, 4 * q + p - 1)
                for dst, src in halves:
                    sp.dma_start(dst, src).then_inc(loaded[p % 2], 16)

            def chunk(q, view, k0, col, between=None):
                for p in range(4):
                    if between:
                        between(p)
                    unit(q, p, [(raw[:, p % 2, r, :], view[:, k0 + 2 * p + r, ds(col, W)]) for r in range(2)])

            for t in range(NT):
                sp.dma_start(xr[:, t, :], x_v[:, t, :]).then_inc(x_in[t], 16)
            sp.dma_start(prow[0:96, 0, :], conv_a_w.rearrange("l k (t p) -> (l k t) p", p=P)).then_inc(prow_in, 16)
            sp.dma_start(prow[96:120, 0, :], conv_a_b.rearrange("l (t p) -> (l t) p", p=P)).then_inc(prow_in, 16)
            sp.dma_start(prow[120:128, 0, :], norm1_w.rearrange("l (t p) -> (l t) p", p=P)).then_inc(prow_in, 16)
            sp.dma_start(prow[0:8, 1, :], norm2_w.rearrange("l (t p) -> (l t) p", p=P)).then_inc(prow_in, 16)
            sp.dma_start(prow[8:24, 1, :], ssd_norm_w.rearrange("l (t p) -> (l t) p", p=P)).then_inc(prow_in, 16)
            sp.dma_start(prow[24:32, 1, :], uv_b[:, 0:D].rearrange("l (t p) -> (l t) p", p=P)).then_inc(prow_in, 16)
            sp.dma_start(prow[32:76, 1, :], conv_f_b.rearrange("l (t p) -> (l t) p", p=P)).then_inc(prow_in, 16)
            cfw = conv_f_w.rearrange("l k (t p) -> (l k t) p", p=P)
            sp.dma_start(prow[76:120, 1, :], cfw[88:132, :]).then_inc(prow_in, 16)
            sp.dma_start(prow[0:88, 2, :], cfw[0:88, :]).then_inc(prow_in, 16)
            sp.dma_start(prow[88:104, 2, :], b_gate.rearrange("l (t p) -> (l t) p", p=P)).then_inc(prow_in, 16)
            chunk(Q_B, win_v, 0, B0)
            chunk(Q_C, win_v, 0, C0)
            chunk(Q_X0, win_v, 0, X0)
            with sp.Fori(0, NG - 1) as j:
                chunk(Q_Z + 2 * j, win_v, 0, Z0 + j * W)
                chunk(Q_Z + 1 + 2 * j, win_v, 0, X0 + W + j * W)
            chunk(Q_Z + 2 * (NG - 1), win_v, 0, Z0 + (NG - 1) * W)
            row = lambda a: a.rearrange("l n -> (l n)").partition_broadcast(P)

            def sgu_rows(p):
                if p:
                    sp.wait_ge(cur_ready, 2 * NG)
                    dst, src = ((uvb, uv_b[:, D:2 * D]), (lnw, v_ln_w), (lnb, v_ln_b))[p - 1]
                    sp.dma_start(dst[:, :], row(src)).then_inc(rows_in, 16)

            chunk(Q_V, win_v, 0, V0, sgu_rows)
            chunk(Q_V + 1, win_v, 0, V0 + W)
            sp.wait_ge(y_ready, NT * NG + 1)
            sp.dma_start(bsb[:, :], b_spatial.rearrange("l g p -> (l g p)").partition_broadcast(P)).then_inc(bsb_in, 16)
            sp.dma_start(wsp[:, :, :], w_spatial.rearrange("l g t s -> t (l g) s")).then_inc(wsp_in, 16)
            for q, view, k0, col in ((Q_U, win_v, 0, U0), (Q_GB, win_v, 0, GB0), (Q_PB, wbr_v, 2 * KD, 0),
                                     (Q_GA, win_v, 0, GA0), (Q_PA, wbr_v, 0, 0), (Q_PA + 2, wbr_v, KD, 0)):
                with sp.Fori(0, 2) as i:
                    chunk(q + i, view, k0, col + i * W)
            sp.wait_ge(aux_ready, J_YA + 2 * KD)
            sp.dma_start(hh[:, :, :], x_v).then_inc(xr_again, 16)
            with sp.Fori(0, 2) as i:
                chunk(Q_WO + i, wout_v, 0, i * W)
            with sp.Fori(0, FC) as i:
                for p in range(4):
                    unit(Q_UP + i, p, [(raw[:, p % 2, r, :].rearrange("p (k n) -> p k n", k=2),
                                        wup_v[:, 2 * p:2 * p + 2, ds(r * FF + i * 256, 256)]) for r in range(2)])
            for n in range(KF):
                c, u = divmod(n, KF // 2)
                unit(Q_DOWN + n // 4, n % 4, [(raw[:, n % 2, r, :], wdn_v[:, 2 * u + r, c * W:(c + 1) * W])
                                              for r in range(2)])
                if n == 0:
                    sp.wait_ge(aux_ready, J_RB + 1)
                    sp.dma_start(fnw[:, :], final_norm_w.partition_broadcast(P)).then_inc(fnw_in, 16)
            for t in range(NT):
                for c in range(2):
                    sp.wait_ge(final, 2 * t + c + 1)
                    sp.dma_start(out_v[:, t, c * W:(c + 1) * W], hh[:, t, c * W:(c + 1) * W]).then_inc(stored, 16)
            sp.wait_ge(stored, 16 * 2 * NT)

        @block.gpsimd
        def _(pool):
            def lo(q, p):
                n = 4 * q + p
                pool.wait_ge(hi_ready, n + 1)
                nc.gpsimd.tensor_tensor(wlo[:, p, :, :], raw[:, p % 2, :, :], whi[:, p, :, :].bitcast(F32),
                                        ALU.subtract).then_inc(lo_ready, 1)

            n_root = [0]

            def root(i, lo=0, hi=NT):
                n_root[0] += 1
                pool.wait_ge(msq_ready, n_root[0])
                cut = slice(i * NT + lo, i * NT + hi)
                nc.gpsimd.tensor_tensor(rst[:, cut], msq[:, cut], minus_half[:, lo:hi], ALU.pow).then_inc(rst_ready, 1)

            for t, v in ((ident, 0.0), (tri, 1.0), (ones, 1.0), (convx, 0.0)):
                nc.gpsimd.memset(t[:], v).then_inc(consts, 1)
            nc.gpsimd.memset(minus_half[:, :], -0.5).then_inc(y_ready, 1)
            pool.wait_ge(y_ready, 1)
            pool.wait_ge(consts, 4)
            nc.gpsimd.affine_select(out=ident[:, :], in_=ident[:, :], compare_op=ALU.not_equal, fill=1.0,
                                    base=0, pattern=[[-1, P]], channel_multiplier=1).then_inc(consts, 1)
            nc.gpsimd.affine_select(out=tri[:, :], in_=tri[:, :], compare_op=ALU.is_ge, fill=0.0,
                                    base=0, pattern=[[1, P]], channel_multiplier=-1).then_inc(consts, 1)
            for t in range(NT):
                root(0, t, t + 1)
            for p in range(4):
                lo(Q_B, p)
            for q in range(Q_C, Q_Z + 1):
                for p in range(4):
                    lo(q, p)

            def group(j):
                qz = Q_Z + 2 * j
                lo(qz + 1, 0)
                lo(qz + 1, 1)
                lo(qz + 1, 2)
                lo(qz + 1, 3)
                for c in range(NT):
                    g8 = ds(j * HG, HG)
                    if c < 3:
                        pool.wait_ge(xdt_ready, 4 * j + c + 1)
                        pool.wait_ge(aux_ready, J_SSD + SSD_JOBS * j + (A_ST[c - 1] + 1 if c else 0))
                        nc.gpsimd.tensor_tensor(
                            xds[:, :].rearrange("p (h d) -> p h d", h=HG),
                            xdt[:, c, :].rearrange("p (h d) -> p h d", h=HG),
                            dsd[:, c, g8].unsqueeze(2).to_broadcast([P, HG, HD]), ALU.mult).then_inc(xds_ready, 1)
                    if c in (1, 2):
                        pool.wait_ge(aux_free, J_SSD + SSD_JOBS * j + A_ST[c - 1] + 1)
                        pool.wait_ge(aux_ready, J_SSD + SSD_JOBS * j + A_OFF[c] + 1)
                        sv = state[:, :].rearrange("p (h d) -> p h d", h=HG)
                        nc.gpsimd.tensor_tensor(sv, sv, etot[:, c, g8].unsqueeze(2).to_broadcast([P, HG, HD]),
                                                ALU.mult).then_inc(state_dec, 1)
                    if c:
                        pool.wait_ge(yt_ready, 3 * j + c)
                    else:
                        pool.wait_ge(aux_free, J_SSD + SSD_JOBS * j + A_YD[0] + 1)
                    pool.wait_ge(acc_free, 4 * qz + c + 1)
                    nc.gpsimd.tensor_tensor(yy[:, c, ds(j * W, W)], yt[:, :], zs[:, c, :],
                                            ALU.mult).then_inc(y_ready, 1)
                    lo(qz + 2, c)

            with pool.Fori(0, NG - 1) as j:
                group(j)
            group(NG - 1)
            for p in range(4):
                lo(Q_U, p)
            root(2)
            for t in range(NT):
                lo(Q_U + 1, t)
            root(1)
            with pool.Fori(0, Q_UP + 1 - Q_GB) as i:
                for p in range(4):
                    lo(Q_GB + i, p)
            root(3)
            with pool.Fori(0, FC - 1) as i:
                for p in range(4):
                    lo(Q_UP + 1 + i, p)
            for n in range(KF):
                lo(Q_DOWN + n // 4, n % 4)
            for t in range(NT):
                root(0, t, t + 1)

        @block.scalar
        def _(act):
            st = Steps(act, act_steps)

            def hi(q, p):
                act.wait_ge(loaded[p % 2], 32 * (2 * q + p // 2) + 32)
                if isinstance(q, int) and q > Q_DOWN:
                    c, u = divmod(4 * (q - 1 - Q_DOWN) + p, KF // 2)
                    if u == KF // 2 - 1:
                        act.wait_ge(acc_ready, 4 * (Q_DOWN + c + 1))
                    else:
                        act.wait_ge(unit_used, 3 * Q_DOWN + c * (KF // 2 - 1) + u + 1)
                elif not (isinstance(q, int) and q == 0):
                    if p == 3:
                        act.wait_ge(acc_ready, 4 * q)
                    else:
                        act.wait_ge(unit_used, 3 * q + p - 2)
                nc.scalar.activation(whi[:, p, :, :], raw[:, p % 2, :, :], ACT.Copy).then_inc(hi_ready, 1)

            def aux_split(job, dst, scale=1.0):
                act.wait_ge(aux_ready, job + 1)
                nc.scalar.activation(dst, aux[:, job % 4, :], ACT.Copy, scale=scale).then_inc(aux_hi, 1)

            def conv_in(a, f, tile):
                act.wait_ge(acc_ready, 4 * a + f + 1)
                if not (isinstance(tile, int) and tile < 2):
                    act.wait_ge(conv_ready, tile - 1)
                nc.scalar.activation(convx[:, f % 2, 3:3 + W], acc[:, f, :], ACT.Copy).then_inc(acc_free, 1)

            def conv_silu(f, tile, dst):
                act.wait_ge(conv_ready, tile + 1)
                nc.scalar.activation(dst, conv1[:, f % 2, :], ACT.Silu).then_inc(silu_ready, 1)

            def conv_chunk(a, tile, dst, early, between=lambda where: None, silu_next=True):
                hi(a + 1, 0)
                hi(a + 1, 1)
                early()
                if silu_next:
                    act.preload_act_table(ACT.Silu)
                conv_in(a, 0, tile)
                conv_in(a, 1, tile + 1)
                hi(a + 1, 2)
                between(1)
                conv_in(a, 2, tile + 2)
                conv_silu(0, tile, dst(0))
                conv_in(a, 3, tile + 3)
                conv_silu(1, tile + 1, dst(1))
                hi(a + 1, 3)
                between(2)
                conv_silu(2, tile + 2, dst(2))
                conv_silu(3, tile + 3, dst(3))

            act.preload_act_table(ACT.Copy)
            for t in range(NT):
                act.wait_ge(x_in[t], 16)
                nc.scalar.activation(xn[:, t, :], xr[:, t, :], ACT.Square,
                                     accum_out=ssq[:, t:t + 1]).then_inc(squares, 1)
            act.dma_start(wdt[:, :, :], win_v[:, :, DT0:DT0 + NH]).then_inc(wdt_in, 16)
            act.dma_start(small[:, 0, :], dt_bias.rearrange("l n -> (l n)").partition_broadcast(P)).then_inc(small_in, 16)
            act.dma_start(small[:, 1, :], a_log.rearrange("l n -> (l n)").partition_broadcast(P)).then_inc(small_in, 16)
            act.dma_start(small[:, 2, :], d_skip.rearrange("l n -> (l n)").partition_broadcast(P)).then_inc(small_in, 16)
            hi(Q_B, 0)
            act.wait_ge(aux_free, J_PAR + 1)
            for k in range(KD):
                aux_split(J_N1 + k, t1h[:, k, :], par[:, C_N1 + k:C_N1 + k + 1])
                if k in (3, 5, 7):
                    hi(Q_B, (k - 1) // 2)
            act.wait_ge(wdt_in, 16)
            nc.scalar.activation(wdts[:, :, 0:NH], wdt[:, :, :], ACT.Copy).then_inc(wdt_hi, 1)

            def decay_tables():
                act.wait_ge(aux_free, J_CUM + 1)
                nc.scalar.activation(eac[:, :, :], acum[:, :, :], ACT.Exp).then_inc(cum_exp, 1)
                act.wait_ge(cum_ready, 1)
                nc.scalar.activation(etot[:, :, :], etot[:, :, :], ACT.Exp).then_inc(cum_exp, 1)
                nc.scalar.activation(dsd[:, :, :], dsd[:, :, :], ACT.Exp).then_inc(cum_exp, 1)
                act.wait_ge(aux_ready, J_ROWS + 1)
                nc.scalar.activation(rows[0:NH, :], aux[0:NH, J_ROWS % 4, :], ACT.Copy).then_inc(aux_free, 1)
                act.wait_ge(aux_free, J_ROWS + 1)
                act.dma_start(ac_rows, rows[0:NH, :]).then_inc(rows_out, 16)
                act.wait_ge(silu_ready, 8)
                current(0, 0)
                current(0, 1)
                act.wait_ge(rows_out, 16)
                load_pair(0, 0)
                load_pair(0, 1)

            def load_pair(j, q):
                act.dma_start(dif[:, 2 * (q % 2):2 * (q % 2) + 2, :, :].rearrange("p h t n -> p h (t n)"),
                              ac_rows[ds(HG * j + 2 * q, 2), :].partition_broadcast(P)).then_inc(pair_in[q % 2], 16)

            def current(g, which):
                src, dst = ((bf, bcur), (cf, ccur))[which]
                nc.scalar.activation(dst[:, :].unsqueeze(1), src[:, ds(g, 1), :], ACT.Copy).then_inc(cur_ready, 1)

            conv_chunk(Q_B, 0, lambda f: bf[:, f, :], early=lambda: None)
            act.wait_ge(dt_pre, 1)
            nc.scalar.activation(dex[:, :, :], du[:, :, :], ACT.Exp).then_inc(dt_exp, 1)
            act.wait_ge(small_in, 48)
            st.link(nc.scalar.activation(small[:, 1, :], small[:, 1, :], ACT.Exp))
            act.wait_ge(dt_one, 1)
            nc.scalar.activation(dln[:, :, :], du[:, :, :], ACT.Ln).then_inc(dt_ln, 1)
            conv_chunk(Q_C, 4, lambda f: cf[:, f, :], early=lambda: None)
            conv_chunk(Q_X0, T_X, lambda f: xf[:, f, :], early=decay_tables)

            def decay(j, *hs):
                for h in hs:
                    act.wait_ge(dif_ready, HG * j + h + 1)
                    nc.scalar.activation(dif[:, h % 4, :, :], dif[:, h % 4, :, :], ACT.Exp).then_inc(exp_ready, 1)

            def beside_z(j):
                a = Q_Z + 2 * j
                hi(a + 1, 0)
                act.preload_act_table(ACT.Exp)
                decay(j, 0, 1, 2, 3)
                hi(a + 1, 1)
                for q in (2, 3):
                    act.wait_ge(m_ready, HG * j + 2 * q - 2)
                    load_pair(j, q)
                hi(a + 1, 2)
                decay(j, 4, 5, 6, 7)
                act.preload_act_table(ACT.Silu)
                for t in range(NT):
                    act.wait_ge(acc_ready, 4 * a + t + 1)
                    if t == 0:
                        act.wait_ge(y_ready, 4 * j + 1)
                    nc.scalar.activation(zs[:, t, :], acc[:, t, :], ACT.Silu).then_inc(acc_free, 1)
                hi(a + 1, 3)

            with act.Fori(0, NG - 1) as j:
                beside_z(j)

                def next_pairs():
                    act.wait_ge(m_ready, HG * j + HG)
                    load_pair(j + 1, 0)
                    load_pair(j + 1, 1)

                def between(where):
                    if where == 1:
                        current(j + 1, 0)
                    elif where == 2:
                        act.wait_ge(aux_ready, J_SSD + SSD_JOBS * j + SSD_JOBS)
                        current(j + 1, 1)

                conv_chunk(Q_Z + 1 + 2 * j, T_X + 4 + 4 * j, lambda f: xf[:, f, :], next_pairs, between, False)
            beside_z(NG - 1)
            for p in range(4):
                hi(Q_V + 1, p)

            def activate_v(a, t, i):
                act.wait_ge(acc_free, 4 * a + t + 1)
                cut = vv[:, t, ds(i * W, W)]
                nc.scalar.activation(cut, cut, GELU).then_inc(uv_act, 1)

            def activate(q, i, dst, func, col):
                for f in range(4):
                    act.wait_ge(acc_ready, 4 * q + f + 1)
                    nc.scalar.activation(dst[:, ds(4 * i + f, 1), :], acc[:, f:f + 1, :], func,
                                         bias=par[:, ds(col + 4 * i + f, 1)]).then_inc(acc_free, 1)

            def split(k, src, dst):
                nc.scalar.activation(dst[:, k, :], src[:, k, :], ACT.Copy).then_inc(own_hi, 1)

            GELU = ACT.Gelu_apprx_tanh
            for t in range(NT):
                activate_v(Q_V, t, 0)
            for p in range(3):
                hi(Q_V + 2, p)
            for t in range(NT):
                activate_v(Q_V + 1, t, 1)
                if t == 2:
                    hi(Q_V + 2, 3)
            for t in range(NT):
                act.wait_ge(y_ready, NT * NG + 1)
                nc.scalar.activation(mg[:, 4 * (t % 2):4 * (t % 2) + 4, :].rearrange("p a n -> p (a n)"), yy[:, t, :],
                                     ACT.Square, accum_out=ssq[:, NT + t:NT + t + 1]).then_inc(squares, 1)
                if t == 1:
                    act.wait_ge(squares, NT + 2)
            act.wait_ge(squares, 2 * NT)
            with act.Fori(0, 2) as i:
                for p in range(3):
                    hi(Q_U + 1 + i, p)
                activate(Q_U + i, i, uu, GELU, C_UB)
                hi(Q_U + 1 + i, 3)
            for p in range(3):
                hi(Q_GB + 1, p)
            activate(Q_GB, 0, mg, ACT.Sigmoid, C_GB + KD)
            hi(Q_GB + 1, 3)

            def split_yb(*ks):
                for k in ks:
                    act.wait_ge(yb_ready, k + 1)
                    split(k, uu, t2h)

            act.wait_ge(aux_ready, J_MIX + SG)
            hi(Q_GB + 2, 0)
            hi(Q_GB + 2, 1)
            split_yb(0, 1, 2, 3)
            hi(Q_GB + 2, 2)
            split_yb(4, 5, 6, 7)
            activate(Q_GB + 1, 1, mg, ACT.Sigmoid, C_GB + KD)
            hi(Q_GB + 2, 3)
            with act.Fori(0, 2) as i:
                for p in range(4):
                    hi(Q_PB + 1 + i, p)
            act.wait_ge(own_lo, KD)
            sn = lambda k: par[:, C_SN + k:C_SN + k + 1]
            for i in range(2):
                hi(Q_GA + 1 + i, 0)
                hi(Q_GA + 1 + i, 1)
                aux_split(J_YA + 4 * i, t2h[:, 4 * i, :], sn(4 * i))
                aux_split(J_YA + 4 * i + 1, t2h[:, 4 * i + 1, :], sn(4 * i + 1))
                hi(Q_GA + 1 + i, 2)
                aux_split(J_YA + 4 * i + 2, t2h[:, 4 * i + 2, :], sn(4 * i + 2))
                activate(Q_GA + i, i, ga, ACT.Sigmoid, C_GB)
                hi(Q_GA + 1 + i, 3)
                aux_split(J_YA + 4 * i + 3, t2h[:, 4 * i + 3, :], sn(4 * i + 3))
            for i in range(2):
                for p in range(4):
                    hi(Q_PA + 1 + i, p)
                    aux_split(J_YA + KD + 4 * i + p, t1h[:, 4 * i + p, :], sn(KD + 4 * i + p))
            for p in range(4):
                hi(Q_PA + 3, p)
            def split_m(*ks):
                for k in ks:
                    act.wait_ge(m_done, KD + k + 1)
                    split(k, mg, t2h)

            hi(Q_WO, 0)
            hi(Q_WO, 1)
            act.wait_ge(acc_ready, 4 * (Q_PA + 2))
            split_m(0, 1, 2, 3)
            hi(Q_WO, 2)
            hi(Q_WO, 3)
            split_m(4, 5, 6, 7)
            for p in range(4):
                hi(Q_WO + 1, p)
            split_h = lambda *ks: [aux_split(J_N2 + k, t1h[:, k, :], par[:, C_N2 + k:C_N2 + k + 1]) for k in ks]
            hi(Q_UP, 0)
            hi(Q_UP, 1)
            split_h(0, 1)
            hi(Q_UP, 2)
            split_h(2, 3)
            hi(Q_UP, 3)
            for t in range(NT):
                act.wait_ge(acc_free, 4 * (Q_WO + 1) + t + 1)
                nc.scalar.activation(hn[:, t, :], hh[:, t, :], ACT.Square,
                                     accum_out=ssq[:, NT + t:NT + t + 1]).then_inc(squares, 1)

            def ffn(i, first=False):
                q, tile = Q_UP + i, T_UP + 4 * i
                hi(q + 1, 0)
                if first:
                    split_h(4, 5)
                hi(q + 1, 1)
                if first:
                    split_h(6, 7)
                hi(q + 1, 2)
                for f in range(2):
                    act.wait_ge(conv_ready, tile + f + 1)
                    nc.scalar.activation(conv2[:, f, :], conv2[:, f, :], ACT.Silu).then_inc(fsilu, 1)
                hi(q + 1, 3)
                for f in range(2):
                    act.wait_ge(fprod, 2 * i + f + 1)
                    nc.scalar.activation(fth[:, ds(2 * i + f, 1), :], conv2[:, 2 + f, :].unsqueeze(1),
                                         ACT.Copy).then_inc(fhi, 1)

            ffn(0, first=True)
            act.preload_act_table(ACT.Silu)
            with act.Fori(0, FC - 1) as i:
                ffn(i + 1)
            for n in range(4, KF):
                hi(Q_DOWN + n // 4, n % 4)
            for c in range(2):
                for t in range(NT):
                    act.wait_ge(acc_free, 4 * (Q_DOWN + c) + t + 1)
                    if c or t >= 2:
                        act.wait_ge(squares, 3 * NT + c * NT + t - 1)
                    nc.scalar.activation(conv2[:, t % 2, :], hh[:, t, c * W:(c + 1) * W], ACT.Square,
                                         accum_out=ssq[:, (2 + c) * NT + t:(2 + c) * NT + t + 1]).then_inc(squares, 1)

        @block.vector
        def _(dve):
            st = Steps(dve, dve_steps)
            V = nc.vector
            tok = lambda ap: ap.unsqueeze(1).to_broadcast([P, NT, NH])
            v4 = lambda ap: ap.rearrange("p (t n) -> p t n", t=4)
            vh = lambda ap: ap.rearrange("p (h d) -> p h d", h=HG)
            heads = lambda ap: ap.unsqueeze(2).to_broadcast([P, HG, HD])
            flat = lambda ap: ap.rearrange("p t n -> p (t n)")
            causal = tri[:, :].unsqueeze(1).to_broadcast([P, 4, P])

            n_root = [0]

            def rsqrt(i, src, n, eps, wait=True):
                V.tensor_scalar(msq[:, i * NT:(i + 1) * NT], src, 1.0 / n, eps, ALU.mult,
                                ALU.add).then_inc(msq_ready, 1)
                n_root[0] += 1
                if wait:
                    dve.wait_ge(rst_ready, n_root[0])

            def rsqrt_tile(t):
                V.tensor_scalar(msq[:, t:t + 1], ssq[:, t:t + 1], 1.0 / D, NORM_EPS, ALU.mult,
                                ALU.add).then_inc(msq_ready, 1)
                n_root[0] += 1

            n_hi = [0]

            def transposed(job, dst_l, dst_h, scale=1.0):
                n_hi[0] += 1
                dve.wait_ge(aux_hi, n_hi[0])
                V.scalar_tensor_tensor(dst_l, aux[:, job % 4, :], scale, dst_h.bitcast(F32), ALU.mult,
                                       ALU.subtract).then_inc(aux_free, 1)

            for t in range(NT):
                dve.wait_ge(squares, t + 1)
                rsqrt_tile(t)
                if t == NT - 1:
                    dve.wait_ge(aux_ready, J_PAR + 1)
                    last = st.mark(V.tensor_copy(par[:, 0:248], aux[:, 0, 0:248]))
                    V.tensor_copy(par[:, 256:360], aux[:, 0, 256:360]).then_inc(aux_free, 1)
                dve.wait_ge(rst_ready, t + 1)
                V.tensor_scalar(xn[:, t, :], xr[:, t, :], rst[:, t:t + 1], None, ALU.mult).then_inc(normed, 1)
            st.wait(last)
            dve.wait_ge(aux_free, J_PAR + 1)
            for k in range(KD):
                transposed(J_N1 + k, t1l[:, k, :], t1h[:, k, :], par[:, C_N1 + k:C_N1 + k + 1])
            dve.wait_ge(wdt_hi, 1)
            V.tensor_tensor(wdts[:, :, NH:2 * NH], wdt[:, :, :], wdts[:, :, 0:NH].bitcast(F32),
                            ALU.subtract).then_inc(wdt_lo, 1)

            class Conv:

                def __init__(self, f, taps, wcols, bcol, dst, ready):
                    self.f, self.taps, self.wcols, self.bcol, self.dst, self.ready = f, taps, wcols, bcol, dst, ready
                    self.i = 0

                def step(self):
                    i, off = self.i, 4 - self.taps + self.i
                    src = convx[:, self.f % 2, off:off + W]
                    if i == 0:
                        self.ready()
                        ins = V.tensor_scalar(self.dst, src, par[:, self.wcols[0]], par[:, self.bcol], ALU.mult, ALU.add)
                    else:
                        st.wait(self.last)
                        ins = V.scalar_tensor_tensor(self.dst, src, par[:, self.wcols[i]], self.dst, ALU.mult, ALU.add)
                    if i == self.taps - 1:
                        ins.then_inc(conv_ready, 1)
                    else:
                        self.last = st.mark(ins)
                    self.i += 1

            def conv_a(a, f, tile, col):
                def ready():
                    dve.wait_ge(acc_free, 4 * a + f + 1)
                    if not (isinstance(tile, int) and tile < 2):
                        dve.wait_ge(silu_ready, tile - 1)

                return Conv(f, 4, [ds(C_CAW + 24 * i + col, 1) for i in range(4)], ds(C_CAB + col, 1),
                            conv1[:, f % 2, :], ready)

            def conv_pair(a, f, tile, col):
                two = [conv_a(a, f + i, tile + i, col + i) for i in range(2)]
                for i in (0, 0, 1, 0, 1, 0, 1, 1):
                    two[i].step()

            conv_pair(Q_B, 0, 0, 16)
            dve.wait_ge(aux_ready, J_DTC + 1)
            V.tensor_copy(dtc[0:2 * NH, :], aux[0:2 * NH, J_DTC % 4, :]).then_inc(aux_free, 1)
            conv_pair(Q_B, 2, 2, 18)

            bank3 = lambda job: aux[:, job % 4, 0:P].rearrange("p (t h) -> p t h", t=NT)
            dve.wait_ge(aux_ready, J_DT + 1)
            dve.wait_ge(small_in, 48)
            two = aux[:, J_DT % 4, 0:2 * P].rearrange("p (t i h) -> p t i h", t=NT, i=2)
            st.link(V.tensor_tensor(dpre[:, :, :], two[:, :, 0, :], tok(small[:, 0, :]), ALU.add))
            V.tensor_tensor(dpre[:, :, :], two[:, :, 1, :], dpre[:, :, :], ALU.add).then_inc(aux_free, 1)
            dve.wait_ge(aux_free, J_DT + 1)
            V.scalar_tensor_tensor(du[:, :, :], dpre[:, :, :], -1.0, dpre[:, :, :], ALU.mult,
                                   ALU.min).then_inc(dt_pre, 1)
            dve.wait_ge(dt_exp, 1)
            V.tensor_scalar(du[:, :, :], dex[:, :, :], 1.0, None, ALU.add).then_inc(dt_one, 1)
            dve.wait_ge(dt_one, 1)
            st.link(V.scalar_tensor_tensor(dex[:, :, :], du[:, :, :], 1.0, dex[:, :, :], ALU.subtract, ALU.subtract))
            st.link(V.reciprocal(adt[:, :, :], du[:, :, :]))
            st.link(V.tensor_tensor(adt[:, :, :], adt[:, :, :], dex[:, :, :], ALU.mult))
            dve.wait_ge(dt_ln, 1)
            st.link(V.tensor_tensor(dln[:, :, :], dln[:, :, :], adt[:, :, :], ALU.subtract))
            st.link(V.scalar_tensor_tensor(dt[:, :, :], dpre[:, :, :], 0.0, dln[:, :, :], ALU.max, ALU.add))
            dve.wait_ge(act_steps, 1)
            V.scalar_tensor_tensor(adt[:, :, :], dt[:, :, :], -1.0, tok(small[:, 1, :]), ALU.mult,
                                   ALU.mult).then_inc(adt_ready, 1)

            dve.wait_ge(aux_ready, J_CUM + 1)
            V.tensor_copy(acum[:, :, :], bank3(J_CUM)).then_inc(aux_free, 1)
            dve.wait_ge(aux_free, J_CUM + 1)
            dve.wait_ge(aux_ready, J_TOT + 1)
            V.tensor_copy(etot[:, :, :], bank3(J_TOT)).then_inc(aux_free, 1)
            dve.wait_ge(aux_free, J_TOT + 1)
            V.tensor_tensor(dsd[:, :, :], etot[:, :, :], acum[:, :, :], ALU.subtract).then_inc(cum_ready, 1)

            for f in (0, 2):
                conv_pair(Q_C, f, 4 + f, 20 + f)
            for f in (0, 2):
                conv_pair(Q_X0, f, T_X + f, f)

            dve.wait_ge(cum_exp, 3)

            def exponents(j, *hs):
                for h in hs:
                    dve.wait_ge(pair_in[h // 2 % 2], 32 * j + 16 * (h // 4) + 16)
                    for c in range(NT):
                        ins = V.tensor_scalar(dif[:, h % 4, c, :], dif[:, h % 4, c, :],
                                              acum[:, c, ds(HG * j + h, 1)], 0.0, ALU.subtract, ALU.min)
                    ins.then_inc(dif_ready, 1)

            def beside_z(j):
                base = J_SSD + SSD_JOBS * j
                bank = lambda k: aux[:, (J_SSD + k) % 4, :]
                g8 = ds(HG * j, HG)

                def masked(h):
                    dve.wait_ge(exp_ready, HG * j + h + 1)
                    V.tensor_tensor(mm[:, h, :, :], dif[:, h % 4, :, :], cbm[:, :, :], ALU.mult).then_inc(m_ready, 1)

                def tokens(c):
                    dve.wait_ge(aux_ready, base + A_XS[c] + 1)
                    V.tensor_tensor(vh(xdt[:, c, :]), vh(bank(A_XS[c])), heads(dt[:, c, g8]),
                                    ALU.mult).then_inc(xdt_ready, 1)
                    V.tensor_tensor(vh(dx[:, c, :]), vh(bank(A_XS[c])), heads(small[:, 2, g8]),
                                    ALU.mult).then_inc(aux_free, 1)

                dve.wait_ge(aux_ready, base + A_BT + 1)
                V.tensor_copy(bt[:, :, :], v4(bank(A_BT))).then_inc(aux_free, 1)
                dve.wait_ge(aux_ready, base + A_CB + 1)
                V.tensor_tensor(cbm[:, :, :], v4(bank(A_CB)), causal, ALU.mult).then_inc(aux_free, 1)
                dve.wait_ge(aux_free, base + A_CB + 1)
                for h in range(4):
                    masked(h)
                tokens(0)
                tokens(1)
                exponents(j, 4, 5, 6, 7)
                for h in range(4, HG):
                    masked(h)
                tokens(2)
                tokens(3)

            def ssd_chunk(j, c):
                base = J_SSD + SSD_JOBS * j
                bank = lambda k: aux[:, (J_SSD + k) % 4, :]
                g8 = ds(HG * j, HG)
                dve.wait_ge(aux_ready, base + A_YD[c] + 1)
                dve.wait_ge(y_ready, NT * j + c + 1)
                V.tensor_tensor(yt[:, :], bank(A_YD[c]), dx[:, c, :], ALU.add).then_inc(aux_free, 1)
                if c:
                    dve.wait_ge(aux_ready, base + A_OFF[c] + 1)
                    dve.wait_ge(aux_free, base + A_YD[c] + 1)
                    V.tensor_tensor(vh(dx[:, c, :]), vh(bank(A_OFF[c])), heads(eac[:, c, g8]),
                                    ALU.mult).then_inc(aux_free, 1)
                    dve.wait_ge(aux_free, base + A_OFF[c] + 1)
                    V.tensor_tensor(yt[:, :], yt[:, :], dx[:, c, :], ALU.add).then_inc(yt_ready, 1)
                if c < NT - 1:
                    dve.wait_ge(aux_ready, base + A_ST[c] + 1)
                    if c:
                        dve.wait_ge(state_dec, 2 * j + c)
                        V.tensor_tensor(state[:, :], bank(A_ST[c]), state[:, :], ALU.add).then_inc(aux_free, 1)
                    else:
                        V.tensor_copy(state[:, :], bank(A_ST[c])).then_inc(aux_free, 1)

            exponents(0, 0, 1, 2, 3)
            with st.loop(NG - 1, 12) as j:
                beside_z(j)
                ssd_chunk(j, 0)
                ssd_chunk(j, 1)
                exponents(j + 1, 0, 1, 2, 3)
                ssd_chunk(j, 2)
                conv_pair(Q_Z + 1 + 2 * j, 0, T_X + 4 + 4 * j, 4 * j + 4)
                ssd_chunk(j, 3)
                conv_pair(Q_Z + 1 + 2 * j, 2, T_X + 4 + 4 * j + 2, 4 * j + 6)
            beside_z(NG - 1)
            for c in range(NT):
                ssd_chunk(NG - 1, c)

            def biased(a, i, dst, bias, col):
                for t in range(NT):
                    dve.wait_ge(acc_ready, 4 * a + t + 1)
                    V.tensor_tensor(dst[:, t, ds(i * W, W)], acc[:, t, :], bias[:, ds(col + i * W, W)],
                                    ALU.add).then_inc(acc_free, 1)

            dve.wait_ge(rows_in, 48)
            dve.wait_ge(y_ready, NT * NG + 1)
            with dve.Fori(0, 2) as i:
                biased(Q_V + i, i, vv, uvb, 0)
            for i in range(2):
                dve.wait_ge(aux_ready, J_WT + i + 1)
                V.tensor_tensor(wst[:, 4 * i:4 * i + 4, :], v4(aux[:, (J_WT + i) % 4, :]), causal,
                                ALU.mult).then_inc(aux_free, 1)
            for t in range(NT):
                dve.wait_ge(uv_act, NT + t + 1)
                for i in range(2):
                    last = st.mark(V.bn_stats(bns[:, t, i, :], vv[:, t, i * W:(i + 1) * W]))
                st.wait(last)
                st.link(V.bn_aggr(bna[:, t, :], bns[:, t, :, :].rearrange("p a b -> p (a b)")))
            rsqrt(2, bna[:, :, 1], 1, LN_EPS)
            for t in range(NT):
                V.scalar_tensor_tensor(vv[:, t, :], vv[:, t, :], bna[:, t, 0:1], lnw[:, :], ALU.subtract,
                                       ALU.mult).then_inc(ln_ready, 1)
            for t in range(NT):
                dve.wait_ge(ln_ready, t + 1)
                V.scalar_tensor_tensor(vv[:, t, :], vv[:, t, :], rst[:, 2 * NT + t:2 * NT + t + 1], lnb[:, :],
                                       ALU.mult, ALU.add).then_inc(v_ready, 1)
            dve.wait_ge(squares, 2 * NT)
            rsqrt(1, ssq[:, NT:2 * NT], DI, NORM_EPS, wait=False)
            dve.wait_ge(bsb_in, 16)

            def mixed(g):
                dve.wait_ge(aux_ready, J_MIX + g + 1)
                if g >= 2:
                    dve.wait_ge(yb_ready, g - 1)
                V.tensor_tensor(v4(convx[:, g % 2, 3:3 + W]), v4(aux[:, (J_MIX + g) % 4, :]),
                                bsb[:, g * P:(g + 1) * P].unsqueeze(1).to_broadcast([P, 4, P]),
                                ALU.add).then_inc(aux_free, 1)

            mixed(0)
            for g in range(SG):
                if g < SG - 1:
                    mixed(g + 1)
                dve.wait_ge(aux_free, J_MIX + g + 1)
                if g == 0:
                    dve.wait_ge(acc_free, 4 * (Q_U + 2))
                V.tensor_tensor(uu[:, g, :], convx[:, g % 2, 3:3 + W], uu[:, g, :], ALU.mult).then_inc(yb_ready, 1)

            n_own = [0]

            def rest(k, src, dst_h, dst_l):
                n_own[0] += 1
                dve.wait_ge(own_hi, n_own[0])
                V.tensor_tensor(dst_l[:, k, :], src[:, k, :], dst_h[:, k, :].bitcast(F32),
                                ALU.subtract).then_inc(own_lo, 1)

            def token_rows(i, ones_t, diag_t, job, dst):
                dve.wait_ge(rst_ready, n_root[0])
                for t in range(NT):
                    last = st.mark(V.tensor_scalar(diag_t[:, t * P:(t + 1) * P], ident[:, :],
                                                   rst[:, i * NT + t:i * NT + t + 1], None, ALU.mult))
                st.wait(last)
                V.memset(ones_t[:, :], 1.0).then_inc(diag_ready, 1)
                dve.wait_ge(aux_ready, job + 1)
                V.tensor_copy(dst[:, :], aux[:, job % 4, :]).then_inc(aux_free, 1)
                dve.wait_ge(aux_free, job + 1)

            token_rows(1, ones1, diag1, J_RY, rby)
            for k in range(KD):
                rest(k, uu, t2h, t2l)
            dve.wait_ge(acc_free, 4 * (Q_GB + 2))
            with dve.Fori(0, 2) as i:
                for f in range(4):
                    dve.wait_ge(acc_ready, 4 * Q_PB + 4 * i + f + 1)
                    m = mg[:, ds(4 * i + f, 1), :]
                    V.tensor_tensor(m, acc[:, f:f + 1, :], m, ALU.mult).then_inc(acc_free, 1)
            sn = lambda k: par[:, C_SN + k:C_SN + k + 1]
            for i in range(2):
                for k in range(4 * i, 4 * i + 3):
                    transposed(J_YA + k, t2l[:, k, :], t2h[:, k, :], sn(k))
                for f in range(4):
                    dve.wait_ge(acc_free, 4 * (Q_GA + i) + f + 1)
                    g = ga[:, 4 * i + f, :]
                    V.tensor_tensor(g, g, rby[:, :], ALU.mult).then_inc(ga_ready, 1)
                k = 4 * i + 3
                transposed(J_YA + k, t2l[:, k, :], t2h[:, k, :], sn(k))

            n_merge = [0]

            def merge(half, c):
                a = Q_PA + 2 * half + c
                for f in range(4):
                    k = 4 * c + f
                    dve.wait_ge(acc_ready, 4 * a + f + 1)
                    pa = convx[:, f % 2, 3:3 + W]
                    if n_merge[0] + f >= 2:
                        dve.wait_ge(m_done, n_merge[0] + f - 1)
                    V.tensor_tensor(pa, acc[:, f, :], ga[:, k, :], ALU.mult).then_inc(acc_free, 1)
                    dve.wait_ge(acc_free, 4 * a + f + 1)
                    V.tensor_tensor(mg[:, k, :], mg[:, k, :], pa, ALU.add).then_inc(m_done, 1)
                n_merge[0] += 4

            def second_half(*ks):
                for k in ks:
                    transposed(J_YA + KD + k, t1l[:, k, :], t1h[:, k, :], sn(KD + k))

            second_half(0, 1, 2)
            dve.wait_ge(ga_ready, KD)
            merge(0, 0)
            second_half(3, 4, 5, 6)
            merge(0, 1)
            second_half(7)
            merge(1, 0)
            for k in range(4):
                rest(k, mg, t2h, t2l)
            merge(1, 1)
            for k in range(4, KD):
                rest(k, mg, t2h, t2l)

            def residual(a, c, *tiles):
                for t in tiles or range(NT):
                    dve.wait_ge(acc_ready, 4 * a + t + 1)
                    cut = slice(c * W, (c + 1) * W)
                    V.tensor_tensor(hh[:, t, cut], acc[:, t, :], hh[:, t, cut], ALU.add).then_inc(acc_free, 1)

            dve.wait_ge(xr_again, 16)
            residual(Q_WO, 0)
            on_channels = lambda k: transposed(J_N2 + k, t1l[:, k, :], t1h[:, k, :], par[:, C_N2 + k:C_N2 + k + 1])
            for k in range(4):
                on_channels(k)
            residual(Q_WO + 1, 1)
            for k in range(4, KD):
                on_channels(k)
            dve.wait_ge(squares, 3 * NT)
            rsqrt(3, ssq[:, NT:2 * NT], D, NORM_EPS)
            token_rows(3, ones2, diag, J_RB, rbc)

            def ffn(i):
                a, tile = Q_UP + i, T_UP + 4 * i

                def scaled(f):
                    if f >= 2:
                        dve.wait_ge(conv_ready, tile + f - 1)
                    dve.wait_ge(acc_ready, 4 * a + f + 1)
                    V.tensor_tensor(convx[:, f % 2, 3:3 + W], acc[:, f, :], rbc[:, :], ALU.mult).then_inc(acc_free, 1)

                def conv_f(f):
                    col = 2 * i + f if f < 2 else KF + 2 * i + f - 2

                    def ready():
                        dve.wait_ge(acc_free, 4 * a + f + 1)
                        if not isinstance(i, int):
                            dve.wait_ge(flo if f >= 2 else fprod, 2 * i)

                    return Conv(f, 3, [ds(C_CF0 + col, 1), ds(C_CF0 + 2 * KF + col, 1), ds(C_CF2 + col, 1)],
                                ds(C_CFB + col, 1), conv2[:, f, :], ready)

                def product(f):
                    dve.wait_ge(conv_ready, tile + 2 + f + 1)
                    dve.wait_ge(fsilu, 2 * i + f + 1)
                    V.tensor_tensor(conv2[:, 2 + f, :], conv2[:, f, :], conv2[:, 2 + f, :],
                                    ALU.mult).then_inc(fprod, 1)

                g0, g1, v0, v1 = (conv_f(f) for f in range(4))
                scaled(0)
                g0.step()
                scaled(1)
                g0.step()
                g1.step()
                g0.step()
                g1.step()
                scaled(2)
                g1.step()
                v0.step()
                scaled(3)
                v0.step()
                v1.step()
                v0.step()
                v1.step()
                product(0)
                v1.step()
                product(1)
                for f in range(2):
                    dve.wait_ge(fhi, 2 * i + f + 1)
                    V.tensor_tensor(ftl[:, ds(2 * i + f, 1), :], conv2[:, 2 + f, :].unsqueeze(1),
                                    fth[:, ds(2 * i + f, 1), :].bitcast(F32), ALU.subtract).then_inc(flo, 1)

            ffn(0)
            with st.loop(FC - 1, 8) as i:
                ffn(i + 1)

            residual(Q_DOWN, 0)
            dve.wait_ge(squares, 4 * NT)
            st.link(V.tensor_scalar(half_ms[:, :], ssq[:, 2 * NT:3 * NT], 1.0 / D, NORM_EPS, ALU.mult, ALU.add))
            dve.wait_ge(fnw_in, 16)
            for t in range(NT):
                residual(Q_DOWN + 1, 1, t)
                r = rst[:, t:t + 1]
                dve.wait_ge(squares, 4 * NT + t + 1)
                V.scalar_tensor_tensor(msq[:, t:t + 1], ssq[:, 3 * NT + t:3 * NT + t + 1], 1.0 / D,
                                       half_ms[:, t:t + 1], ALU.mult, ALU.add).then_inc(msq_ready, 1)
                n_root[0] += 1
                dve.wait_ge(rst_ready, n_root[0])
                for c in range(2):
                    cut = slice(c * W, (c + 1) * W)
                    V.scalar_tensor_tensor(hh[:, t, cut], hh[:, t, cut], r, fnw[:, cut], ALU.mult,
                                           ALU.mult).then_inc(final, 1)

        @block.tensor
        def _(pe):
            MM = nc.tensor.matmul

            def unit(n, slot, first, last, a, acts, ks, kind, at=None):
                pe.wait_ge(lo_ready, n + 1)
                ah, al = acts
                for t in range(4):
                    if first and not (isinstance(a, int) and a == 0):
                        pe.wait_ge(acc_free, 4 * a + t - 3)
                    for r, k in enumerate(ks):
                        for i, (w, x) in enumerate(((whi, ah), (whi, al), (wlo, ah))):
                            flags = dict(start=first and r == 0 and i == 0, stop=last and r == 1 and i == 2)
                            if kind == "tokens":
                                ins = MM(acc[:, t, :], x[:, k, t * P:(t + 1) * P], w[:, slot, r, :], **flags)
                            elif kind == "channels":
                                ins = MM(acc[:, t, :], w[:, slot, r, t * P:(t + 1) * P], x[:, k, :], **flags)
                            else:
                                ins = MM(acc[:, t, :], w[:, slot, t // 2, r * 256 + t % 2 * P:r * 256 + t % 2 * P + P],
                                         x[:, k, :], **flags)
                    if last and t < 3:
                        ins.then_inc(acc_ready, 1)
                ins.then_inc(acc_ready if last else unit_used, 1)

            def gemm(q, a, acts, kind, between=None, parts=None, done=aux_free):
                for p in range(4):
                    if parts is not None:
                        pe.wait_ge(done, parts + 2 * p + 2)
                    unit(4 * q + p, p, p == 0, p == 3, a, acts, (2 * p, 2 * p + 1), kind)
                    if between:
                        between(p)

            def job(n, k=None):
                if not (isinstance(n, int) and n < 4):
                    pe.wait_ge(aux_free, n - 3)
                return aux[:, (n if k is None else k) % 4, :]

            def turn(n, src):
                bank = job(n)
                for t in range(NT):
                    ins = nc.tensor.transpose(bank[:, t * P:(t + 1) * P], src(t), ident[:, :])
                ins.then_inc(aux_ready, 1)

            t1, t2 = (t1h, t1l), (t2h, t2l)

            pe.wait_ge(consts, 6)
            pe.wait_ge(prow_in, 10 * 16)
            for i, n in enumerate((P, 120, 104)):
                ins = nc.tensor.transpose(aux[:, 0, i * P:i * P + n], prow[0:n, i, :], ident[0:n, 0:n])
            ins.then_inc(aux_ready, 1)
            banks = [job(J_N1 + k) for k in range(3)]
            for t in range(NT):
                pe.wait_ge(normed, t + 1)
                for k, bank in enumerate(banks):
                    ins = nc.tensor.transpose(bank[:, t * P:(t + 1) * P], xn[:, t, k * P:(k + 1) * P], ident[:, :])
                    if t == NT - 1:
                        ins.then_inc(aux_ready, 1)
            turn_x = lambda k: turn(J_N1 + k, lambda t: xn[:, t, k * P:(k + 1) * P])
            turn_x(3)

            def raw_dt(p):
                if p == 0:
                    for k in range(4, KD):
                        turn_x(k)
                if p == 3:
                    pe.wait_ge(wdt_lo, 1)
                    bank = job(J_DTC)
                    for k in range(KD):
                        for i, x in enumerate((t1h, t1l)):
                            ins = MM(bank[0:2 * NH, :], wdts[:, k, :], x[:, k, :], start=k == 0 and i == 0,
                                     stop=k == KD - 1 and i == 1)
                    ins.then_inc(aux_ready, 1)

            gemm(Q_B, Q_B, t1, "channels", raw_dt, parts=J_N1)
            flat = lambda ap: ap.rearrange("p t n -> p (t n)")

            def cumulative(p):
                if p == 0:
                    pe.wait_ge(aux_free, J_DTC + 1)
                    bank = job(J_DT)
                    for t in range(NT):
                        ins = nc.tensor.transpose(bank[:, t * 2 * NH:(t + 1) * 2 * NH],
                                                  dtc[0:2 * NH, t * P:(t + 1) * P], ident[0:2 * NH, 0:2 * NH])
                    ins.then_inc(aux_ready, 1)
                if p == 2:
                    pe.wait_ge(adt_ready, 1)
                    for n, m in ((J_CUM, tri), (J_TOT, ones)):
                        MM(job(n)[:, 0:P], m[:, :], flat(adt[:, :, :]), start=True, stop=True).then_inc(aux_ready, 1)

            def rows_over(p):
                if p == 0:
                    pe.wait_ge(aux_free, J_CUM + 1)
                    bank = job(J_ROWS)
                    for t in range(NT):
                        ins = nc.tensor.transpose(bank[0:NH, t * P:(t + 1) * P], acum[:, t, :], ident[:, :])
                    ins.then_inc(aux_ready, 1)

            gemm(Q_C, Q_C, t1, "channels", cumulative)
            gemm(Q_X0, Q_X0, t1, "channels", rows_over)

            def decays(j):
                base = J_SSD + SSD_JOBS * j
                bank = lambda k: job(base + k, J_SSD + k)

                def tokens(c):
                    b = bank(A_XS[c])
                    for f in range(4):
                        ins = nc.tensor.transpose(b[:, f * P:(f + 1) * P], xf[:, f, c * P:(c + 1) * P], ident[:, :])
                    ins.then_inc(aux_ready, 1)

                def between(p):
                    if p == 0:
                        pe.wait_ge(cur_ready, 2 * j + 2)
                        b = bank(A_BT)
                        for c in range(NT):
                            ins = nc.tensor.transpose(b[:, c * P:(c + 1) * P], bcur[:, c * P:(c + 1) * P], ident[:, :])
                        ins.then_inc(aux_ready, 1)
                        b = bank(A_CB)
                        for c in range(NT):
                            cc = slice(c * P, (c + 1) * P)
                            ins = MM(b[:, cc], bcur[:, cc], ccur[:, cc], start=True, stop=True)
                        ins.then_inc(aux_ready, 1)
                    elif p == 1:
                        pe.wait_ge(silu_ready, T_X + 4 * j + 4)
                        tokens(0)
                        tokens(1)
                    elif p == 2:
                        tokens(2)
                        tokens(3)

                return between

            def chunks(j):
                base = J_SSD + SSD_JOBS * j
                bank = lambda k: job(base + k, J_SSD + k)

                def between(c):
                    if c == 0:
                        pe.wait_ge(m_ready, HG * j + HG)
                        pe.wait_ge(xdt_ready, NT * j + NT)
                    b = bank(A_YD[c])
                    for h in range(HG):
                        cut = slice(h * HD, (h + 1) * HD)
                        ins = MM(b[:, cut], mm[:, h, c, :], xdt[:, c, cut], start=True, stop=True)
                    ins.then_inc(aux_ready, 1)
                    if c:
                        pe.wait_ge(aux_free, base + A_ST[c - 1] + 1)
                        MM(bank(A_OFF[c]), ccur[:, c * P:(c + 1) * P], state[:, :], start=True,
                           stop=True).then_inc(aux_ready, 1)
                    if c < NT - 1:
                        pe.wait_ge(xds_ready, 3 * j + c + 1)
                        MM(bank(A_ST[c]), bt[:, c, :], xds[:, :], start=True, stop=True).then_inc(aux_ready, 1)

                return between

            with pe.Fori(0, NG - 1) as j:
                gemm(Q_Z + 2 * j, Q_Z + 2 * j, t1, "tokens", decays(j))
                gemm(Q_Z + 1 + 2 * j, Q_Z + 1 + 2 * j, t1, "channels", chunks(j))
            gemm(Q_Z + 2 * NG - 2, Q_Z + 2 * NG - 2, t1, "tokens", decays(NG - 1))
            last = chunks(NG - 1)
            gemm(Q_V, Q_V, t1, "tokens", lambda p: last(p) if p < 2 else (last(2), last(3)) if p == 2 else None)
            gemm(Q_V + 1, Q_V + 1, t1, "tokens")

            pe.wait_ge(wsp_in, 16)
            for i in range(2):
                turn(J_WT + i, lambda t: wsp[:, 4 * i + t, :])
            with pe.Fori(0, 2) as i:
                gemm(Q_U + i, Q_U + i, t1, "channels")

            def mix(p):
                if p == 0:
                    pe.wait_ge(v_ready, NT)
                    pe.wait_ge(aux_free, J_WT + 2)
                for g in ((0, 1, 2), (3, 4, 5), (6, 7), ())[p]:
                    bank = job(J_MIX + g)
                    for t in range(NT):
                        ins = MM(bank[:, t * P:(t + 1) * P], vv[:, t, g * P:(g + 1) * P], wst[:, g, :], start=True,
                                 stop=True)
                    ins.then_inc(aux_ready, 1)

            gemm(Q_GB, Q_GB, t1, "channels", mix)

            def y_rms(p):
                if p == 1:
                    pe.wait_ge(diag_ready, 1)
                    MM(job(J_RY), ones1[:, :], diag1[:, :], start=True, stop=True).then_inc(aux_ready, 1)

            gemm(Q_GB + 1, Q_GB + 1, t1, "channels", y_rms)
            with pe.Fori(0, 2) as i:
                gemm(Q_PB + i, Q_PB + i, t2, "channels", parts=0, done=own_lo)
            for i in range(2):
                gemm(Q_GA + i, Q_GA + i, t1, "channels",
                     lambda p: turn(J_YA + 4 * i + p, lambda t: yy[:, t, (4 * i + p) * P:(4 * i + p + 1) * P]))
            for i in range(2):
                def second_half(p):
                    k = KD + 4 * i + p
                    turn(J_YA + k, lambda t: yy[:, t, k * P:(k + 1) * P])

                gemm(Q_PA + i, Q_PA + i, t2, "channels", second_half, parts=J_YA)
            gemm(Q_PA + 2, Q_PA + 2, t1, "channels", parts=J_YA + KD)

            gemm(Q_PA + 3, Q_PA + 3, t1, "channels")

            def turn_h(*ks):
                for k in ks:
                    turn(J_N2 + k, lambda t: hh[:, t, k * P:(k + 1) * P])

            def first_h(p):
                if p == 1:
                    pe.wait_ge(acc_free, 4 * Q_WO + 4)
                if p in (1, 2):
                    turn_h(2 * p - 2, 2 * p - 1)

            gemm(Q_WO, Q_WO, t2, "tokens", parts=KD, done=own_lo)
            gemm(Q_WO + 1, Q_WO + 1, t2, "tokens", first_h)

            def rest_h(p):
                if p == 0:
                    pe.wait_ge(acc_free, 4 * Q_WO + 8)
                if p in (0, 1):
                    turn_h(2 * p + 4, 2 * p + 5)
                if p == 2:
                    pe.wait_ge(diag_ready, 2)
                    MM(job(J_RB), ones2[:, :], diag[:, :], start=True, stop=True).then_inc(aux_ready, 1)

            gemm(Q_UP, Q_UP, t1, "pairs", rest_h, parts=J_N2)
            with pe.Fori(0, FC - 1) as i:
                gemm(Q_UP + 1 + i, Q_UP + 1 + i, t1, "pairs")
            half = KF // 2
            for n in range(KF - 4):
                c, u = divmod(n, half)
                pe.wait_ge(flo, 2 * u + 2)
                unit(4 * Q_DOWN + n, n % 4, u == 0, u == half - 1, Q_DOWN + c, (fth, ftl),
                     (2 * u, 2 * u + 1), "tokens")
            for t in range(4):
                for n in range(KF - 4, KF):
                    if t == 0:
                        pe.wait_ge(lo_ready, 4 * Q_DOWN + n + 1)
                    for r in range(2):
                        k = 2 * (n - half) + r
                        for i, (w, x) in enumerate(((whi, fth), (whi, ftl), (wlo, fth))):
                            ins = MM(acc[:, t, :], x[:, k, t * P:(t + 1) * P], w[:, n % 4, r, :], start=False,
                                     stop=n == KF - 1 and r == 1 and i == 2)
                ins.then_inc(acc_ready, 1)


_INS = ["x", "norm1_w", "w_in", "b_gate", "conv_a_w", "conv_a_b", "dt_bias", "a_log", "d_skip", "ssd_norm_w",
        "uv_b", "v_ln_w", "v_ln_b", "w_spatial", "b_spatial", "w_branch", "w_out", "norm2_w", "w_up",
        "conv_f_w", "conv_f_b", "w_down", "final_norm_w"]


def kernel(**inputs):
    import numpy as np
    import concourse.bacc as bacc
    from concourse import mybir as mb
    from concourse.bass_utils import run_bass_kernel_spmd

    nc = bacc.Bacc("TRN2", target_bir_lowering=False, num_devices=1)
    arrays, args = {}, []
    for name in _INS:
        a = np.ascontiguousarray(inputs[name])
        arrays[f"in_{name}"] = a
        args.append(nc.dram_tensor(f"in_{name}", a.shape, mb.dt.from_np(a.dtype), kind="ExternalInput").ap())
    out = nc.dram_tensor("out_0", (1, S, D), F32, kind="ExternalOutput").ap()
    hybrid_block(nc, *args, out)
    return run_bass_kernel_spmd(nc, [arrays], core_ids=[0]).results[0]["out_0"]
```
